# Optimizing a Trainium2 kernel written in Bass

```python
import jax, jax.numpy as jnp
from jax import lax
import numpy as np

D_MODEL = 1024
BATCH = 1
SEQ = 256
DEPTH = 2

HEAD_DIM = 64
HG_HEADS = 4
HG_WIDTH = HG_HEADS * HEAD_DIM
HG_CHUNK = 64
ATT_HEADS = 8
ATT_KV_HEADS = 2
ATT_WIDTH = ATT_HEADS * HEAD_DIM
ATT_KV_WIDTH = ATT_KV_HEADS * HEAD_DIM
WINDOW = 128
ROPE_THETA = 10000.0
SG_GROUPS = 4
SG_WIDTH = SG_GROUPS * HEAD_DIM
SG_CHUNK = 128

MIX_WIDTH = HG_WIDTH + ATT_WIDTH + SG_WIDTH
IN_SPLITS = (HG_WIDTH, HG_WIDTH, HG_WIDTH, HG_WIDTH,
             ATT_WIDTH, ATT_KV_WIDTH, ATT_KV_WIDTH,
             SG_WIDTH, SG_WIDTH)
IN_WIDTH = sum(IN_SPLITS)
D_FF = 2816
PLE_DIM = 256
N_NORMS = 8
EPS = 1e-6
MASK_VALUE = -1e30
LB_FLOOR = 1e-30


def rmsnorm(x, g):
    xf = x.astype(jnp.float32)
    y = xf * lax.rsqrt(jnp.mean(xf * xf, axis=-1, keepdims=True) + EPS)
    return (y * g.astype(jnp.float32)).astype(x.dtype)

def layernorm(x, g):
    xf = x.astype(jnp.float32)
    mu = jnp.mean(xf, axis=-1, keepdims=True)
    xc = xf - mu
    y = xc * lax.rsqrt(jnp.mean(xc * xc, axis=-1, keepdims=True) + EPS)
    return (y * g.astype(jnp.float32)).astype(x.dtype)

def swiglu(x, w_gu, w_down):
    gate, up = jnp.split(x @ w_gu, 2, axis=-1)
    return (jax.nn.silu(gate) * up) @ w_down

def rope(x, pos):
    half = x.shape[-1] // 2
    inv = ROPE_THETA ** (-jnp.arange(half, dtype=jnp.float32) / half)
    ang = pos.astype(jnp.float32)[..., None] * inv
    cos = jnp.cos(ang)[:, :, None, :]
    sin = jnp.sin(ang)[:, :, None, :]
    xf = x.astype(jnp.float32)
    x1, x2 = xf[..., :half], xf[..., half:]
    return jnp.concatenate([x1 * cos - x2 * sin, x2 * cos + x1 * sin], axis=-1).astype(x.dtype)

def hgrn2(q, f_raw, i, lb):
    B, S, _ = q.shape
    C = HG_CHUNK
    n = S // C
    q = q.astype(jnp.float32)
    v = i.astype(jnp.float32)
    lb = lb.astype(jnp.float32)
    logf = jnp.logaddexp(jnp.log(jnp.maximum(lb, LB_FLOOR)),
                         jnp.log1p(-lb) + jax.nn.log_sigmoid(f_raw.astype(jnp.float32)))
    k = -jnp.expm1(logf)

    def heads(t):
        return t.reshape(B, n, C, HG_HEADS, HEAD_DIM).transpose(1, 0, 3, 2, 4)

    causal = jnp.tril(jnp.ones((C, C), dtype=bool))[:, :, None]

    def step(state, inp):
        qc, kc, vc, lc = inp
        b = jnp.cumsum(lc, axis=2)
        o_inter = jnp.einsum('bhcd,bhde->bhce', qc * jnp.exp(b), state)
        diff = b[:, :, :, None, :] - b[:, :, None, :, :]
        dec = jnp.where(causal, jnp.exp(jnp.where(causal, diff, 0.0)), 0.0)
        att = jnp.einsum('bhid,bhjd,bhijd->bhij', qc, kc, dec)
        o_intra = jnp.einsum('bhij,bhje->bhie', att, vc)
        b_last = b[:, :, -1:, :]
        new_state = (jnp.exp(b_last[:, :, 0, :])[..., None] * state
                     + jnp.einsum('bhcd,bhce->bhde', kc * jnp.exp(b_last - b), vc))
        return new_state, o_inter + o_intra

    s0 = jnp.zeros((B, HG_HEADS, HEAD_DIM, HEAD_DIM), jnp.float32)
    _, o = lax.scan(step, s0, (heads(q), heads(k), heads(v), heads(logf)))
    return o.transpose(1, 0, 3, 2, 4).reshape(B, S, HG_HEADS, HEAD_DIM)

def swa_sink_attention(q, k, v, sinks, pos):
    B, S, _ = q.shape
    G = ATT_HEADS // ATT_KV_HEADS
    nb = S // WINDOW
    q = rope(q.reshape(B, S, ATT_HEADS, HEAD_DIM), pos)
    k = rope(k.reshape(B, S, ATT_KV_HEADS, HEAD_DIM), pos)
    v = v.reshape(B, S, ATT_KV_HEADS, HEAD_DIM)
    qb = q.reshape(B, nb, WINDOW, ATT_KV_HEADS, G, HEAD_DIM)

    def with_prev(t):
        t = t.reshape(B, nb, WINDOW, ATT_KV_HEADS, HEAD_DIM)
        prev = jnp.concatenate([jnp.zeros_like(t[:, :1]), t[:, :-1]], axis=1)
        return jnp.concatenate([prev, t], axis=2)

    kk, vv = with_prev(k), with_prev(v)
    s = jnp.einsum('bnqkgd,bnskd->bnkgqs', qb, kk).astype(jnp.float32) * (HEAD_DIM ** -0.5)
    qi = jnp.arange(WINDOW)[:, None]
    sj = jnp.arange(2 * WINDOW)[None, :]
    rel = qi + WINDOW - sj
    band = (rel >= 0) & (rel < WINDOW)
    exists = (jnp.arange(nb)[:, None, None] * WINDOW + sj[None] - WINDOW) >= 0
    mask = (band[None] & exists)[None, :, None, None]
    s = jnp.where(mask, s, MASK_VALUE)
    sink = sinks.astype(jnp.float32).reshape(1, 1, ATT_KV_HEADS, G, 1, 1)
    m = jnp.maximum(jnp.max(s, axis=-1, keepdims=True), sink)
    pr = jnp.where(mask, jnp.exp(s - m), 0.0)
    denom = jnp.sum(pr, axis=-1, keepdims=True) + jnp.exp(sink - m)
    o = jnp.einsum('bnkgqs,bnskd->bnqkgd', (pr / denom).astype(v.dtype), vv)
    return o.reshape(B, S, ATT_WIDTH)

def spatial_gating(u, v, ln_g, w_s, b_s):
    B, S, _ = u.shape
    nc = S // SG_CHUNK
    u = jax.nn.gelu(u)
    v = layernorm(jax.nn.gelu(v), ln_g)
    vg = v.reshape(B, nc, SG_CHUNK, SG_GROUPS, HEAD_DIM)
    w = w_s * jnp.tril(jnp.ones((SG_CHUNK, SG_CHUNK), w_s.dtype))
    mix = jnp.einsum('gts,bnsgd->bntgd', w, vg) + b_s.T[:, :, None]
    return (u.reshape(B, nc, SG_CHUNK, SG_GROUPS, HEAD_DIM) * mix).reshape(B, S, SG_WIDTH)

def hybrid_layer(h, p_i, pos, lb, norm_g, w_in, w_out, ffn1_gu, ffn1_down, ffn2_gu, ffn2_down,
                 hg_norm_g, sinks, sg_ln_g, sg_w, sg_b, ple_proj, ple_gate):
    B, S, _ = h.shape
    h = h + 0.5 * rmsnorm(swiglu(rmsnorm(h, norm_g[0]), ffn1_gu, ffn1_down), norm_g[1])
    z = rmsnorm(h, norm_g[2]) @ w_in
    idx = [int(c) for c in np.cumsum(IN_SPLITS)[:-1]]
    hq, hf, hi, hg, aq, ak, av, su, sv = jnp.split(z, idx, axis=-1)
    o_a = hgrn2(hq, hf, hi, lb)
    o_a = rmsnorm(o_a, hg_norm_g) * jax.nn.sigmoid(hg.astype(jnp.float32).reshape(B, S, HG_HEADS, HEAD_DIM))
    o_a = o_a.reshape(B, S, HG_WIDTH).astype(h.dtype)
    o_b = swa_sink_attention(aq, ak, av, sinks, pos).astype(h.dtype)
    o_c = spatial_gating(su, sv, sg_ln_g, sg_w, sg_b).astype(h.dtype)
    mixed = jnp.concatenate([o_a, o_b, o_c], axis=-1) @ w_out
    h = h + rmsnorm(mixed, norm_g[3])
    h = h + 0.5 * rmsnorm(swiglu(rmsnorm(h, norm_g[4]), ffn2_gu, ffn2_down), norm_g[5])
    gate = jax.nn.sigmoid(rmsnorm(h, norm_g[6]) @ ple_gate)
    h = h + rmsnorm((p_i @ ple_proj) * gate, norm_g[7])
    return h

def first_inputs(seed: int = 0) -> dict:
    key = jax.random.key(seed)
    ks = jax.random.split(key, 20)

    def nrm(k, shape, scale):
        return jax.random.normal(k, shape, jnp.float32) * scale

    x = nrm(ks[0], (BATCH, SEQ, D_MODEL), 1.0)
    p = nrm(ks[1], (DEPTH, BATCH, SEQ, PLE_DIM), 1.0)
    positions = (jnp.arange(SEQ, dtype=jnp.int32)[None, :]
                 + jax.random.randint(ks[2], (BATCH, 1), 0, 1024, dtype=jnp.int32))
    return {
        "x": x,
        "p": p,
        "positions": positions,
        "norm_gains": 1.0 + nrm(ks[3], (DEPTH, N_NORMS, D_MODEL), 0.05),
        "w_in": nrm(ks[4], (DEPTH, D_MODEL, IN_WIDTH), D_MODEL ** -0.5),
        "w_out": nrm(ks[5], (DEPTH, MIX_WIDTH, D_MODEL), MIX_WIDTH ** -0.5),
        "ffn1_gate_up": nrm(ks[6], (DEPTH, D_MODEL, 2 * D_FF), D_MODEL ** -0.5),
        "ffn1_down": nrm(ks[7], (DEPTH, D_FF, D_MODEL), D_FF ** -0.5),
        "ffn2_gate_up": nrm(ks[8], (DEPTH, D_MODEL, 2 * D_FF), D_MODEL ** -0.5),
        "ffn2_down": nrm(ks[9], (DEPTH, D_FF, D_MODEL), D_FF ** -0.5),
        "hgrn_lb_logits": nrm(ks[10], (DEPTH, HG_WIDTH), 0.5),
        "hgrn_norm_gain": 1.0 + nrm(ks[11], (DEPTH, HEAD_DIM), 0.05),
        "attn_sinks": nrm(ks[12], (DEPTH, ATT_HEADS), 0.5),
        "sg_ln_gain": 1.0 + nrm(ks[13], (DEPTH, SG_WIDTH), 0.05),
        "sg_spatial_w": nrm(ks[14], (DEPTH, SG_GROUPS, SG_CHUNK, SG_CHUNK), SG_CHUNK ** -0.5),
        "sg_spatial_b": 1.0 + nrm(ks[15], (DEPTH, SG_GROUPS, SG_CHUNK), 0.1),
        "ple_proj": nrm(ks[16], (DEPTH, PLE_DIM, D_MODEL), PLE_DIM ** -0.5),
        "ple_gate": nrm(ks[17], (DEPTH, D_MODEL, D_MODEL), D_MODEL ** -0.5),
    }

def first_block(x, p, positions, norm_gains, w_in, w_out, ffn1_gate_up, ffn1_down, ffn2_gate_up,
              ffn2_down, hgrn_lb_logits, hgrn_norm_gain, attn_sinks, sg_ln_gain, sg_spatial_w,
              sg_spatial_b, ple_proj, ple_gate):
    probs = jax.nn.softmax(hgrn_lb_logits.astype(jnp.float32), axis=0)
    lower_bounds = jnp.cumsum(probs, axis=0) - probs[0]
    h = x
    for l in range(DEPTH):
        h = hybrid_layer(h, p[l], positions, lower_bounds[l], norm_gains[l], w_in[l], w_out[l],
                         ffn1_gate_up[l], ffn1_down[l], ffn2_gate_up[l], ffn2_down[l],
                         hgrn_norm_gain[l], attn_sinks[l], sg_ln_gain[l], sg_spatial_w[l],
                         sg_spatial_b[l], ple_proj[l], ple_gate[l])
    return h


N_META = 16
N_A_LAYERS = DEPTH // 2
N_B_LAYERS = DEPTH - N_A_LAYERS
CONV_W = 3
N_HEADS = 8
QK_NOPE_DIM = 128
QK_ROPE_DIM = 64
V_DIM = 128
Q_RANK = 384
KV_RANK = 256
Q_BLOCK = 128
N_GROUPS = 8
EXPERTS_PER_GROUP = 8
N_EXPERTS = N_GROUPS * EXPERTS_PER_GROUP
TOP_K_IN_GROUP = 2
D_EXPERT = 256
EXPERT_BLOCK = 128
NORM_EPS = 1e-6


def rmsnorm_2(x, g):
    xf = x.astype(jnp.float32)
    y = xf * lax.rsqrt(jnp.mean(xf * xf, axis=-1, keepdims=True) + NORM_EPS)
    return (y * g.astype(jnp.float32)).astype(x.dtype)

def rope_tables(t):
    inv = ROPE_THETA ** (-jnp.arange(0, QK_ROPE_DIM, 2, dtype=jnp.float32) / QK_ROPE_DIM)
    ang = jnp.arange(t, dtype=jnp.float32)[:, None] * inv[None, :]
    return jnp.cos(ang), jnp.sin(ang)

def apply_rope(x, cos, sin):
    half = x.shape[-1] // 2
    x1, x2 = x[..., :half], x[..., half:]
    cos = cos.astype(x.dtype)
    sin = sin.astype(x.dtype)
    return jnp.concatenate([x1 * cos - x2 * sin, x1 * sin + x2 * cos], axis=-1)

def short_conv_mixer(hn, w_in, conv_w, w_out):
    bcu = hn @ w_in
    b, c, u = jnp.split(bcu, 3, axis=-1)
    z = c * u
    z = lax.conv_general_dilated(z, conv_w.astype(z.dtype), window_strides=(1,),
                                 padding=((CONV_W - 1, 0),),
                                 dimension_numbers=('NWC', 'WIO', 'NWC'),
                                 feature_group_count=z.shape[-1])
    return (b * z) @ w_out

def shared_kv_side(h, kv_g, w_dkv, ckv_g, w_ukv, cos, sin):
    bsz, t, _ = h.shape
    a = rmsnorm_2(h, kv_g) @ w_dkv
    c_kv = rmsnorm_2(a[..., :KV_RANK], ckv_g)
    k_rope = apply_rope(a[..., KV_RANK:], cos, sin)
    kv = (c_kv @ w_ukv).reshape(bsz, t, N_HEADS, QK_NOPE_DIM + V_DIM)
    return kv[..., :QK_NOPE_DIM], k_rope, kv[..., QK_NOPE_DIM:]

def causal_block_attention(q_nope, q_rope, k_nope, k_rope, v):
    bsz, t, nh, _ = q_nope.shape
    nqb = -(-t // Q_BLOCK)
    pad = nqb * Q_BLOCK - t
    def blocks(q):
        q = jnp.pad(q, ((0, 0), (0, pad), (0, 0), (0, 0)))
        return q.reshape(bsz, nqb, Q_BLOCK, nh, q.shape[-1]).transpose(1, 0, 2, 3, 4)
    qn, qr = blocks(q_nope), blocks(q_rope)
    kpos = jnp.arange(t)
    scale = (QK_NOPE_DIM + QK_ROPE_DIM) ** -0.5
    def one_block(args):
        qn_b, qr_b, j = args
        qpos = j * Q_BLOCK + jnp.arange(Q_BLOCK)
        s = (jnp.einsum('bqhd,bkhd->bhqk', qn_b, k_nope)
             + jnp.einsum('bqhd,bkd->bhqk', qr_b, k_rope)).astype(jnp.float32) * scale
        s = jnp.where(kpos[None, :] <= qpos[:, None], s, -jnp.inf)
        p = jax.nn.softmax(s, axis=-1).astype(v.dtype)
        return jnp.einsum('bhqk,bkhd->bqhd', p, v)
    o = lax.map(one_block, (qn, qr, jnp.arange(nqb, dtype=jnp.int32)))
    o = o.transpose(1, 0, 2, 3, 4).reshape(bsz, nqb * Q_BLOCK, nh * v.shape[-1])
    return o[:, :t]

def mla_mixer(hn, w_dq, cq_g, w_uq, w_o, k_nope, k_rope, v, cos, sin):
    bsz, t, _ = hn.shape
    cq = rmsnorm_2(hn @ w_dq, cq_g)
    q = (cq @ w_uq).reshape(bsz, t, N_HEADS, QK_NOPE_DIM + QK_ROPE_DIM)
    q_nope = q[..., :QK_NOPE_DIM]
    q_rope = apply_rope(q[..., QK_NOPE_DIM:], cos[:, None, :], sin[:, None, :])
    o = causal_block_attention(q_nope, q_rope, k_nope, k_rope, v)
    return o @ w_o

def hier_moe(hn, w_grp, w_exp, w_gate, w_up, w_down):
    bsz, t, d = hn.shape
    n = bsz * t
    xf = hn.reshape(n, d)
    g_logits = (xf @ w_grp).astype(jnp.float32)
    p_grp = jax.nn.softmax(g_logits, axis=-1)
    grp = jnp.argmax(g_logits, axis=-1).astype(jnp.int32)
    p_g = jnp.max(p_grp, axis=-1, keepdims=True)
    e_logits = (xf @ w_exp).astype(jnp.float32).reshape(n, N_GROUPS, EXPERTS_PER_GROUP)
    e_in = jnp.einsum('ng,nge->ne', jax.nn.one_hot(grp, N_GROUPS, dtype=jnp.float32), e_logits)
    top_p, top_i = lax.top_k(jax.nn.softmax(e_in, axis=-1), TOP_K_IN_GROUP)
    gate = p_g * top_p / jnp.sum(top_p, axis=-1, keepdims=True)
    expert = grp[:, None] * EXPERTS_PER_GROUP + top_i.astype(jnp.int32)
    a = n * TOP_K_IN_GROUP
    e_a = expert.reshape(a)
    w_a = gate.reshape(a).astype(hn.dtype)
    tok_a = jnp.repeat(jnp.arange(n, dtype=jnp.int32), TOP_K_IN_GROUP)
    counts = jax.ops.segment_sum(jnp.ones((a,), jnp.int32), e_a, num_segments=N_EXPERTS)
    padded = ((counts + EXPERT_BLOCK - 1) // EXPERT_BLOCK) * EXPERT_BLOCK
    pad_end = jnp.cumsum(padded)
    pad_start = pad_end - padded
    start = jnp.cumsum(counts) - counts
    order = jnp.argsort(e_a)
    e_s = e_a[order]
    dest = pad_start[e_s] + jnp.arange(a, dtype=jnp.int32) - start[e_s]
    n_blocks = (a + N_EXPERTS * (EXPERT_BLOCK - 1) + EXPERT_BLOCK - 1) // EXPERT_BLOCK
    p_slots = n_blocks * EXPERT_BLOCK
    slot_tok = jnp.full((p_slots,), n, jnp.int32).at[dest].set(tok_a[order])
    slot_w = jnp.zeros((p_slots,), hn.dtype).at[dest].set(w_a[order])
    blk_expert = jnp.minimum(jnp.searchsorted(pad_end, jnp.arange(n_blocks, dtype=jnp.int32) * EXPERT_BLOCK,
                                              side='right'), N_EXPERTS - 1).astype(jnp.int32)
    x_pad = jnp.concatenate([xf, jnp.zeros((1, d), xf.dtype)], axis=0)
    xs = x_pad[slot_tok].reshape(n_blocks, EXPERT_BLOCK, d)
    def expert_block(args):
        xb, e = args
        hh = jax.nn.silu(xb @ w_gate[e]) * (xb @ w_up[e])
        return hh @ w_down[e]
    ys = lax.map(expert_block, (xs, blk_expert)).reshape(p_slots, d)
    y = jnp.zeros((n + 1, d), ys.dtype).at[slot_tok].add(ys * slot_w[:, None])[:n]
    return y.reshape(bsz, t, d)

def second_inputs(seed: int = 0) -> dict:
    key = jax.random.key(seed)
    ks = jax.random.split(key, 21)
    def nrm(k, shape, scale):
        return jax.random.normal(k, shape, jnp.float32) * scale
    d = D_MODEL
    return {
        'x': nrm(ks[0], (BATCH, SEQ, d), 1.0),
        'meta_tokens': nrm(ks[1], (N_META, d), 1.0),
        'norm_mix_g': 1.0 + nrm(ks[2], (DEPTH, d), 0.02),
        'norm_ffn_g': 1.0 + nrm(ks[3], (DEPTH, d), 0.02),
        'conv_w_in': nrm(ks[4], (N_A_LAYERS, d, 3 * d), d ** -0.5),
        'conv_w': nrm(ks[5], (N_A_LAYERS, CONV_W, 1, d), CONV_W ** -0.5),
        'conv_w_out': nrm(ks[6], (N_A_LAYERS, d, d), d ** -0.5),
        'kv_norm_g': 1.0 + nrm(ks[7], (d,), 0.02),
        'w_dkv': nrm(ks[8], (d, KV_RANK + QK_ROPE_DIM), d ** -0.5),
        'ckv_norm_g': 1.0 + nrm(ks[9], (KV_RANK,), 0.02),
        'w_ukv': nrm(ks[10], (KV_RANK, N_HEADS * (QK_NOPE_DIM + V_DIM)), KV_RANK ** -0.5),
        'w_dq': nrm(ks[11], (N_B_LAYERS, d, Q_RANK), d ** -0.5),
        'cq_norm_g': 1.0 + nrm(ks[12], (N_B_LAYERS, Q_RANK), 0.02),
        'w_uq': nrm(ks[13], (N_B_LAYERS, Q_RANK, N_HEADS * (QK_NOPE_DIM + QK_ROPE_DIM)), Q_RANK ** -0.5),
        'w_o': nrm(ks[14], (N_B_LAYERS, N_HEADS * V_DIM, d), (N_HEADS * V_DIM) ** -0.5),
        'w_grp': nrm(ks[15], (DEPTH, d, N_GROUPS), d ** -0.5),
        'w_exp': nrm(ks[16], (DEPTH, d, N_EXPERTS), d ** -0.5),
        'w_gate': nrm(ks[17], (DEPTH, N_EXPERTS, d, D_EXPERT), d ** -0.5),
        'w_up': nrm(ks[18], (DEPTH, N_EXPERTS, d, D_EXPERT), d ** -0.5),
        'w_down': nrm(ks[19], (DEPTH, N_EXPERTS, D_EXPERT, d), D_EXPERT ** -0.5),
        'final_norm_g': 1.0 + nrm(ks[20], (d,), 0.02),
    }

def second_block(x, meta_tokens, norm_mix_g, norm_ffn_g, conv_w_in, conv_w, conv_w_out,
              kv_norm_g, w_dkv, ckv_norm_g, w_ukv, w_dq, cq_norm_g, w_uq, w_o,
              w_grp, w_exp, w_gate, w_up, w_down, final_norm_g):
    bsz = x.shape[0]
    meta = jnp.broadcast_to(meta_tokens[None].astype(x.dtype), (bsz, N_META, x.shape[-1]))
    h = jnp.concatenate([meta, x], axis=1)
    cos, sin = rope_tables(h.shape[1])
    shared = None
    for i in range(DEPTH):
        if i < N_A_LAYERS:
            h = h + short_conv_mixer(rmsnorm_2(h, norm_mix_g[i]), conv_w_in[i], conv_w[i], conv_w_out[i])
        else:
            if shared is None:
                shared = shared_kv_side(h, kv_norm_g, w_dkv, ckv_norm_g, w_ukv, cos, sin)
            j = i - N_A_LAYERS
            k_nope, k_rope, v = shared
            h = h + mla_mixer(rmsnorm_2(h, norm_mix_g[i]), w_dq[j], cq_norm_g[j], w_uq[j], w_o[j],
                              k_nope, k_rope, v, cos, sin)
        h = h + hier_moe(rmsnorm_2(h, norm_ffn_g[i]), w_grp[i], w_exp[i], w_gate[i], w_up[i], w_down[i])
    return rmsnorm_2(h, final_norm_g)[:, N_META:]


def setup_inputs(seed=0):
    out = dict(first_inputs(seed))
    for name, value in second_inputs(seed + 1).items():
        if name != "x":
            out[name + "_2"] = value
    return out


def reference(
    x, p, positions, norm_gains, w_in, w_out, ffn1_gate_up, ffn1_down, ffn2_gate_up, ffn2_down,
    hgrn_lb_logits, hgrn_norm_gain, attn_sinks, sg_ln_gain, sg_spatial_w, sg_spatial_b,
    ple_proj, ple_gate, meta_tokens_2, norm_mix_g_2, norm_ffn_g_2, conv_w_in_2, conv_w_2,
    conv_w_out_2, kv_norm_g_2, w_dkv_2, ckv_norm_g_2, w_ukv_2, w_dq_2, cq_norm_g_2, w_uq_2,
    w_o_2, w_grp_2, w_exp_2, w_gate_2, w_up_2, w_down_2, final_norm_g_2,
):
    x = first_block(
        x, p, positions, norm_gains, w_in, w_out, ffn1_gate_up, ffn1_down, ffn2_gate_up,
        ffn2_down, hgrn_lb_logits, hgrn_norm_gain, attn_sinks, sg_ln_gain, sg_spatial_w,
        sg_spatial_b, ple_proj, ple_gate,
    )
    return second_block(
        x, meta_tokens_2, norm_mix_g_2, norm_ffn_g_2, conv_w_in_2, conv_w_2, conv_w_out_2,
        kv_norm_g_2, w_dkv_2, ckv_norm_g_2, w_ukv_2, w_dq_2, cq_norm_g_2, w_uq_2, w_o_2,
        w_grp_2, w_exp_2, w_gate_2, w_up_2, w_down_2, final_norm_g_2,
    )


_drawn_inputs = setup_inputs


def setup_inputs(seed=0):
    import zlib

    import numpy as np

    out = dict(_drawn_inputs(seed))
    spreads = {}
    factors = {'attn_sinks': 4.041,
     'norm_mix_g_2': 3.59,
     'norm_ffn_g_2': 3.805,
     'kv_norm_g_2': 8.0,
     'ckv_norm_g_2': 8.0,
     'cq_norm_g_2': 8.0,
     'final_norm_g_2': 2.827}
    for name, (base, spread) in spreads.items():
        noise = np.random.default_rng([zlib.crc32(name.encode()), seed]).standard_normal(out[name].shape)
        drawn = base * np.exp(spread * noise) if base else spread * noise
        out[name] = __import__('jax').numpy.asarray(drawn.astype(out[name].dtype))
    for name, factor in factors.items():
        out[name] = (out[name] * factor).astype(out[name].dtype)
    return out
```

```python
from contextlib import ExitStack

import numpy as np
import concourse.bass as bass
from concourse import mybir

F32 = mybir.dt.float32
I32 = mybir.dt.int32
U32 = mybir.dt.uint32
ALU = mybir.AluOpType
ACT = mybir.ActivationFunctionType
AX = mybir.AxisListType

P = 128
D = 1024
KD = D // P
SEQ = 256
DEPTH = 2
META = 16
T2 = META + SEQ
EPS = 1e-6
SLOTS = 4
UNIT = 6144

D_FF = 2816
FF_UNITS = D_FF // 256
FT = D_FF // P
IN_W = 2304
HD = 64
PLE = 256
LN_FLOOR = float(np.log(np.float32(1e-30)))

NG = 8
NE = 64
BLK = 32
TOPK = 2
GROUP = SLOTS
MAX_BLOCKS = NE + (T2 * TOPK) // BLK
MAX_GROUPS = -(-MAX_BLOCKS // GROUP)
DE = 256
Q_RANK = 384
KV_RANK = 256
ROPE2 = 64
NH2 = 8

TWO_PI = 2.0 * np.pi
C1 = 6.28125
C2 = float(np.float32(TWO_PI - C1))
C3 = float(np.float32(TWO_PI - C1 - np.float64(np.float32(C2))))
ROUND = 1.5 * 2.0 ** 23

LEVELS = [64, 32, 16, 8, 4, 2, 1, 0]


def const_table():
    p = np.arange(P)[:, None].astype(np.float64)
    c = np.arange(P)[None, :].astype(np.float64)
    parts, at, n = [], {}, 0

    def put(name, a):
        nonlocal n
        a = np.ascontiguousarray(np.broadcast_to(a, (P, a.shape[1]))).astype(np.float32)
        at[name] = (n, a.shape[1])
        parts.append(a)
        n += a.shape[1]

    put("ident", (p == c))
    put("ones", np.ones((P, P)))
    put("before", (p < c))
    put("upto", (p <= c))
    neg = -1e30
    put("window", np.concatenate([np.where(c > p, 0, neg), np.where(c <= p, 0, neg)], 1))
    key = np.arange(T2)[None, :]
    first, parts, first_n, n = parts, [], n, 0
    put("causal0", np.where(key <= META + p, 0, neg))
    put("causal1", np.where(key <= META + P + p, 0, neg))
    put("causal2", np.where(key[:, :META] <= p, 0, neg))
    put("iota", np.broadcast_to(c, (P, P)))
    put("group_starts", np.broadcast_to(P * (1 + np.arange(MAX_GROUPS))[None], (P, MAX_GROUPS)))
    put("block_starts", np.broadcast_to(BLK * (1 + np.arange(8))[None], (P, 8)))
    put("token_id", p + P * np.arange(3)[None])
    put("valid", np.concatenate([np.ones((P, 2)), (p < META)], 1))
    second, parts, second_n, n = parts, first, n, first_n
    inv = np.float32(10000.0) ** (-np.arange(32, dtype=np.float32) / np.float32(32))
    put("inv_freq", inv[None])
    inv2 = np.float32(10000.0) ** (-np.arange(0, 64, 2, dtype=np.float32) / np.float32(64))
    first, parts, first_n, n = parts, second, n, second_n
    pos = [np.arange(P) + META, np.arange(P) + META + P, np.minimum(np.arange(P), META - 1)]
    ang = np.stack([q.astype(np.float32)[:, None] * inv2[None] for q in pos], 1).astype(np.float32)
    put("cos2", np.cos(ang.astype(np.float64)).reshape(P, -1))
    put("sin2", np.sin(ang.astype(np.float64)).reshape(P, -1))
    second, parts, n = parts, first, first_n
    masks = []
    for s in LEVELS:
        if s:
            node = (p // (2 * s)) == (c // (2 * s))
            masks.append(node & (p % (2 * s) < s) & (c % (2 * s) >= s))
        else:
            masks.append(p == c)
    put("levels", np.concatenate(masks, 1))
    put("minus_half", np.full((P, 8), -0.5))
    return np.concatenate(parts, 1), np.concatenate(second, 1), at


CONSTS, CONSTS2, CONST_AT = const_table()
NCONST = CONSTS.shape[1]
NCONST2 = CONSTS2.shape[1]
SECOND = ("causal0", "causal1", "causal2", "iota", "group_starts", "block_starts", "token_id", "valid", "cos2", "sin2")
ROWS2 = ["norm_mix_g_2", "norm_ffn_g_2", "kv_norm_g_2", "ckv_norm_g_2", "cq_norm_g_2", "conv_w_2",
         "hgrn_lb_logits"]


def row_starts(shapes):
    at, n = {}, 0
    for name in ROWS2:
        at[name] = n
        n += int(np.prod(shapes[name])) // P
    return at, n

ARENA = 12032


class Semaphores:

    def __init__(self, sem):
        self.const_loaded = sem("const_loaded")
        self.small_loaded = sem("small_loaded")
        self.h_loaded = sem("h_loaded")
        self.meta_loaded = sem("meta_loaded")
        self.rows_loaded = sem("rows_loaded")
        self.pad = sem("pad")
        self.h_upd = sem("h_upd")
        self.ms_ready = sem("ms_ready")
        self.rstd_ready = sem("rstd_ready")
        self.square_done = sem("square_done")
        self.xn_ready = sem("xn_ready")
        self.xn_turned = sem("xn_turned")
        self.xT_ready = sem("xT_ready")
        self.gateup_done = sem("gateup_done")
        self.silu_ready = sem("silu_ready")
        self.hidden_ready = sem("hidden_ready")
        self.down_done = sem("down_done")
        self.qf_done = sem("qf_done")
        self.qf_copied = sem("qf_copied")
        self.z_done = sem("z_done")
        self.hihg_copied = sem("hihg_copied")
        self.susv_copied = sem("susv_copied")
        self.qkv_copied = sem("qkv_copied")
        self.hgrn_vec = sem("hgrn_vec")
        self.hgrn_act = sem("hgrn_act")
        self.hgrn_pe = sem("hgrn_pe")
        self.roped = sem("roped")
        self.qk_turned = sem("qk_turned")
        self.qkT_ready = sem("qkT_ready")
        self.scores_done = sem("scores_done")
        self.scores_ready = sem("scores_ready")
        self.probs_ready = sem("probs_ready")
        self.probs_turned = sem("probs_turned")
        self.probsT_ready = sem("probsT_ready")
        self.attn_done = sem("attn_done")
        self.sgw_turned = sem("sgw_turned")
        self.sgw_ready = sem("sgw_ready")
        self.centred = sem("centred")
        self.sv_ready = sem("sv_ready")
        self.spatial_done = sem("spatial_done")
        self.wout_done = sem("wout_done")
        self.gate_done = sem("gate_done")
        self.gate_ready = sem("gate_ready")
        self.p_turned = sem("p_turned")
        self.pT_ready = sem("pT_ready")
        self.proj_done = sem("proj_done")
        self.ple_ready = sem("ple_ready")
        self.lb_vec = sem("lb_vec")
        self.lb_act = sem("lb_act")
        self.rope_vec = sem("rope_vec")
        self.rope_ready = sem("rope_ready")
        self.rowsT_done = sem("rowsT_done")
        self.out_ready = sem("out_ready")
        self.out_stored = sem("out_stored")
        self.conv_products = sem("conv_products")
        self.conv_ready = sem("conv_ready")
        self.conv_copied = sem("conv_copied")
        self.mixed_done = sem("mixed_done")
        self.blank_ready = sem("blank_ready")
        self.y_cleared = sem("y_cleared")
        self.const2_loaded = sem("const2_loaded")
        self.final_loaded = sem("final_loaded")
        self.mla_down_done = sem("mla_down_done")
        self.mla_normed = sem("mla_normed")
        self.mla_turned = sem("mla_turned")
        self.mla_latents = sem("mla_latents")
        self.mla_copied = sem("mla_copied")
        self.mla_products = sem("mla_products")
        self.mla_roped = sem("mla_roped")
        self.mla_scores = sem("mla_scores")
        self.mla_probs = sem("mla_probs")
        self.mla_probs_turned = sem("mla_probs_turned")
        self.mla_probsT = sem("mla_probsT")
        self.mla_pv = sem("mla_pv")
        self.mla_out = sem("mla_out")
        self.mla_lat_copied = sem("mla_lat_copied")
        self.mla_masked = sem("mla_masked")


class MoeSemaphores:

    def __init__(self, sem):
        self.router_loaded = sem("router_loaded")
        self.x_stored = sem("x_stored")
        self.logits = sem("logits")
        self.vec_step = sem("vec_step")
        self.act_step = sem("act_step")
        self.counted = sem("counted")
        self.tables = sem("tables")
        self.routed = sem("routed")
        self.index_ready = sem("index_ready")
        self.gathered = sem("gathered")
        self.xg_turned = sem("xg_turned")
        self.xgT_ready = sem("xgT_ready")
        self.gateup = sem("gateup")
        self.silu = sem("silu")
        self.hidden = sem("hidden")
        self.y_copied = sem("y_copied")
        self.y_stored = sem("y_stored")




def build(nc, A, out, x_table, y_table):
    ctx = ExitStack()
    with ctx:
        def sb(name, shape, dt=F32):
            return ctx.enter_context(nc.sbuf_tensor(name, shape, dt))

        S = Semaphores(lambda name: ctx.enter_context(nc.semaphore(name)))
        S_mla = [ctx.enter_context(nc.semaphore(f"mla_loaded{i}")) for i in range(5)]
        taken = [[ctx.enter_context(nc.semaphore(f"moe{i}_taken{t}")) for t in range(3)] for i in range(DEPTH)]
        unit_loaded = [ctx.enter_context(nc.semaphore(f"unit_loaded{i}")) for i in range(SLOTS)]
        unit_free = [ctx.enter_context(nc.semaphore(f"unit_free{i}")) for i in range(SLOTS)]

        ring = sb("ring", [P, SLOTS, UNIT])
        h = sb("h", [P, 3, D])
        xn = sb("xn", [P, 3, D])
        xT = sb("xT", [P, KD, T2])
        const = sb("const", [P, NCONST])
        gT1 = sb("gT1", [P, P])
        gT2 = sb("gT2", [P, P])
        small = sb("small", [P, 256])
        rows = sb("rows", [P, 4, D])
        arena = sb("arena", [P, ARENA])
        PS = ctx.enter_context(nc.psum_tensor("PS", [P, 8, 512], F32))

        rowsf = rows[:, :, :].rearrange("p a b -> p (a b)")
        const2 = rowsf[:, 0:NCONST2]
        xT2 = rowsf[:, 1024:1024 + KD * T2].rearrange("p (k t) -> p k t", k=KD)

        def cst(name):
            o, n = CONST_AT[name]
            return const2[:, o:o + n] if name in SECOND else const[:, o:o + n]

        ident = cst("ident")
        row_at, n_rows2 = row_starts({k: A[k].shape for k in ROWS2})

        ss = small[:, 0:8]
        ms = small[:, 8:16]
        rs = small[:, 16:24]
        mean = small[:, 24:26]
        lb = small[:, 32:44].rearrange("p (l v c) -> p l v c", l=2, v=3)
        lbl = small[:, 44:50].rearrange("p (v c) -> p v c", v=3)
        smax = small[:, 56:64]
        sneg = small[:, 64:72]
        ssink = small[:, 72:80]
        ssum = small[:, 80:88]
        sden = small[:, 88:96]
        srden = small[:, 96:104]
        posf = small[:, 104:106]
        posi = small[:, 106:108].bitcast(I32)
        lbt = small[:, 108:124]
        gl = sb("gl", [P, 8 * KD])
        rope_cos = sb("rope_cos", [P, 2, 32])[:, :, :]
        rope_sin = sb("rope_sin", [P, 2, 32])[:, :, :]
        sgw = sb("sgw", [P, 4, P])
        sgb = sb("sgb", [P, 4])
        lng = sb("lng", [P, 256])
        hgn = sb("hgn", [P, HD])
        sinks = sb("sinks", [P, 8])

        def take(at, shape):
            n = int(np.prod(shape))
            assert at + n <= ARENA, (at, shape)
            v = arena[:, at:at + n]
            if len(shape) == 2:
                v = v.rearrange("p (a b) -> p a b", a=shape[0])
            elif len(shape) == 3:
                v = v.rearrange("p (a b c) -> p a b c", a=shape[0], b=shape[1])
            elif len(shape) == 4:
                v = v.rearrange("p (a b c d) -> p a b c d", a=shape[0], b=shape[1], c=shape[2])
            return v

        silu = take(0, [2, 256])
        hid = take(512, [2, 256])
        z = take(0, [2, 1792])
        qT = take(3584, [2, 256])
        fs = take(4096, [2, 256])
        w1 = take(4608, [2, 256])
        w2 = take(5120, [2, 256])
        w3 = take(5632, [2, 256])
        w4 = take(6144, [2, 256])
        w5 = take(6656, [2, 256])
        w6 = take(7168, [2, 256])
        kT = take(7680, [2, 256])
        dif = take(5120, [2, 2, 256])
        ex = take(8192, [2, 2, 256])
        lev = take(9216, [2, 2, 256])
        att = xn[:, 2, :].rearrange("p (a b c q) -> p a b c q", a=2, b=2, c=2)
        att10 = take(11520, [2, 2, P])
        rprod = take(4608, [4, 1280 // 2])
        rot = take(8192, [2, 640])
        qkT = take(10240, [5, 256])
        ssb = take(3584, [8, 256])
        pT_ = take(7680, [8, 2, P])
        lnw = take(5760, [2, 256])
        sgwT = take(6272, [4, P])
        sgm_mix = take(6784, [2, 256])
        sgm = take(0, [2, D])
        pleT = take(2048, [2, 256])

        def xcol(t):
            return slice(META + P * t, META + P * (t + 1)) if t < 2 else slice(0, META)

        def yps(t):
            return PS[:, 2 * t:2 * t + 2, :]

        def tile2(v):
            return v.rearrange("p (a b) -> p a b", a=2)

        def slot_w(slot, k, w):
            return ring[:, slot, 0:k * w].rearrange("p (k w) -> p k w", k=k)

        x_in = A["x"].rearrange("o (t p) d -> p (o t) d", p=P)
        block = ctx.enter_context(nc.Block())
        U_FFN1, U_IN, U_OUT, U_FFN2, U_PLE, U_LAYER = 0, 11, 16, 18, 29, 32
        USES = U_LAYER // SLOTS
        IN_COLS = [(0, 512), (512, 512), (1024, 512), (1536, 256), (1792, 512)]
        Z_AT = [None, 0, 512, 1024, 1280]


        G2 = {k: row_at[k] for k in ROWS2}

        def cols(name, n, first=0):
            return gT2[:, G2[name] + first:G2[name] + first + n]

        moe_loaded = [[ctx.enter_context(nc.semaphore(f"moe{i}_loaded{s}")) for s in range(SLOTS)] for i in range(DEPTH)]
        moe_free = [[ctx.enter_context(nc.semaphore(f"moe{i}_free{s}")) for s in range(SLOTS)] for i in range(DEPTH)]
        M = [MoeSemaphores(lambda name: ctx.enter_context(nc.semaphore(f"moe{i}_{name}"))) for i in range(DEPTH)]

        cb = take(0, [2, 2, T2])
        zp = take(1088, [2, T2 + 2])
        cy = take(1636, [2, T2])
        convT = take(2180, [KD, T2])
        wr = take(0, [KD, NG + NE])
        lg2 = take(576, [3, NG + NE])
        r8 = [take(800 + 24 * i, [3, 8]) for i in range(10)]
        r1 = [arena[:, 1044 + 4 * i:1047 + 4 * i] for i in range(12)]
        e1, e2, msel, rsel, ta, tb = [take(1100 + 192 * i, [3, NE]) for i in range(6)]
        thr = take(2252, [NE, 8])
        nblk, bend, bstart = [arena[:, 2764 + 64 * i:2828 + 64 * i] for i in range(3)]
        GC = MAX_GROUPS + 1
        cmpg = take(2960, [3, MAX_GROUPS])
        a1, a2 = take(3100, [3, P]), take(3484, [3, P])
        b1, b2 = take(3868, [3, GC]), take(3940, [3, GC])
        dg = arena[:, 4010:4074]
        endcol = arena[:, 4075:4076]
        cmpe = arena[:, 4076:4172]
        eid = arena[:, 4172:4268].bitcast(I32)
        slot_tok = arena[:, 4268:4268 + GC].bitcast(I32)
        ng = arena[:, 4294:4295].bitcast(I32)
        idxc = arena[:, 4296:4297].bitcast(I32)
        posi2 = arena[:, 4298:4304].bitcast(I32)
        cmpk = arena[:, 4304:4328]
        ngf = arena[:, 4328:4329]
        xg = arena[:, 4400:5424]
        xgT = take(5424, [KD, P])
        sl = take(6448, [2, 2, BLK])
        hh = take(6576, [2, 2, BLK])
        ysb = arena[:, 6704:7728]
        ybuf = [[arena[:, o:o + D] for o in (4400 + 2304 * 0, 5424)], [arena[:, o:o + D] for o in (6704, 7728)],
                [arena[:, o:o + D] for o in (8752, 9776)]]
        wgt = {i: arena[:, 10800 + 4 * i:10803 + 4 * i] for i in range(2)}

        lat = take(0, [3, KV_RANK + ROPE2 + Q_RANK])
        ckvT = take(2112, [2, T2])
        cqT = take(2656, [3, T2])
        krT = arena[:, 3472:3472 + T2]
        qrT = take(3744, [NH2 // 2, T2])
        val = take(4832, [3, NH2 * P])
        qr = take(7904, [3, NH2 * ROPE2])
        qro = take(9440, [3, NH2 * ROPE2])
        kro = take(10976, [3, 2, ROPE2])
        knT, qnT = xT2, xT
        prob = [take(0, [4, T2]), take(1088, [4, T2])]
        probT = [take(7904, [4, 3, P]), take(9440, [4, 3, P])]
        STEPS = [(t, hf) for t in range(3) for hf in range(2)]

        def keys(t):
            return {0: (META + P, [0, 2]), 1: (T2, [0, 1, 2]), 2: (META, [2])}[t]

        def mla_weights(sp, groups):
            def load(n, slot, parts):
                for dst, src in parts:
                    sp.dma_start(dst, src).then_inc(S_mla[n], 16)
            for j in range(3 + 1):
                sp.wait_ge(moe_free[0][j], groups + 1)
                if j == 0:
                    dkv, dq = mla_down_views()
                    load(0, 0, [(dkv, A["w_dkv_2"].rearrange("(k p) f -> p k f", p=P)),
                                (dq[:, 0:4], A["w_dq_2"][0].rearrange("(k p) f -> p k f", p=P)[:, 0:4]),
                                (dq[:, 4:8], A["w_dq_2"][0].rearrange("(k p) f -> p k f", p=P)[:, 4:8])])
                elif j == 1:
                    src, dst = A["w_ukv_2"].rearrange("(k p) f -> p k f", p=P), slot_w(1, 2, 2 * D)
                    load(1, 1, [(dst[:, k:k + 1], src[:, k:k + 1]) for k in range(2)])
                elif j == 2:
                    src, dst = A["w_uq_2"][0].rearrange("(k p) f -> p k f", p=P), slot_w(2, 3, 1536)
                    load(2, 2, [(dst[:, k:k + 1], src[:, k:k + 1]) for k in range(3)])
            wo = A["w_o_2"][0].rearrange("(k p) f -> p k f", p=P)
            load(3, 3, [(slot_w(3, KD, 512)[:, a:a + 4], wo[:, a:a + 4, 0:512]) for a in (0, 4)])
            sp.wait_ge(S.mla_down_done, 1)
            load(4, 0, [(slot_w(0, KD, 512)[:, a:a + 4], wo[:, a:a + 4, 512:1024]) for a in (0, 4)])

        MLA_LOADS = [3, 2, 3, 2, 2]

        def mla_down_views():
            return (ring[:, 0, 0:KD * 320].rearrange("p (k f) -> p k f", k=KD),
                    ring[:, 0, KD * 320:KD * 704].rearrange("p (k f) -> p k f", k=KD))

        def mla_pe(pe, turn):
            mm = nc.tensor.matmul
            turn(12, 3)
            dkv, dq = mla_down_views()
            pe.wait_ge(S_mla[0], 16 * MLA_LOADS[0])
            for t in range(3):
                dense_rows(xT2, dkv, 5 + t, t, 320, KD)
                last = dense_rows(xT, dq, t, t, 384, KD)
            last.then_inc(S.mla_down_done, 1)
            pe.wait_ge(S.mla_normed, 1)
            for t in range(3):
                w = META if t == 2 else P
                for bank, c0 in ((3, 0), (4, P), (5, 320), (6, 320 + P), (7, 320 + 2 * P)):
                    nc.tensor.transpose(PS[:, bank, xcol(t)], lat[0:w, t, c0:c0 + P], ident[0:w, 0:w])
                last = nc.tensor.transpose(PS[:, 0, xcol(t)], kro[0:w, t].rearrange("p a b -> p (a b)"), ident[0:w, 0:w])
            last.then_inc(S.mla_turned, 1)
            pe.wait_ge(S.mla_latents, 1)
            ukv = slot_w(1, 2, 2 * D).rearrange("p k (h f) -> p k h f", h=NH2)
            uq = slot_w(2, 3, 1536).rearrange("p k (h f) -> p k h f", h=NH2)
            n = 0

            def bank_of(n):
                if n >= 8:
                    pe.wait_ge(S.mla_copied, n - 7)
                return n % 8
            pe.wait_ge(S_mla[2], 16 * MLA_LOADS[2])
            for t in range(3):
                w, b = (META if t == 2 else P), bank_of(n)
                for k in range(3):
                    last = mm(PS[0:w, b, :], lhsT=cqT[:, k, xcol(t)], rhs=uq[:, k, :, P:P + ROPE2], start=k == 0, stop=k == 2)
                last.then_inc(S.mla_products, 1)
                n += 1
            pe.wait_ge(S_mla[1], 16 * MLA_LOADS[1])
            for wt, src, kk in ((ukv, ckvT, 2), (uq, cqT, 3)):
                for hd in range(NH2):
                    b = bank_of(n)
                    for k in range(kk):
                        last = mm(PS[:, b, 0:T2], lhsT=wt[:, k, hd, 0:P], rhs=src[:, k, :], start=k == 0, stop=k == kk - 1)
                    last.then_inc(S.mla_products, 1)
                    n += 1
            for t in range(3):
                w = META if t == 2 else P
                for hf in range(2):
                    b = bank_of(n)
                    for k in range(2):
                        last = mm(PS[0:w, b, :], lhsT=ckvT[:, k, xcol(t)], rhs=ukv[:, k, 4 * hf:4 * hf + 4, P:2 * P],
                                  start=k == 0, stop=k == 1)
                    last.then_inc(S.mla_products, 1)
                    n += 1
            pe.wait_ge(S.mla_roped, 1)
            for pair in range(NH2 // 2):
                b = bank_of(n)
                for t in range(3):
                    w = META if t == 2 else P
                    last = nc.tensor.transpose(PS[:, b, xcol(t)], qro[0:w, t, pair * P:(pair + 1) * P], ident[0:w, 0:w])
                last.then_inc(S.mla_products, 1)
                n += 1
            assert n == MLA_ITEMS
            pe.wait_ge(S.mla_copied, MLA_ITEMS)

            def scores(s):
                (t, hf), nk = STEPS[s], keys(STEPS[s][0])[0]
                w = META if t == 2 else P
                if s >= 2:
                    pe.wait_ge(S.mla_out, s - 1)
                for i in range(4):
                    hd = 4 * hf + i
                    r = slice(64 * (hd % 2), 64 * (hd % 2) + 64)
                    o = PS[0:w, 4 * (s % 2) + i, 0:nk]
                    mm(o, lhsT=qnT[:, hd, xcol(t)], rhs=knT[:, hd, 0:nk], start=True, stop=False)
                    last = mm(o, lhsT=qrT[r, hd // 2, xcol(t)], rhs=krT[r, 0:nk], start=False, stop=True)
                last.then_inc(S.mla_scores, 1)

            def outputs(s):
                (t, hf), pieces = STEPS[s], keys(STEPS[s][0])[1]
                w, b = (META if t == 2 else P), 4 * (s % 2)
                pe.wait_ge(S.mla_probs, s + 1)
                for i in range(4):
                    for c in pieces:
                        ck = META if c == 2 else P
                        last = nc.tensor.transpose(PS[0:ck, b + i, c * P:c * P + w], prob[s % 2][0:w, i, xcol(c)], ident[0:w, 0:w])
                last.then_inc(S.mla_probs_turned, 1)
                pe.wait_ge(S.mla_probsT, s + 1)
                for i in range(4):
                    hd = 4 * hf + i
                    for n_, c in enumerate(pieces):
                        ck = META if c == 2 else P
                        last = mm(PS[0:w, b, i * P:(i + 1) * P], lhsT=probT[s % 2][0:ck, i, c, 0:w],
                                  rhs=val[0:ck, c, hd * P:(hd + 1) * P], start=n_ == 0, stop=n_ == len(pieces) - 1)
                last.then_inc(S.mla_pv, 1)
            scores(0)
            for s in range(len(STEPS)):
                if s + 1 < len(STEPS):
                    scores(s + 1)
                outputs(s)
            turn(13, 3)
            for i, (slot, n) in enumerate([(3, 3), (0, 4)]):
                pe.wait_ge(S_mla[n], 16 * MLA_LOADS[n])
                for t in range(3):
                    last = dense_rows(xT, slot_w(slot, KD, 512), 2 * t + i, t, 512, KD)
            last.then_inc(S.mixed_done, 1)

        MLA_ITEMS = 3 + 2 * NH2 + 6 + NH2 // 2

        def mla_act(act, norm):
            a_ = nc.scalar
            norm(10, 3)
            act.wait_ge(S.mla_lat_copied, 1)
            for r, c0, n in ((23, 0, KV_RANK), (24, 320, Q_RANK)):
                act.wait_ge(S.ms_ready, r)
                for t in range(3):
                    w = META if t == 2 else P
                    last = a_.activation(xn[0:w, t, 0:n], lat[0:w, t, c0:c0 + n], ACT.Square, accum_out=ss[0:w, t:t + 1])
                last.then_inc(S.square_done, 1)
                if r == 23:
                    act.drain()
            n = 0

            def copy(dst, w, cols_):
                nonlocal n
                act.wait_ge(S.mla_products, n + 1)
                a_.activation(dst, PS[0:w, n % 8, 0:cols_], ACT.Copy).then_inc(S.mla_copied, 1)
                n += 1
            for t in range(3):
                w = META if t == 2 else P
                copy(qr[0:w, t, :], w, 512)
            for dst in (knT, qnT):
                for hd in range(NH2):
                    copy(dst[:, hd, :], P, T2)
            for t in range(3):
                for hf in range(2):
                    w = META if t == 2 else P
                    copy(val[0:w, t, hf * 512:(hf + 1) * 512], w, 512)
            for pair in range(NH2 // 2):
                copy(qrT[:, pair, :], P, T2)
            for s, (t, hf) in enumerate(STEPS):
                w, (nk, pieces), b = (META if t == 2 else P), keys(t), 4 * (s % 2)
                act.wait_ge(S.mla_masked, s + 1)
                for i in range(4):
                    last = a_.activation(prob[s % 2][0:w, i, 0:nk], prob[s % 2][0:w, i, 0:nk], ACT.Exp,
                                         bias=sneg[0:w, b + i:b + i + 1], accum_out=ssum[0:w, b + i:b + i + 1])
                last.then_inc(S.mla_probs, 1)
                act.wait_ge(S.mla_probs_turned, s + 1)
                nx = len(pieces) - 1
                if nx:
                    a_.activation(probT[s % 2][:, :, 0:nx, :], PS[:, b:b + 4, 0:nx * P].rearrange("p i (c q) -> p i c q", q=P), ACT.Copy)
                a_.activation(probT[s % 2][0:META, :, 2, 0:w], PS[0:META, b:b + 4, 2 * P:2 * P + w], ACT.Copy).then_inc(S.mla_probsT, 1)
            act.wait_ge(S.h_upd, 12)
            act.dma_start(rows[:, 3, :], A["final_norm_g_2"].unsqueeze(0).to_broadcast([P, D])).then_inc(S.final_loaded, 16)

        def mla_vec(dve, rstd, turned, norm):
            v_, settle = nc.vector, dve.drain
            norm(22, 12, [(xT, cols("norm_mix_g_2", 8, 8)), (xT2, cols("kv_norm_g_2", 8))], 3)
            dve.wait_ge(S.mla_down_done, 1)
            for t in range(3):
                w = META if t == 2 else P
                v_.tensor_copy(lat[0:w, t, 0:320], PS[0:w, 5 + t, 0:320])
                last = v_.tensor_copy(lat[0:w, t, 320:704], PS[0:w, t, 0:384])
            last.then_inc(S.mla_lat_copied, 1)
            settle()

            def rotate(w, ts, x, heads, out, scratch):
                nt = ts.stop - ts.start
                cs, sn = [cst(n).rearrange("p (t d) -> p t d", d=32)[0:w, ts].unsqueeze(2).to_broadcast([w, nt, heads, 32])
                          for n in ("cos2", "sin2")]
                size = nt * heads * 32
                pr = [scratch[0:w, i * size:(i + 1) * size].rearrange("p (t h d) -> p t h d", t=nt, d=32) for i in range(4)]
                for p_, (e, c) in zip(pr, [(0, cs), (1, sn), (0, sn), (1, cs)]):
                    v_.tensor_tensor(p_, x[:, :, :, e, :], c, ALU.mult)
                settle()
                outs = []
                for e, (a, b, op) in enumerate([(pr[0], pr[1], ALU.subtract), (pr[2], pr[3], ALU.add)]):
                    o = out(e)
                    if o.shape[2] != heads:
                        a, b = a.to_broadcast([w, nt, o.shape[2], 32]), b.to_broadcast([w, nt, o.shape[2], 32])
                    outs.append(v_.tensor_tensor(o, a, b, op))
                return outs[-1]

            TILES = ((P, slice(0, 2)), (META, slice(2, 3)))
            for w, ts in TILES:
                rotate(w, ts, lat[0:w, ts, KV_RANK:320].rearrange("p t (h e d) -> p t h e d", h=1, e=2), 1,
                       lambda e: kro[0:w, ts, :, e * 32:(e + 1) * 32], arena[:, 11360:11744])
                settle()
            for r, c0, n in ((23, 0, KV_RANK), (24, 320, Q_RANK)):
                rstd(r, 3, n)
                for t in range(3):
                    w = META if t == 2 else P
                    last = v_.tensor_scalar(lat[0:w, t, c0:c0 + n], lat[0:w, t, c0:c0 + n], rs[0:w, t:t + 1], None, ALU.mult)
            last.then_inc(S.mla_normed, 1)
            dve.wait_ge(S.mla_turned, 1)
            for k in range(2):
                v_.tensor_scalar(ckvT[:, k, :], PS[:, 3 + k, 0:T2], cols("ckv_norm_g_2", 1, k), None, ALU.mult)
            for k in range(3):
                v_.tensor_scalar(cqT[:, k, :], PS[:, 5 + k, 0:T2], cols("cq_norm_g_2", 1, k), None, ALU.mult)
            v_.tensor_copy(krT, PS[:, 0, 0:T2]).then_inc(S.mla_latents, 1)
            dve.wait_ge(S.mla_copied, 3)
            scratch = xn[:, :, :].rearrange("p t d -> p (t d)")
            for w, ts in TILES:
                x = qr[0:w, ts].rearrange("p t (h e d) -> p t h e d", h=NH2, e=2)
                y = qro[0:w, ts].rearrange("p t (h e d) -> p t h e d", h=NH2, e=2)
                last = rotate(w, ts, x, NH2, lambda e: y[:, :, :, e, :], scratch)
                if ts.start == 0:
                    settle()
            last.then_inc(S.mla_roped, 1)

            def masked(s):
                (t, hf), nk, b = STEPS[s], keys(STEPS[s][0])[0], 4 * (s % 2)
                w = META if t == 2 else P
                dve.wait_ge(S.mla_scores, s + 1)
                pv = prob[s % 2][0:w, :, 0:nk]
                v_.scalar_tensor_tensor(pv, PS[0:w, b:b + 4, 0:nk], (P + ROPE2) ** -0.5,
                                        cst(f"causal{t}")[0:w, 0:nk].unsqueeze(1).to_broadcast([w, 4, nk]), ALU.mult, ALU.add)
                settle()
                v_.tensor_reduce(smax[0:w, b:b + 4], pv, AX.X, ALU.max)
                settle()
                v_.tensor_scalar(sneg[0:w, b:b + 4], smax[0:w, b:b + 4], -1.0, None, ALU.mult).then_inc(S.mla_masked, 1)
            masked(0)
            for s, (t, hf) in enumerate(STEPS):
                w, b = (META if t == 2 else P), 4 * (s % 2)
                if s + 1 < len(STEPS):
                    masked(s + 1)
                dve.wait_ge(S.mla_pv, s + 1)
                v_.reciprocal(srden[0:w, b:b + 4], ssum[0:w, b:b + 4])
                settle()
                v_.tensor_tensor(xn[0:w, t, hf * 512:(hf + 1) * 512].rearrange("p (h e) -> p h e", e=P),
                                 PS[0:w, b, :].rearrange("p (h e) -> p h e", e=P),
                                 srden[0:w, b:b + 4].unsqueeze(2).to_broadcast([w, 4, P]), ALU.mult).then_inc(S.mla_out, 1)
            dve.drain().then_inc(S.xn_ready, 1)
            turned(13, 3, [(xT, None)])
            dve.wait_ge(S.mixed_done, 2)
            add_to_h()

        def second_weights(sp, load):
            bcu = A["conv_w_in_2"][0].rearrange("(k p) f -> p k f", p=P)
            for i in range(4):
                v = ring[:, i, :].rearrange("p (s k f) -> p s k f", s=3, k=KD)
                load(16, i, [(v[:, s], bcu[:, :, s * D + 256 * i:s * D + 256 * (i + 1)]) for s in range(3)])
            for i in range(2):
                w = A["conv_w_out_2"][0].rearrange("(k p) f -> p k f", p=P)
                dst = slot_w(i, KD, 512)
                load(17, i, [(dst[:, a:b], w[:, a:b, 512 * i:512 * (i + 1)]) for a, b in ((0, 3), (3, 6), (6, 8))])
            groups = experts(sp, 0)
            mla_weights(sp, groups)
            experts(sp, 1)

        def experts(sp, i):
            sp.wait_ge(M[i].routed, 1)
            groups = sp.value_load(ng[0:1, 0:1], min_val=1, max_val=MAX_GROUPS)
            with sp.Fori(0, groups) as g:
                for j in range(GROUP):
                    e = sp.value_load(eid[0:1, bass.ds(g * GROUP + j, 1)], min_val=0, max_val=NE - 1)
                    sp.wait_ge(moe_free[i][j], g + 1)
                    v = ring[:, j, 0:4096].rearrange("p (s k f) -> p s k f", s=2, k=KD)
                    for s, name in enumerate(("w_gate_2", "w_up_2")):
                        sp.dma_start(v[:, s], A[name][i][bass.ds(e, 1)].rearrange("o (k p) f -> p (o k) f", p=P)).then_inc(moe_loaded[i][j], 16)
                    sp.dma_start(ring[:, j, 4096:6144].rearrange("p (f n) -> p f n", f=2),
                                 A["w_down_2"][i][bass.ds(e, 1)].rearrange("o (f p) n -> p (o f) n", p=P)).then_inc(moe_loaded[i][j], 16)
            return groups

        def second_pool(pool, rstd):
            rstd(20, 3)
            rstd(21, 3)
            moe_pool(pool, 0)
            rstd(22, 3)
            rstd(23, 3)
            rstd(24, 3)
            rstd(25, 3)
            moe_pool(pool, 1)
            rstd(26, 2)

        def moe_pool(pool, i):
            def gather(n):
                pool.wait_ge(M[i].index_ready, n)
                pool.sem_inc(S.pad, 1)
                nc.gpsimd.indirect_dma_start(out=xg, out_offset=None, in_=x_table,
                                             in_offset=bass.IndirectOffsetOnAxis(idxc, 0)).then_inc(M[i].gathered, 16)
            pool.wait_ge(M[i].routed, 1)
            groups = pool.value_load(ng[0:1, 0:1], min_val=1, max_val=MAX_GROUPS)
            pool.wait_ge(M[i].x_stored, 32)
            gather(1)
            with pool.Fori(0, groups) as g:
                gather(g + 2)
            pool.wait_ge(M[i].gathered, groups * 16 + 16)
            pool.sem_inc(S.pad, 1)
            pool.wait_ge(M[i].y_stored, groups * 16 + 16)
            pool.sem_inc(S.pad, 1)
            for t in range(3):
                w = META if t == 2 else P
                for c in range(2):
                    nc.gpsimd.indirect_dma_start(out=ybuf[t][c][0:w, :], out_offset=None, in_=y_table,
                                                 in_offset=bass.IndirectOffsetOnAxis(posi2[0:w, 3 * c + t:3 * c + t + 1], 0)
                                                 ).then_inc(taken[i][t], 16)

        def second_act(act, norm, squares):
            a_ = nc.scalar
            act.wait_ge(S.h_upd, 9)
            act.dma_start(const2, A["const_table2"]).then_inc(S.const2_loaded, 16)
            norm(8, 3)
            for x in range(KD):
                act.wait_ge(S.conv_products, x + 1)
                if x >= 2:
                    act.wait_ge(S.conv_ready, x - 1)
                for s in range(2):
                    last = a_.activation(cb[:, x % 2, s, :], PS[:, 3 * (x % 2) + s, 0:T2], ACT.Copy)
                last.then_inc(S.conv_copied, 1)
            moe_act(act, 0, norm, 9)
            mla_act(act, norm)
            moe_act(act, 1, norm, 11)
            act.wait_ge(S.h_upd, 13)
            squares(0, 2, lambda t: h[:, t, :])

        def moe_act(act, i, norm, n):
            a_ = nc.scalar
            act.wait_ge(S.h_upd, n + 1)
            with nc.allow_non_contiguous_dma(reason="short rows"):
                act.dma_start(wr[:, :, 0:NG], A["w_grp_2"][i].rearrange("(k p) f -> p k f", p=P)).then_inc(M[i].router_loaded, 16)
            act.dma_start(wr[:, :, NG:], A["w_exp_2"][i].rearrange("(k p) f -> p k f", p=P)).then_inc(M[i].router_loaded, 16)
            norm(n, 3)
            act.wait_ge(S.xn_ready, 12 if i == 0 else 15)
            act.dma_start(x_table[0:2 * P, :].rearrange("(t p) d -> p t d", p=P), xn[:, 0:2, :]).then_inc(M[i].x_stored, 16)
            act.dma_start(x_table[2 * P:T2, :], xn[0:META, 2, :]).then_inc(M[i].x_stored, 16)
            act.wait_ge(M[i].vec_step, 1)
            a_.activation(r8[2], r8[1], ACT.Exp).then_inc(M[i].act_step, 1)
            act.wait_ge(M[i].vec_step, 2)
            a_.activation(r1[4], r1[3], ACT.Exp).then_inc(M[i].act_step, 1)
            act.wait_ge(M[i].routed, 1)
            groups = act.value_load(ng[0:1, 0:1], min_val=1, max_val=MAX_GROUPS)
            act.sem_inc(M[i].y_copied, 1)
            act.sem_inc(M[i].y_stored, 16)
            with act.Fori(0, groups) as g:
                for j in range(GROUP):
                    act.wait_ge(M[i].gateup, g * GROUP + j + 1)
                    act.wait_ge(M[i].hidden, g * GROUP + j + 1)
                    a_.activation(sl[:, j % 2], PS[:, 2 + j % 2, 0:2 * BLK].rearrange("p (f c) -> p f c", f=2),
                                  ACT.Silu).then_inc(M[i].silu, 1)
                act.wait_ge(moe_free[i][GROUP - 1], g + 2)
                act.wait_ge(M[i].y_stored, g * 16 + 16)
                a_.activation(tile2(ysb), PS[:, 4:6, :], ACT.Copy).then_inc(M[i].y_copied, 1)
                act.wait_ge(M[i].y_copied, g + 2)
                act.dma_start(y_table[bass.ds(g * P, P), :], ysb).then_inc(M[i].y_stored, 16)

        def second_vec(dve, rstd, turned, norm):
            v_, settle = nc.vector, dve.drain
            v_.memset(zp[:, :, 0:2], 0.0)
            norm(20, 10, [(xT, cols("norm_mix_g_2", 8))], 3)
            for x in range(KD):
                b = x % 2
                dve.wait_ge(S.conv_copied, x + 1)
                v_.tensor_tensor(zp[:, b, 2:], cb[:, b, 1, :], PS[:, 3 * b + 2, 0:T2], ALU.mult)
                settle()
                w = [cols("conv_w_2", 1, 8 * k + x) for k in range(3)]
                v_.tensor_scalar(cy[:, b, :], zp[:, b, 0:T2], w[0], None, ALU.mult)
                settle()
                for k in (1, 2):
                    v_.scalar_tensor_tensor(cy[:, b, :], zp[:, b, k:k + T2], w[k], cy[:, b, :], ALU.mult, ALU.add)
                    settle()
                v_.tensor_tensor(convT[:, x, :], cy[:, b, :], cb[:, b, 0, :], ALU.mult).then_inc(S.conv_ready, 1)
            dve.wait_ge(S.mixed_done, 1)
            add_to_h()
            moe_vec(dve, 0, rstd, turned, norm, 21, 11)
            mla_vec(dve, rstd, turned, norm)
            moe_vec(dve, 1, rstd, turned, norm, 25, 14)
            rstd(26, 2, D)
            dve.wait_ge(S.final_loaded, 16)
            for t in range(2):
                last = v_.scalar_tensor_tensor(xn[:, t, :], h[:, t, :], rs[:, t:t + 1], rows[:, 3, :], ALU.mult, ALU.mult)
            last.then_inc(S.out_ready, 1)

        def add_to_h():
            for t in range(3):
                w = META if t == 2 else P
                last = nc.vector.tensor_tensor(tile2(h[0:w, t, :]), tile2(h[0:w, t, :]), PS[0:w, 2 * t:2 * t + 2, :], ALU.add)
            last.then_inc(S.h_upd, 1)

        def moe_vec(dve, i, rstd, turned, norm, r, q):
            v_, settle = nc.vector, dve.drain
            dve.wait_ge(S.const2_loaded, 16)
            iota = cst("iota")
            iota8 = iota[:, 0:8].unsqueeze(1).to_broadcast([P, 3, 8])

            def b8(v):
                return v.unsqueeze(2).to_broadcast([P, 3, 8])

            def first_of(dst, vals, top, cand, least):
                v_.tensor_tensor(cand, vals, b8(top), ALU.is_equal)
                settle()
                v_.scalar_tensor_tensor(cand, cand, -1000.0, iota8, ALU.mult, ALU.add)
                settle()
                v_.tensor_reduce(least, cand, AX.X, ALU.min)
                settle()
                v_.tensor_tensor(dst, cand, b8(least), ALU.is_equal)

            norm(r, q, [(xT, cols("norm_ffn_g_2", 8, 8 * i))], 3)
            v_.memset(lg2, 0.0)
            settle()
            dve.wait_ge(M[i].logits, 1)
            v_.tensor_copy(lg2[:, 0:2, :], PS[:, 5, 0:144].rearrange("p (t c) -> p t c", t=2))
            v_.tensor_copy(lg2[0:META, 2, :], PS[0:META, 5, 144:216])
            settle()
            gl8 = lg2[:, :, 0:NG]
            v_.tensor_reduce(r1[0], gl8, AX.X, ALU.max)
            settle()
            v_.tensor_tensor(r8[1], gl8, b8(r1[0]), ALU.subtract).then_inc(M[i].vec_step, 1)
            first_of(r8[3], gl8, r1[0], r8[0], r1[1])
            settle()
            tmp = e1.rearrange("p t (e g) -> p t e g", e=8)
            v_.tensor_tensor(tmp, lg2[:, :, NG:].rearrange("p t (g e) -> p t e g", g=NG),
                             r8[3].unsqueeze(2).to_broadcast([P, 3, 8, 8]), ALU.mult)
            settle()
            v_.tensor_reduce(r8[4], tmp, AX.X, ALU.add)
            settle()
            v_.tensor_reduce(r1[1], r8[4], AX.X, ALU.max)
            settle()
            first_of(r8[5], r8[4], r1[1], r8[0], r1[2])
            settle()
            v_.scalar_tensor_tensor(r8[6], r8[5], -1e30, r8[4], ALU.mult, ALU.add)
            settle()
            v_.tensor_reduce(r1[2], r8[6], AX.X, ALU.max)
            settle()
            v_.tensor_tensor(r1[3], r1[2], r1[1], ALU.subtract).then_inc(M[i].vec_step, 1)
            first_of(r8[7], r8[6], r1[2], r8[0], r1[5])
            v_.tensor_tensor(r8[8], r8[3], b8(cst("valid")), ALU.mult)
            settle()
            for dst, one in ((e1, r8[5]), (e2, r8[7])):
                v_.tensor_tensor(dst.rearrange("p t (g e) -> p t g e", g=NG), r8[8].unsqueeze(3).to_broadcast([P, 3, 8, 8]),
                                 one.unsqueeze(2).to_broadcast([P, 3, 8, 8]), ALU.mult)
            settle()
            v_.tensor_tensor(msel, e1, e2, ALU.add).then_inc(M[i].vec_step, 1)
            dve.wait_ge(M[i].act_step, 2)
            v_.tensor_reduce(r1[6], r8[2], AX.X, ALU.add)
            v_.tensor_scalar(r1[7], r1[4], 1.0, None, ALU.add)
            settle()
            v_.tensor_tensor(r1[6], r1[6], r1[7], ALU.mult)
            settle()
            v_.reciprocal(wgt[0], r1[6])
            settle()
            v_.tensor_tensor(wgt[1], wgt[0], r1[4], ALU.mult)
            dve.wait_ge(M[i].counted, 1)
            cnt = PS[:, 6, 192:256]
            v_.tensor_tensor(thr, cnt.unsqueeze(2).to_broadcast([P, NE, 8]),
                             cst("block_starts").unsqueeze(1).to_broadcast([P, NE, 8]), ALU.is_gt)
            settle()
            v_.tensor_reduce(nblk, thr, AX.X, ALU.add)
            settle()
            v_.tensor_scalar(nblk, nblk, 1.0, None, ALU.add)
            settle()
            v_.tensor_tensor_scan(bend, cst("ones")[:, 0:NE], nblk, 0.0, ALU.mult, ALU.add)
            settle()
            v_.tensor_tensor(bstart, bend, nblk, ALU.subtract)
            v_.tensor_tensor(dg, bend, ident[:, 0:NE], ALU.mult)
            v_.tensor_scalar(cmpk, iota[:, 0:24], float(GROUP), bend[:, NE - 1:NE], ALU.mult, ALU.is_lt)
            settle()
            v_.tensor_reduce(endcol, dg, AX.X, ALU.add)
            v_.tensor_reduce(ngf, cmpk, AX.X, ALU.add)
            v_.scalar_tensor_tensor(rsel, bstart.unsqueeze(1).to_broadcast([P, 3, NE]), float(BLK),
                                    PS[:, 6, 0:192].rearrange("p (t e) -> p t e", t=3), ALU.mult, ALU.add)
            settle()
            v_.tensor_scalar(cmpe[0:NE, :], iota[0:NE, 0:96], endcol[0:NE, :], None, ALU.is_ge)
            v_.tensor_copy(ng, ngf)
            v_.tensor_tensor(ta, e1, rsel, ALU.mult)
            v_.tensor_tensor(tb, e2, rsel, ALU.mult)
            settle()
            v_.tensor_reduce(r1[8], ta, AX.X, ALU.add)
            v_.tensor_reduce(r1[9], tb, AX.X, ALU.add)
            settle()
            v_.tensor_copy(posi2[:, 0:3], r1[8])
            v_.tensor_copy(posi2[:, 3:6], r1[9])
            for pos, a, b in ((r1[8], a1, b1), (r1[9], a2, b2)):
                v_.tensor_tensor(cmpg, pos.unsqueeze(2).to_broadcast([P, 3, MAX_GROUPS]),
                                 cst("group_starts").unsqueeze(1).to_broadcast([P, 3, MAX_GROUPS]), ALU.is_ge)
                settle()
                v_.tensor_reduce(r1[10], cmpg, AX.X, ALU.add)
                settle()
                v_.scalar_tensor_tensor(r1[11], r1[10], -float(P), pos, ALU.mult, ALU.add)
                v_.tensor_tensor(b, iota[:, 0:GC].unsqueeze(1).to_broadcast([P, 3, GC]),
                                 r1[10].unsqueeze(2).to_broadcast([P, 3, GC]), ALU.is_equal)
                settle()
                v_.tensor_tensor(a, iota.unsqueeze(1).to_broadcast([P, 3, P]),
                                 r1[11].unsqueeze(2).to_broadcast([P, 3, P]), ALU.is_equal)
                v_.tensor_tensor(b, b, cst("token_id").unsqueeze(2).to_broadcast([P, 3, GC]), ALU.mult)
                settle()
                last = v_.tensor_tensor(b, b, cst("valid").unsqueeze(2).to_broadcast([P, 3, GC]), ALU.mult)
            last.then_inc(M[i].vec_step, 1)
            dve.wait_ge(M[i].tables, 1)
            v_.tensor_scalar(eid, PS[:, 7, 32:128], float(NE - 1), None, ALU.min)
            v_.tensor_copy(slot_tok, PS[:, 7, 0:GC]).then_inc(M[i].routed, 1)
            dve.wait_ge(M[i].routed, 1)
            groups = dve.value_load(ng[0:1, 0:1], min_val=1, max_val=MAX_GROUPS)
            dve.sem_inc(M[i].hidden, 2)
            v_.tensor_copy(idxc, slot_tok[:, 0:1]).then_inc(M[i].index_ready, 1)
            with dve.Fori(0, groups) as g:
                dve.wait_ge(M[i].xg_turned, g + 1)
                v_.tensor_tensor(xgT, PS[:, 0:2, :].rearrange("p a (k w) -> p (a k) w", w=P),
                                 cols("norm_ffn_g_2", 8, 8 * i).unsqueeze(2).to_broadcast([P, KD, P]), ALU.mult).then_inc(M[i].xgT_ready, 1)
                v_.tensor_copy(idxc, slot_tok[:, bass.ds(g + 1, 1)]).then_inc(M[i].index_ready, 1)
                for j in range(GROUP):
                    dve.wait_ge(M[i].silu, g * GROUP + j + 1)
                    dve.wait_ge(moe_free[i][(j + 2) % 4], g + 2 - (j < 2))
                    v_.tensor_tensor(hh[:, j % 2], sl[:, j % 2],
                                     PS[:, 2 + j % 2, 2 * BLK:4 * BLK].rearrange("p (f c) -> p f c", f=2),
                                     ALU.mult).then_inc(M[i].hidden, 1)
            for t in range(3):
                w = META if t == 2 else P
                dve.wait_ge(taken[i][t], 32)
                for c in range(2):
                    last = v_.scalar_tensor_tensor(h[0:w, t, :], ybuf[t][c][0:w, :], wgt[c][0:w, t:t + 1], h[0:w, t, :],
                                                   ALU.mult, ALU.add)
                    if c == 0 or t < 2:
                        settle()
            last.then_inc(S.h_upd, 1)

        def second_pe(pe, turn, loaded, dense):
            mm = nc.tensor.matmul
            turn(10, 3)
            for x in range(KD):
                slot, j, b = x // 2, x % 2, x % 2
                w = ring[:, slot, :].rearrange("p (s k f) -> p s k f", s=3, k=KD)
                if j == 0:
                    loaded(16, slot)
                if x >= 2:
                    pe.wait_ge(S.conv_ready, x - 1)
                for s in range(3):
                    for k in range(KD):
                        last = mm(PS[:, 3 * b + s, 0:T2], lhsT=w[:, s, k, j * P:(j + 1) * P], rhs=xT[:, k, :],
                                  start=k == 0, stop=k == KD - 1)
                last.then_inc(S.conv_products, 1)
                if j == 1:
                    pe.drain().then_inc(unit_free[slot], 1)
            pe.wait_ge(S.conv_ready, KD)
            for i in range(2):
                loaded(17, i)
                for t in range(3):
                    last = dense_rows(convT, slot_w(i, KD, 512), 2 * t + i, t, 512, KD)
            last.then_inc(S.mixed_done, 1)
            moe_pe(pe, 0, turn, 11)
            mla_pe(pe, turn)
            moe_pe(pe, 1, turn, 14)

        def dense_rows(src, w, bank, t, width, kk, at=0):
            rows_ = META if t == 2 else P
            for k in range(kk):
                last = nc.tensor.matmul(PS[0:rows_, bank, at:at + width], lhsT=src[:, k, xcol(t)], rhs=w[:, k, 0:width],
                                        start=k == 0, stop=k == kk - 1)
            return last

        def moe_pe(pe, i, turn, q):
            mm = nc.tensor.matmul
            for f in moe_free[i]:
                pe.drain().then_inc(f, 1)
            turn(q, 3)
            pe.wait_ge(M[i].router_loaded, 32)
            for t in range(3):
                last = dense_rows(xT, wr, 5, t, NG + NE, KD, at=t * (NG + NE))
            last.then_inc(M[i].logits, 1)
            pe.wait_ge(M[i].vec_step, 3)
            for t in range(3):
                for s in range(t + 1):
                    mm(PS[:, 6, t * NE:(t + 1) * NE], lhsT=cst("before") if s == t else cst("ones"), rhs=msel[:, s, :],
                       start=s == 0, stop=s == t)
            for s in range(3):
                last = mm(PS[:, 6, 192:256], lhsT=cst("ones"), rhs=msel[:, s, :], start=s == 0, stop=s == 2)
            last.then_inc(M[i].counted, 1)
            pe.wait_ge(M[i].vec_step, 4)
            n = 0
            for a, b in ((a1, b1), (a2, b2)):
                for t in range(3):
                    mm(PS[:, 7, 0:GC], lhsT=a[:, t, :], rhs=b[:, t, :], start=n == 0, stop=n == 5)
                    n += 1
            mm(PS[:, 7, 32:128], lhsT=cst("ones")[0:NE, :], rhs=cmpe[0:NE, :], start=True, stop=True).then_inc(M[i].tables, 1)
            pe.wait_ge(M[i].routed, 1)
            groups = pe.value_load(ng[0:1, 0:1], min_val=1, max_val=MAX_GROUPS)
            with pe.Fori(0, groups) as g:
                pe.wait_ge(M[i].gathered, g * 16 + 16)
                for k in range(KD):
                    last = nc.tensor.transpose(PS[:, k // 4, (k % 4) * P:(k % 4 + 1) * P], xg[:, k * P:(k + 1) * P], ident)
                last.then_inc(M[i].xg_turned, 1)
                pe.wait_ge(M[i].xgT_ready, g + 1)

                def gate_up(j):
                    pe.wait_ge(moe_loaded[i][j], g * 48 + 48)
                    w = ring[:, j, 0:4096].rearrange("p (s k f) -> p s k f", s=2, k=KD)
                    for s in range(2):
                        for f in range(2):
                            for k in range(KD):
                                last = mm(PS[:, 2 + j % 2, (2 * s + f) * BLK:(2 * s + f + 1) * BLK],
                                          lhsT=w[:, s, k, f * P:(f + 1) * P], rhs=xgT[:, k, j * BLK:(j + 1) * BLK],
                                          start=k == 0, stop=k == KD - 1)
                    last.then_inc(M[i].gateup, 1)

                def down(j):
                    if j == 0:
                        pe.wait_ge(M[i].y_copied, g + 1)
                    pe.wait_ge(M[i].hidden, g * GROUP + j + 3)
                    w = ring[:, j, 4096:6144].rearrange("p (f n) -> p f n", f=2)
                    for n in range(2):
                        for f in range(2):
                            last = mm(PS[BLK * j:BLK * (j + 1), 4 + n, :], lhsT=hh[:, j % 2, f, :],
                                      rhs=w[:, f, n * 512:(n + 1) * 512], start=f == 0, stop=f == 1)
                    last.then_inc(moe_free[i][j], 1)

                gate_up(0)
                gate_up(1)
                down(0)
                gate_up(2)
                down(1)
                gate_up(3)
                down(2)
                down(3)

        @block.sync
        def _(sp):
            sp.dma_start(const[:, :], A["const_table"]).then_inc(S.const_loaded, 16)
            sp.dma_start(h[:, 0:2, :], x_in).then_inc(S.h_loaded, 16)

            def load(use, slot, parts):
                assert len(parts) == 3
                sp.wait_ge(unit_free[slot], use + 1)
                for dst, src in parts:
                    sp.dma_start(dst, src).then_inc(unit_loaded[slot], 16)

            def kparts(slot, w, c0, n, splits=(0, 3, 6, 8)):
                dst = slot_w(slot, KD, n)
                src = w.rearrange("o (k p) f -> p (o k) f", p=P)
                return [(dst[:, a:b, :], src[:, a:b, c0:c0 + n]) for a, b in zip(splits, splits[1:])]

            def ff_parts(slot, gu, down, u):
                g = gu.rearrange("o (k p) f -> p (o k) f", p=P)
                v = ring[:, slot, 0:4096].rearrange("p (s k f) -> p s k f", s=2, k=KD)
                dn = ring[:, slot, 4096:6144].rearrange("p (j n) -> p j n", j=2)
                return [(v[:, 0], g[:, :, bass.ds(u * 256, 256)]),
                        (v[:, 1], g[:, :, bass.ds(u * 256 + D_FF, 256)]),
                        (dn, down[:, bass.ds(u * 256, 256), :].rearrange("o (j p) n -> p (o j) n", p=P))]

            def ffn(l, u0, gu, down):
                gu, down = A[gu][bass.ds(l, 1)], A[down][bass.ds(l, 1)]
                with sp.Fori(0, FF_UNITS // SLOTS) as it:
                    for j in range(SLOTS):
                        load(USES * l + it + (u0 + j) // SLOTS, (u0 + j) % SLOTS,
                             ff_parts((u0 + j) % SLOTS, gu, down, SLOTS * it + j))
                for u in range(SLOTS * (FF_UNITS // SLOTS), FF_UNITS):
                    load(USES * l + (u0 + u) // SLOTS, (u0 + u) % SLOTS,
                         ff_parts((u0 + u) % SLOTS, gu, down, u))

            with sp.Fori(0, DEPTH) as l:
                ffn(l, U_FFN1, "ffn1_gate_up", "ffn1_down")
                for i, (c0, n) in enumerate(IN_COLS):
                    u = U_IN + i
                    load(USES * l + u // SLOTS, u % SLOTS,
                         kparts(u % SLOTS, A["w_in"][bass.ds(l, 1)], c0, n))
                for i in range(2):
                    u = U_OUT + i
                    load(USES * l + u // SLOTS, u % SLOTS,
                         kparts(u % SLOTS, A["w_out"][bass.ds(l, 1)], 512 * i, 512))
                ffn(l, U_FFN2, "ffn2_gate_up", "ffn2_down")
                for i in range(2):
                    u = U_PLE + i
                    load(USES * l + u // SLOTS, u % SLOTS,
                         kparts(u % SLOTS, A["ple_gate"][bass.ds(l, 1)], 512 * i, 512))
                u = U_PLE + 2
                s = u % SLOTS
                proj = A["ple_proj"][bass.ds(l, 1)].rearrange("o (k p) n -> p (o k) n", p=P)
                load(USES * l + u // SLOTS, s, [
                    (ring[:, s, 0:D], proj[:, 0, :]), (ring[:, s, D:2 * D], proj[:, 1, :]),
                    (ring[:, s, 2 * D:2 * D + 512].rearrange("p (t d) -> p t d", t=2),
                     A["p"][bass.ds(l, 1), 0].rearrange("o (t p) d -> p (o t) d", p=P))])
            second_weights(sp, load)
            sp.wait_ge(S.out_ready, 1)
            sp.dma_start(out.rearrange("o (t p) d -> p (o t) d", p=P), xn[:, 0:2, :]).then_inc(S.out_stored, 16)
            sp.wait_ge(S.out_stored, 16)

        @block.gpsimd
        def _(pool):
            nc_ = nc.gpsimd
            with nc.allow_non_contiguous_dma(reason="a few hundred words, once"):
                nc_.dma_start(posi, A["positions"].rearrange("o (t p) -> p (o t)", p=P)).then_inc(S.small_loaded, 16)
            nc_.dma_start(gT1[:, :], A["norm_gains"].rearrange("l n (k c) -> (l n k) c", c=P)).then_inc(S.small_loaded, 16)
            for name in ROWS2:
                r0, ap = row_at[name], A[name]
                n = int(np.prod(ap.shape)) // P
                dims = " ".join(f"d{i}" for i in range(len(ap.shape) - 1))
                src = ap.rearrange(f"{dims} (k c) -> ({dims} k) c", c=P) if dims else ap.rearrange("(k c) -> k c", c=P)
                nc_.dma_start(gT2[r0:r0 + n, :], src).then_inc(S.small_loaded, 16)
            nc_.dma_start(h[0:META, 2, :], A["meta_tokens_2"]).then_inc(S.meta_loaded, 16)

            def rstd(r, n):
                pool.wait_ge(S.ms_ready, r + 1)
                nc_.tensor_tensor(rs[:, 0:n], ms[:, 0:n], cst("minus_half")[:, 0:n], ALU.pow).then_inc(S.rstd_ready, 1)

            blank = arena[:, 9776:9776 + D]
            nc_.memset(blank, 0.0).then_inc(S.blank_ready, 1)
            pool.wait_ge(S.blank_ready, 1)
            for g in range(NE // GROUP, MAX_GROUPS):
                nc_.dma_start(y_table[g * P:(g + 1) * P, :], blank).then_inc(S.y_cleared, 16)
            pool.wait_ge(S.y_cleared, 16 * (MAX_GROUPS - NE // GROUP))
            pool.wait_ge(S.const_loaded, 16)
            with pool.Fori(0, DEPTH) as l:
                pool.wait_ge(S.h_upd, 4 * l + 1)
                pool.sem_inc(S.pad, 1)
                for i in range(4):
                    nc_.dma_start(rows[:, i, :], A["norm_gains"][bass.ds(l, 1), 2 * i + 1, :].to_broadcast([P, D])).then_inc(S.rows_loaded, 16)
                nc_.dma_start(sgw[:, :, :], A["sg_spatial_w"][bass.ds(l, 1)].rearrange("o g t s -> t (o g) s")).then_inc(S.rows_loaded, 16)
                with nc.allow_non_contiguous_dma(reason="512 words"):
                    nc_.dma_start(sgb[:, :], A["sg_spatial_b"][bass.ds(l, 1)].rearrange("o g t -> t (o g)")).then_inc(S.rows_loaded, 16)
                nc_.dma_start(lng[:, :], A["sg_ln_gain"][bass.ds(l, 1), :].to_broadcast([P, 256])).then_inc(S.rows_loaded, 16)
                nc_.dma_start(hgn[:, :], A["hgrn_norm_gain"][bass.ds(l, 1), :].to_broadcast([P, HD])).then_inc(S.rows_loaded, 16)
                nc_.dma_start(sinks[:, :], A["attn_sinks"][bass.ds(l, 1), :].to_broadcast([P, 8])).then_inc(S.rows_loaded, 16)
                for i, n in enumerate([2, 2, 2, 8, 2, 2, 2, 2, 2, 2]):
                    rstd(10 * l + i, n)
            second_pool(pool, rstd)

        @block.scalar
        def _(act):
            a_ = nc.scalar

            def squares(r, tiles, src, parts=P):
                for t in range(tiles):
                    pr = META if t == 2 else P
                    d = xn[0:pr, t, :]
                    s = src(t)
                    if len(s.shape) == 3:
                        d = tile2(d)
                    last = a_.activation(d, s, ACT.Square, accum_out=ss[0:pr, t:t + 1])
                last.then_inc(S.square_done, 1)

            def norm(n, tiles=2):
                act.wait_ge(S.h_upd, n + 1)
                squares(0, tiles, lambda t: h[0:(META if t == 2 else P), t, :])

            def ffn(m):
                def one(f, b, first=False):
                    act.wait_ge(S.gateup_done, FT * m + f + 1)
                    if not first:
                        act.wait_ge(S.hidden_ready, FT * m + f - 1)
                    a_.activation(silu[:, b % 2, :], PS[:, 4 + b % 4, 0:256], ACT.Silu).then_inc(S.silu_ready, 1)
                one(0, 0, True)
                one(1, 1, True)
                with act.Fori(0, (FT - 2) // 4) as it:
                    for k in range(4):
                        one(4 * it + 2 + k, 2 + k)
                act.wait_ge(S.down_done, FT * (m + 1))
                squares(0, 2, yps)

            def mixer(l):
                act.wait_ge(S.qf_done, 2 * l + 1)
                a_.activation(qT, PS[:, 0, :].rearrange("p (c n) -> p c n", c=2), ACT.Copy)
                act.wait_ge(S.qf_done, 2 * l + 2)
                a_.activation(fs, PS[:, 1, :].rearrange("p (c n) -> p c n", c=2), ACT.Copy).then_inc(S.qf_copied, 1)
                for t in range(2):
                    act.wait_ge(S.z_done, 8 * l + 1 + t)
                    a_.activation(z[:, t, 0:256], PS[:, 2 + t, 0:256], ACT.Copy)
                    last = a_.activation(z[:, t, 256:512], PS[:, 2 + t, 256:512], ACT.Sigmoid)
                last.then_inc(S.hihg_copied, 1)
                for t in range(2):
                    act.wait_ge(S.z_done, 8 * l + 7 + t)
                    last = a_.activation(z[:, t, 1280:1792], PS[:, 2 + t, :], ACT.Gelu_apprx_tanh)
                last.then_inc(S.susv_copied, 1)
                act.preload_act_table_set("natural_log_exp_and_others")
                NV = 20
                act.wait_ge(S.hgrn_vec, NV * l + 1)
                a_.activation(w2, w1, ACT.Exp)
                act.drain()
                a_.activation(w3, w2, ACT.Ln, bias=1.0).then_inc(S.hgrn_act, 1)
                act.wait_ge(S.hgrn_vec, NV * l + 2)
                for c in range(2):
                    a_.activation(kT[:, c, :], w2[:, c, :], ACT.Exp, bias=lbl[:, 1, c:c + 1])
                a_.activation(w3, w5, ACT.Exp)
                act.drain()
                a_.activation(w4, w3, ACT.Ln, bias=1.0).then_inc(S.hgrn_act, 1)
                for i, s in enumerate([P] + LEVELS[:-1]):
                    act.wait_ge(S.hgrn_vec, NV * l + 3 + 2 * i)
                    dv = dif[:, i % 2].rearrange("p c (n e s) -> p (c n) e s", e=2, s=s)
                    ev = ex[:, i % 2].rearrange("p c (n e s) -> p (c n) e s", e=2, s=s)
                    a_.activation(ev[:, :, 0, :], dv[:, :, 0, :], ACT.Exp, scale=-1.0)
                    a_.activation(ev[:, :, 1, :], dv[:, :, 1, :], ACT.Exp).then_inc(S.hgrn_act, 1)
                act.wait_ge(S.hgrn_pe, 10 * l + 10)
                a_.activation(w4, PS[:, 4, :].rearrange("p (c n) -> p c n", c=2), ACT.Square).then_inc(S.square_done, 1)
                act.wait_ge(S.qk_turned, l + 1)
                for b in range(3):
                    n = 512 if b < 2 else 256
                    last = a_.activation(qkT[:, 2 * b:2 * b + n // 256, :],
                                         PS[:, 5 + b, 0:n].rearrange("p (c n) -> p c n", n=256), ACT.Copy)
                last.then_inc(S.qkT_ready, 1)
                for n in range(2):
                    nk = P * (n + 1)
                    act.wait_ge(S.scores_ready, 2 * l + n + 1)
                    for hd in range(8):
                        a_.activation(ssb[:, hd, 0:nk], ssb[:, hd, 0:nk], ACT.Exp, bias=sneg[:, hd:hd + 1],
                                      accum_out=ssum[:, hd:hd + 1])
                    a_.activation(sden, ssink, ACT.Exp).then_inc(S.probs_ready, 1)
                    act.wait_ge(S.probs_turned, 2 * l + n + 1)
                    for b in range(2):
                        src = (PS[:, 2 + b, :] if n == 0 else PS[:, 2 * b:2 * b + 2, :].rearrange("p a b -> p (a b)"))
                        dst = (pT_[:, 4 * b:4 * b + 4, 0:n + 1, :])
                        last = a_.activation(dst, src.rearrange("p (a c q) -> p a c q", a=4, q=P), ACT.Copy)
                    last.then_inc(S.probsT_ready, 1)
                act.wait_ge(S.centred, l + 1)
                for t in range(2):
                    last = a_.activation(sgm_mix[:, t, :], lnw[:, t, :], ACT.Square, accum_out=ss[:, t:t + 1])
                last.then_inc(S.square_done, 1)
                act.wait_ge(S.wout_done, l + 1)
                squares(0, 2, yps)

            def ple(l):
                act.wait_ge(S.gate_done, l + 1)
                for t in range(2):
                    last = a_.activation(tile2(sgm[:, t, :]), yps(t), ACT.Sigmoid)
                last.then_inc(S.gate_ready, 1)
                act.wait_ge(S.ple_ready, l + 1)
                squares(0, 2, lambda t: sgm[:, t, :])

            act.wait_ge(S.lb_vec, 1)
            a_.activation(lbt[:, 4:8], lbt[:, 0:4], ACT.Exp).then_inc(S.lb_act, 1)
            act.wait_ge(S.lb_vec, 2)
            a_.activation(lbt[:, 10:12], lbt[:, 8:10], ACT.Ln).then_inc(S.lb_act, 1)
            act.wait_ge(S.rope_vec, 1)
            a_.activation(rope_cos, rope_cos, ACT.Sin)
            a_.activation(rope_sin, rope_sin, ACT.Sin).then_inc(S.rope_ready, 1)

            with act.Fori(0, DEPTH) as l:
                norm(4 * l)
                ffn(2 * l)
                norm(4 * l + 1)
                mixer(l)
                norm(4 * l + 2)
                ffn(2 * l + 1)
                norm(4 * l + 3)
                ple(l)
            second_act(act, norm, squares)

        @block.vector
        def _(dve):
            v_ = nc.vector
            settle = dve.drain

            def rstd(r, n, width, sums=None):
                dve.wait_ge(S.square_done, r + 1)
                if sums is not None:
                    v_.tensor_reduce(ss[:, 0:n], sums, AX.X, ALU.add)
                    settle()
                v_.tensor_scalar(ms[:, 0:n], ss[:, 0:n], 1.0 / width, EPS, ALU.mult, ALU.add).then_inc(S.ms_ready, 1)
                dve.wait_ge(S.rstd_ready, r + 1)

            def turned(q, tiles, gains):
                for n_, (dst, g) in enumerate(gains):
                    for t in range(tiles):
                        w = META if t == 2 else P
                        src = (PS[:, 2 * t:2 * t + 2, :].rearrange("p a (k w) -> p (a k) w", w=w) if t < 2
                               else PS[:, 4, 0:KD * w].rearrange("p (k w) -> p k w", w=w))
                        if n_ == 0 and t == 0:
                            dve.wait_ge(S.xn_turned, q + 1)
                        if g is None:
                            last = v_.tensor_copy(dst[:, :, xcol(t)], src)
                        else:
                            last = v_.tensor_tensor(dst[:, :, xcol(t)], src,
                                                    g.unsqueeze(2).to_broadcast([P, KD, w]), ALU.mult)
                last.then_inc(S.xT_ready, 1)

            def norm(r, q, gains, tiles=2):
                rstd(r, tiles, D)
                for t in range(tiles):
                    pr = META if t == 2 else P
                    last = v_.tensor_scalar(xn[0:pr, t, :], h[0:pr, t, :], rs[0:pr, t:t + 1], None, ALU.mult)
                last.then_inc(S.xn_ready, 1)
                turned(q, tiles, gains)

            def postnorm(l, r, i, factor, src):
                rstd(r, 2, D)
                if i == 0:
                    dve.wait_ge(S.rows_loaded, 16 * 9 * l + 16 * 9)
                for t in range(2):
                    v_.scalar_tensor_tensor(tile2(xn[:, t, :]), src(t), rs[:, t:t + 1], tile2(rows[:, i, :]),
                                            ALU.mult, ALU.mult)
                settle()
                for t in range(2):
                    last = v_.scalar_tensor_tensor(h[:, t, :], xn[:, t, :], factor, h[:, t, :], ALU.mult, ALU.add)
                last.then_inc(S.h_upd, 1)

            def ffn(m):
                def one(f, b, first=False):
                    dve.wait_ge(S.silu_ready, FT * m + f + 1)
                    if not first:
                        dve.wait_ge(S.down_done, FT * m + f - 1)
                    v_.tensor_tensor(hid[:, b % 2, :], silu[:, b % 2, :], PS[:, 4 + b % 4, 256:512],
                                     ALU.mult).then_inc(S.hidden_ready, 1)
                one(0, 0, True)
                one(1, 1, True)
                with dve.Fori(0, (FT - 2) // 4) as it:
                    for k in range(4):
                        one(4 * it + 2 + k, 2 + k)

            def mixer(l):
                for i, (a, b, bank) in enumerate([(512, 1024, 4), (1024, 1280, 6)]):
                    for t in range(2):
                        dve.wait_ge(S.z_done, 8 * l + 3 + 2 * i + t)
                        last = v_.tensor_copy(z[:, t, a:b], PS[:, bank + t, 0:b - a])
                last.then_inc(S.qkv_copied, 1)
                dve.wait_ge(S.qf_copied, l + 1)
                v_.scalar_tensor_tensor(w1, fs, -1.0, fs, ALU.mult, ALU.min).then_inc(S.hgrn_vec, 1)
                v_.memset(att, 0.0)
                NA = 10
                dve.wait_ge(S.hgrn_act, NA * l + 1)
                v_.scalar_tensor_tensor(w1, fs, 0.0, w3, ALU.min, ALU.subtract)
                settle()
                v_.tensor_tensor(w2, w1, fs, ALU.subtract)
                for c in range(2):
                    v_.tensor_scalar(w4[:, c, :], w1[:, c, :], lbl[:, 2, c:c + 1], None, ALU.add)
                    v_.tensor_scalar(w6[:, c, :], w1[:, c, :], lbl[:, 1, c:c + 1], None, ALU.add)
                settle()
                v_.scalar_tensor_tensor(w5, w4, -1.0, w4, ALU.mult, ALU.min).then_inc(S.hgrn_vec, 1)
                dve.wait_ge(S.hgrn_act, NA * l + 2)
                for c in range(2):
                    v_.scalar_tensor_tensor(w5[:, c, :], w6[:, c, :], lbl[:, 0, c:c + 1], w4[:, c, :],
                                            ALU.max, ALU.add)
                settle()
                for c in range(2):
                    v_.tensor_tensor_scan(w1[:, c, :], cst("ones")[:, 0:1].to_broadcast([P, 256]), w5[:, c, :], 0.0,
                                          ALU.mult, ALU.add)
                settle()

                sizes = [P] + LEVELS[:-1]

                def distance(i):
                    s = sizes[i]
                    b = w1.rearrange("p c (n s) -> p (c n) s", s=2 * s)
                    n = b.shape[1]
                    v_.tensor_tensor(dif[:, i % 2].rearrange("p c (n s) -> p (c n) s", s=2 * s), b,
                                     b[:, :, s - 1:s].to_broadcast([P, n, 2 * s]), ALU.subtract).then_inc(S.hgrn_vec, 1)

                def decayed(i):
                    s = sizes[i]
                    split = lambda v: v.rearrange("p c (n e s) -> p (c n) e s", e=2, s=s)
                    dve.wait_ge(S.hgrn_act, NA * l + 3 + i)
                    v_.tensor_tensor(split(lev[:, i % 2])[:, :, 0, :], split(kT)[:, :, 0, :],
                                     split(ex[:, i % 2])[:, :, 0, :], ALU.mult)
                    v_.tensor_tensor(split(lev[:, i % 2])[:, :, 1, :], split(qT)[:, :, 1, :],
                                     split(ex[:, i % 2])[:, :, 1, :], ALU.mult).then_inc(S.hgrn_vec, 1)

                def gathered(i):
                    settle()
                    dve.wait_ge(S.hgrn_pe, 10 * l + 1 + i)
                    b = 2 * (i % 2)
                    if i == 0:
                        v_.tensor_copy(att10, PS[:, b:b + 2, 0:256].rearrange("p a (c n) -> p a c n", c=2))
                    else:
                        dve.sem_inc(S.pad, 1)
                        m = cst("levels")[:, (i - 1) * P:i * P].bitcast(I32)
                        v_.copy_predicated(att.rearrange("p a b c q -> p (a b c) q"), m.unsqueeze(1).to_broadcast([P, 8, P]),
                                           PS[:, b:b + 2, :].rearrange("p a (c q) -> p (a c) q", q=P))

                distance(0)
                for i in range(8):
                    if i < 7:
                        distance(i + 1)
                    decayed(i)
                    if i:
                        gathered(i - 1)
                gathered(7)
                dve.drain().then_inc(S.hgrn_vec, 1)
                gathered(8)
                dve.drain().then_inc(S.hgrn_vec, 1)
                dve.wait_ge(S.square_done, 10 * l + 4)
                rstd(10 * l + 3, 8, HD, sums=w4.rearrange("p c (h e) -> p (c h) e", e=HD))
                o = PS[:, 4, :].rearrange("p (n e) -> p n e", e=HD)
                wv = w2.rearrange("p c (h e) -> p (c h) e", e=HD)
                v_.tensor_tensor(wv, o, rs[:, 0:8].unsqueeze(2).to_broadcast([P, 8, HD]), ALU.mult)
                settle()
                v_.tensor_tensor(wv, wv, hgn[:, :].unsqueeze(1).to_broadcast([P, 8, HD]), ALU.mult)
                settle()
                dve.wait_ge(S.hihg_copied, l + 1)
                v_.tensor_tensor(xn[:, 0:2, 0:256], w2, z[:, :, 256:512], ALU.mult)

                x12 = z[:, :, 512:1152].rearrange("p t (h e d) -> p t h e d", e=2, d=32)
                cs = rope_cos[:, :, :].unsqueeze(2).to_broadcast([P, 2, 10, 32])
                sn = rope_sin[:, :, :].unsqueeze(2).to_broadcast([P, 2, 10, 32])
                settle()
                pr = [rprod[:, i, :].rearrange("p (t h d) -> p t h d", t=2, h=10) for i in range(4)]
                dve.wait_ge(S.rope_ready, 1)
                for i, (e, c) in enumerate([(0, cs), (1, sn), (1, cs), (0, sn)]):
                    v_.tensor_tensor(pr[i], x12[:, :, :, e, :], c, ALU.mult)
                settle()
                for e, (a, b, op) in enumerate([(pr[0], pr[1], ALU.subtract), (pr[2], pr[3], ALU.add)]):
                    for t in range(2):
                        ro = rot[:, t, 0:512].rearrange("p (j g e d) -> p g j e d", g=2, e=2, d=32)
                        v_.tensor_tensor(ro[:, :, :, e, :], a[:, t, 0:8, :].rearrange("p (g j) d -> p g j d", g=2),
                                         b[:, t, 0:8, :].rearrange("p (g j) d -> p g j d", g=2), op)
                    ro = rot[:, :, 512:640].rearrange("p t (h e d) -> p t h e d", e=2, d=32)
                    last = v_.tensor_tensor(ro[:, :, :, e, :], a[:, :, 8:10, :], b[:, :, 8:10, :], op)
                last.then_inc(S.roped, 1)
                settle()
                for n in range(2):
                    nk = P * (n + 1)
                    dve.wait_ge(S.scores_done, 2 * l + n + 1)
                    src = (PS[:, 0:2, :] if n == 0 else PS[:, 4:8, :]).rearrange("p a (h k) -> p (a h) k", k=nk)
                    bias = cst("window")[:, P:2 * P] if n == 0 else cst("window")
                    v_.scalar_tensor_tensor(ssb[:, :, 0:nk], src, HD ** -0.5,
                                            bias.unsqueeze(1).to_broadcast([P, 8, nk]), ALU.mult, ALU.add)
                    settle()
                    v_.tensor_reduce(smax, ssb[:, :, 0:nk], AX.X, ALU.max)
                    settle()
                    v_.tensor_tensor(smax, smax, sinks[:, :], ALU.max)
                    settle()
                    v_.tensor_scalar(sneg, smax, -1.0, None, ALU.mult)
                    v_.tensor_tensor(ssink, sinks[:, :], smax, ALU.subtract).then_inc(S.scores_ready, 1)
                    if n == 0:
                        dve.wait_ge(S.sgw_turned, l + 1)
                        v_.tensor_tensor(sgwT, PS[:, 5, :].rearrange("p (g t) -> p g t", g=4),
                                         cst("upto").unsqueeze(1).to_broadcast([P, 4, P]), ALU.mult)
                        dve.drain().then_inc(S.sgw_ready, 1)
                    dve.wait_ge(S.attn_done, 2 * l + n + 1)
                    v_.tensor_tensor(srden, ssum, sden, ALU.add)
                    settle()
                    v_.reciprocal(srden, srden)
                    settle()
                    ob = PS[:, 0 if n == 0 else 4, :].rearrange("p (h e) -> p h e", e=HD)
                    v_.tensor_tensor(xn[:, n, 256:768].rearrange("p (h e) -> p h e", e=HD), ob,
                                     srden.unsqueeze(2).to_broadcast([P, 8, HD]), ALU.mult)
                dve.wait_ge(S.susv_copied, l + 1)
                v_.tensor_reduce(mean, z[:, :, 1536:1792], AX.X, ALU.add)
                settle()
                v_.tensor_scalar(mean, mean, -1.0 / 256, None, ALU.mult)
                settle()
                for t in range(2):
                    last = v_.tensor_scalar(lnw[:, t, :], z[:, t, 1536:1792], mean[:, t:t + 1], None, ALU.add)
                last.then_inc(S.centred, 1)
                rstd(10 * l + 4, 2, 256)
                for t in range(2):
                    last = v_.scalar_tensor_tensor(lnw[:, t, :], lnw[:, t, :], rs[:, t:t + 1], lng[:, :], ALU.mult, ALU.mult)
                last.then_inc(S.sv_ready, 1)
                dve.wait_ge(S.spatial_done, l + 1)
                v_.tensor_tensor(sgm_mix.rearrange("p t (g e) -> p t g e", e=HD),
                                 PS[:, 6, :].rearrange("p (t g e) -> p t g e", t=2, e=HD),
                                 sgb[:, :].unsqueeze(1).unsqueeze(3).to_broadcast([P, 2, 4, HD]), ALU.add)
                settle()
                v_.tensor_tensor(xn[:, 0:2, 768:1024], sgm_mix, z[:, :, 1280:1536], ALU.mult).then_inc(S.xn_ready, 1)
                turned(5 * l + 2, 2, [(xT, None)])

            def ple(l):
                dve.wait_ge(S.p_turned, l + 1)
                v_.tensor_copy(pleT, PS[:, 4, :].rearrange("p (k t) -> p k t", k=2)).then_inc(S.pT_ready, 1)
                dve.wait_ge(S.gate_ready, l + 1)
                dve.wait_ge(S.proj_done, l + 1)
                for t in range(2):
                    last = v_.tensor_tensor(tile2(sgm[:, t, :]), tile2(sgm[:, t, :]), PS[:, 4 + 2 * t:6 + 2 * t, :], ALU.mult)
                last.then_inc(S.ple_ready, 1)

            dve.wait_ge(S.rowsT_done, 1)
            v_.tensor_copy(gT1[:, :], PS[:, 0, 0:P])
            v_.tensor_copy(gT2[:, 0:n_rows2], PS[:, 1, 0:n_rows2])
            settle()
            lg = gT2[:, row_at["hgrn_lb_logits"]:row_at["hgrn_lb_logits"] + 4]
            v_.tensor_tensor(lbt[:, 12:14], lg[:, 0:2], lg[:, 2:4], ALU.max)
            settle()
            v_.tensor_tensor(lbt[:, 0:2], lg[:, 0:2], lbt[:, 12:14], ALU.subtract)
            v_.tensor_tensor(lbt[:, 2:4], lg[:, 2:4], lbt[:, 12:14], ALU.subtract).then_inc(S.lb_vec, 1)
            dve.wait_ge(S.lb_act, 1)
            v_.tensor_tensor(lbt[:, 8:10], lbt[:, 4:6], lbt[:, 6:8], ALU.add).then_inc(S.lb_vec, 1)
            dve.wait_ge(S.lb_act, 2)
            v_.memset(lb[:, 0, 0, :], LN_FLOOR)
            v_.memset(lb[:, 0, 1, :], 0.0)
            v_.memset(lb[:, 0, 2, :], -LN_FLOOR)
            v_.tensor_tensor(lb[:, 1, 0, :], lbt[:, 2:4], lbt[:, 10:12], ALU.subtract)
            v_.tensor_tensor(lb[:, 1, 1, :], lbt[:, 0:2], lbt[:, 10:12], ALU.subtract)
            settle()
            v_.tensor_scalar(lb[:, 1, 0, :], lb[:, 1, 0, :], LN_FLOOR, None, ALU.max)
            settle()
            v_.tensor_tensor(lb[:, 1, 2, :], lb[:, 1, 1, :], lb[:, 1, 0, :], ALU.subtract)
            v_.tensor_copy(posf, posi)
            settle()
            ang = arena[:, 0:64].rearrange("p (t d) -> p t d", t=2)
            k1 = arena[:, 64:128].rearrange("p (t d) -> p t d", t=2)
            k2 = arena[:, 128:192].rearrange("p (t d) -> p t d", t=2)
            for t in range(2):
                v_.tensor_scalar(ang[:, t, :], cst("inv_freq"), posf[:, t:t + 1], None, ALU.mult)
            settle()
            for k, quarter in ((k1, 0.0), (k2, 0.25)):
                v_.tensor_scalar(k, ang, 1.0 / TWO_PI, quarter, ALU.mult, ALU.add)
                settle()
                v_.tensor_scalar(k, k, ROUND, None, ALU.add)
                settle()
                v_.tensor_scalar(k, k, -ROUND, None, ALU.add)
                settle()
            for k, dst, quarter in ((k1, rope_sin, 0.0), (k2, rope_cos, np.pi / 2)):
                v_.scalar_tensor_tensor(dst[:, :, :], k, -C1, ang, ALU.mult, ALU.add)
                settle()
                v_.scalar_tensor_tensor(dst[:, :, :], k, -C2, dst[:, :, :], ALU.mult, ALU.add)
                settle()
                v_.scalar_tensor_tensor(dst[:, :, :], k, -C3, dst[:, :, :], ALU.mult, ALU.add)
                settle()
                v_.tensor_scalar(dst[:, :, :], dst[:, :, :], float(quarter), 3.1415925, ALU.add, ALU.min)
                settle()
                last = v_.tensor_scalar(dst[:, :, :], dst[:, :, :], -3.1415925, None, ALU.max)
            last.then_inc(S.rope_vec, 1)
            dve.wait_ge(S.h_loaded, 16)
            dve.wait_ge(S.meta_loaded, 16)
            dve.drain().then_inc(S.h_upd, 1)

            with dve.Fori(0, DEPTH) as l:
                v_.tensor_copy(gl[:, :], gT1[:, bass.ds(l * 64, 64)])
                v_.tensor_copy(lbl, lb.rearrange("p l v c -> p l (v c)")[:, bass.ds(l, 1), :].rearrange("p o (v c) -> p (o v) c", v=3))
                settle()
                norm(10 * l, 5 * l, [(xT, gl[:, 0:8])])
                ffn(2 * l)
                postnorm(l, 10 * l + 1, 0, 0.5, yps)
                norm(10 * l + 2, 5 * l + 1, [(xT, gl[:, 16:24])])
                mixer(l)
                postnorm(l, 10 * l + 5, 1, 1.0, yps)
                norm(10 * l + 6, 5 * l + 3, [(xT, gl[:, 32:40])])
                ffn(2 * l + 1)
                postnorm(l, 10 * l + 7, 2, 0.5, yps)
                norm(10 * l + 8, 5 * l + 4, [(xT, gl[:, 48:56])])
                ple(l)
                postnorm(l, 10 * l + 9, 3, 1.0, lambda t: tile2(sgm[:, t, :]))
            second_vec(dve, rstd, turned, norm)

        @block.tensor
        def _(pe):
            mm = nc.tensor.matmul

            def turn(q, tiles=2):
                pe.wait_ge(S.xn_ready, q + 1)
                for t in range(tiles):
                    w = META if t == 2 else P
                    for k in range(KD):
                        o = (PS[:, 2 * t + k // 4, (k % 4) * P:(k % 4) * P + P] if t < 2
                             else PS[:, 4, k * w:(k + 1) * w])
                        last = nc.tensor.transpose(o, xn[0:w, t, k * P:(k + 1) * P], ident[0:w, 0:w])
                last.then_inc(S.xn_turned, 1)
                pe.wait_ge(S.xT_ready, q + 1)

            def loaded(use, slot):
                pe.wait_ge(unit_loaded[slot], 48 * use + 48)

            def ffn(l, m, u0):
                def gate_up(f, local):
                    unit = u0 + local // 2
                    slot = unit % SLOTS
                    w = ring[:, slot, 0:4096].rearrange("p (s k f) -> p s k f", s=2, k=KD)
                    j = local % 2
                    if j == 0:
                        loaded(USES * l + f[0] + unit // SLOTS, slot)
                    for s in range(2):
                        for k in range(KD):
                            last = mm(PS[:, 4 + local % 4, s * 256:(s + 1) * 256], lhsT=w[:, s, k, j * P:(j + 1) * P],
                                      rhs=xT[:, k, META:T2], start=k == 0, stop=k == KD - 1)
                            if s == k == 0 and j == 1 and local > 1:
                                last.then_inc(unit_free[(unit - 1) % SLOTS], 1)
                    last.then_inc(S.gateup_done, 1)

                def down(f, local, first=False, final=False):
                    slot = (u0 + local // 2) % SLOTS
                    j = local % 2
                    w = ring[:, slot, 4096:6144].rearrange("p (j n) -> p j n", j=2)
                    pe.wait_ge(S.hidden_ready, FT * m + 8 * f[0] + local + 1)
                    for t in range(2):
                        for n in range(2):
                            last = mm(PS[:, 2 * t + n, :], lhsT=hid[:, j, t * P:(t + 1) * P],
                                      rhs=w[:, j, n * 512:(n + 1) * 512], start=first, stop=final,
                                      skip_group_check=True)
                    last.then_inc(S.down_done, 1)
                    if final:
                        pe.drain().then_inc(unit_free[slot], 1)

                gate_up([0], 0)
                gate_up([0], 1)
                down([0], 0, first=True)
                with pe.Fori(0, 2) as it:
                    for k in range(8):
                        gate_up([it], 2 + k)
                        down([it], 1 + k)
                for local in range(17, FT):
                    if local + 1 < FT:
                        gate_up([0], local + 1)
                    down([0], local, final=local == FT - 1)

            def dense(slot, w, bank, t, width, src=xT, kk=KD, at=0):
                for k in range(kk):
                    last = mm(PS[:, bank, at:at + width], lhsT=src[:, k, xcol(t)], rhs=w[:, k, 0:width],
                              start=k == 0, stop=k == kk - 1)
                return last

            def mixer(l):
                slot, use = U_IN % SLOTS, USES * l + U_IN // SLOTS
                loaded(use, slot)
                w = slot_w(slot, KD, 512)
                for m in range(4):
                    for k in range(KD):
                        last = mm(PS[:, m // 2, (m % 2) * 256:(m % 2) * 256 + 256], lhsT=w[:, k, m * P:(m + 1) * P],
                                  rhs=xT[:, k, META:T2], start=k == 0, stop=k == KD - 1)
                    if m % 2:
                        last.then_inc(S.qf_done, 1)
                pe.drain().then_inc(unit_free[slot], 1)
                for i, bank in enumerate([2, 4, 6, 2]):
                    u = U_IN + 1 + i
                    width = IN_COLS[1 + i][1]
                    slot = u % SLOTS
                    loaded(USES * l + u // SLOTS, slot)
                    if i == 3:
                        pe.wait_ge(S.hihg_copied, l + 1)
                    for t in range(2):
                        last = dense(slot, slot_w(slot, KD, width), bank + t, t, width)
                        last.then_inc(S.z_done, 1)
                    pe.drain().then_inc(unit_free[slot], 1)
                for i in range(9):
                    b = 2 * (i % 2)
                    if i < 8:
                        pe.wait_ge(S.hgrn_vec, 20 * l + 4 + 2 * i + (1 if i < 7 else 0))
                    for hd in range(4):
                        par, c = hd % 2, hd // 2
                        rows_ = slice(64 * par, 64 * par + 64)
                        ks = lev[rows_, i % 2, c, :] if i < 8 else kT[rows_, c, :]
                        qs = lev[rows_, i % 2, c, :] if i < 8 else qT[rows_, c, :]
                        if i == 0:
                            last = mm(PS[:, b + par, c * P:(c + 1) * P], lhsT=ks[:, 0:P], rhs=qs[:, P:2 * P],
                                      start=True, stop=True)
                        else:
                            for t in range(2):
                                last = mm(PS[:, b + par, (2 * c + t) * P:(2 * c + t + 1) * P],
                                          lhsT=ks[:, t * P:(t + 1) * P], rhs=qs[:, t * P:(t + 1) * P],
                                          start=True, stop=True)
                    last.then_inc(S.hgrn_pe, 1)
                    if i == 7:
                        pe.wait_ge(S.hgrn_vec, 20 * l + 18 + 1)
                pe.wait_ge(S.hgrn_vec, 20 * l + 20)
                pe.wait_ge(S.hihg_copied, l + 1)
                for t in range(2):
                    for hd in range(4):
                        par, c = hd % 2, hd // 2
                        o = PS[:, 4, (4 * t + hd) * HD:(4 * t + hd + 1) * HD]
                        last = mm(o, lhsT=att[:, par, c, t, :], rhs=z[:, t, hd * HD:(hd + 1) * HD], start=True, stop=t == 0)
                        if t:
                            last = mm(o, lhsT=att10[:, par, c, :], rhs=z[:, 0, hd * HD:(hd + 1) * HD], start=False, stop=True)
                last.then_inc(S.hgrn_pe, 1)
                pe.wait_ge(S.roped, l + 1)
                for t in range(2):
                    for j in range(5):
                        src = rot[:, t, j * P:(j + 1) * P]
                        last = nc.tensor.transpose(PS[:, 5 + j // 2, (j % 2) * 256 + t * P:(j % 2) * 256 + (t + 1) * P],
                                                   src, ident)
                last.then_inc(S.qk_turned, 1)
                pe.wait_ge(S.qkT_ready, l + 1)
                for n in range(2):
                    nk = P * (n + 1)
                    for hd in range(8):
                        g, j = hd // 4, hd % 4
                        r = slice(64 * g, 64 * g + 64)
                        per = 512 // nk
                        last = mm(PS[:, (0 if n == 0 else 4) + hd // per, (hd % per) * nk:(hd % per + 1) * nk],
                                  lhsT=qkT[r, j, n * P:(n + 1) * P], rhs=qkT[r, 4, 0:nk], start=True, stop=True)
                    last.then_inc(S.scores_done, 1)
                    if n == 0:
                        for g in range(4):
                            last = nc.tensor.transpose(PS[:, 5, g * P:(g + 1) * P], sgw[:, g, :], ident)
                        last.then_inc(S.sgw_turned, 1)
                    pe.wait_ge(S.probs_ready, 2 * l + n + 1)
                    for hd in range(8):
                        for c in range(n + 1):
                            i = hd * (n + 1) + c
                            last = nc.tensor.transpose(PS[:, (2 if n == 0 else 0) + i // 4, (i % 4) * P:(i % 4 + 1) * P],
                                                       ssb[:, hd, c * P:(c + 1) * P], ident)
                    last.then_inc(S.probs_turned, 1)
                    pe.wait_ge(S.probsT_ready, 2 * l + n + 1)
                    if n == 0:
                        pe.wait_ge(S.qkv_copied, l + 1)
                        pe.wait_ge(S.sgw_ready, l + 1)
                    for hd in range(8):
                        for c in range(n + 1):
                            g = hd // 4
                            last = mm(PS[:, 0 if n == 0 else 4, hd * HD:(hd + 1) * HD], lhsT=pT_[:, hd, c, :],
                                      rhs=z[:, c, 1152 + g * HD:1152 + (g + 1) * HD], start=c == 0, stop=c == n)
                    last.then_inc(S.attn_done, 1)
                pe.wait_ge(S.sv_ready, l + 1)
                for t in range(2):
                    for g in range(4):
                        last = mm(PS[:, 6, (4 * t + g) * HD:(4 * t + g + 1) * HD], lhsT=sgwT[:, g, :],
                                  rhs=lnw[:, t, g * HD:(g + 1) * HD], start=True, stop=True)
                last.then_inc(S.spatial_done, 1)
                turn(5 * l + 2)
                for i in range(2):
                    u = U_OUT + i
                    slot = u % SLOTS
                    loaded(USES * l + u // SLOTS, slot)
                    for t in range(2):
                        last = dense(slot, slot_w(slot, KD, 512), 2 * t + i, t, 512)
                    last.then_inc(unit_free[slot], 1)
                pe.drain().then_inc(S.wout_done, 1)

            def ple(l):
                for i in range(2):
                    u = U_PLE + i
                    slot = u % SLOTS
                    loaded(USES * l + u // SLOTS, slot)
                    for t in range(2):
                        last = dense(slot, slot_w(slot, KD, 512), 2 * t + i, t, 512)
                    last.then_inc(unit_free[slot], 1)
                pe.drain().then_inc(S.gate_done, 1)
                u = U_PLE + 2
                slot = u % SLOTS
                loaded(USES * l + u // SLOTS, slot)
                pv = ring[:, slot, 2 * D:2 * D + 512].rearrange("p (t d) -> p t d", t=2)
                for t in range(2):
                    for k in range(2):
                        last = nc.tensor.transpose(PS[:, 4, k * 256 + t * P:k * 256 + (t + 1) * P], pv[:, t, k * P:(k + 1) * P], ident)
                last.then_inc(S.p_turned, 1)
                pe.wait_ge(S.pT_ready, l + 1)
                w = slot_w(slot, 2, D)
                for t in range(2):
                    for n in range(2):
                        for k in range(2):
                            last = mm(PS[:, 4 + 2 * t + n, :], lhsT=pleT[:, k, t * P:(t + 1) * P],
                                      rhs=w[:, k, n * 512:(n + 1) * 512], start=k == 0, stop=k == 1)
                last.then_inc(unit_free[slot], 1)
                pe.drain().then_inc(S.proj_done, 1)

            for f in unit_free:
                pe.sem_inc(f, 1)
            pe.wait_ge(S.const_loaded, 16)
            pe.wait_ge(S.small_loaded, 16 * (2 + len(ROWS2)))
            nc.tensor.transpose(PS[:, 0, 0:P], gT1[:, :], ident)
            nc.tensor.transpose(PS[:, 1, 0:n_rows2], gT2[0:n_rows2, :], ident[0:n_rows2, 0:n_rows2]).then_inc(S.rowsT_done, 1)
            with pe.Fori(0, DEPTH) as l:
                turn(5 * l)
                ffn(l, 2 * l, U_FFN1)
                turn(5 * l + 1)
                mixer(l)
                turn(5 * l + 3)
                ffn(l, 2 * l + 1, U_FFN2)
                turn(5 * l + 4)
                ple(l)
            second_pe(pe, turn, loaded, dense)




def kernel(**inputs):
    import concourse.bacc as bacc
    from concourse.bass_utils import run_bass_kernel_spmd

    nc = bacc.Bacc("TRN2", target_bir_lowering=False, num_devices=1)
    arrays = {k: np.ascontiguousarray(v) for k, v in inputs.items()}
    arrays["const_table"] = CONSTS
    arrays["const_table2"] = CONSTS2
    aps = {k: nc.dram_tensor(k, a.shape, mybir.dt.from_np(a.dtype), kind="ExternalInput").ap()
           for k, a in arrays.items()}
    out = nc.dram_tensor("out", (1, SEQ, D), F32, kind="ExternalOutput").ap()
    x_table = nc.dram_tensor("x_table", (T2, D), F32, kind="Internal").ap()
    y_table = nc.dram_tensor("y_table", (MAX_GROUPS * P, D), F32, kind="Internal").ap()
    build(nc, aps, out, x_table, y_table)
    r = run_bass_kernel_spmd(nc, [arrays], core_ids=[0])
    return r.results[0]["out"]
```

```python
from contextlib import ExitStack

import numpy as np
import concourse.bass as bass
from concourse import mybir

F32 = mybir.dt.float32
I32 = mybir.dt.int32
ALU = mybir.AluOpType
ACT = mybir.ActivationFunctionType
AX = mybir.AxisListType

P = 128
D = 1024
KD = D // P
SEQ = 256
DEPTH = 2
META = 16
T2 = META + SEQ
EPS = 1e-6
SLOTS = 4
UNIT = 6144

D_FF = 2816
FF_UNITS = D_FF // 256
FT = D_FF // P
HD = 64
LN_FLOOR = float(np.log(np.float32(1e-30)))

NG = 8
NE = 64
BLK = 32
TOPK = 2
GROUP = SLOTS
MAX_BLOCKS = NE + (T2 * TOPK) // BLK
MAX_GROUPS = -(-MAX_BLOCKS // GROUP)
DE = 256
Q_RANK = 384
KV_RANK = 256
ROPE2 = 64
NH2 = 8

TWO_PI = 2.0 * np.pi
C1 = 6.28125
C2 = float(np.float32(TWO_PI - C1))
C3 = float(np.float32(TWO_PI - C1 - np.float64(np.float32(C2))))
ROUND = 1.5 * 2.0 ** 23

LEVELS = [64, 32, 16, 8, 4, 2, 1, 0]


def const_table():
    p = np.arange(P)[:, None].astype(np.float64)
    c = np.arange(P)[None, :].astype(np.float64)
    parts, at, n = [], {}, 0

    def put(name, a):
        nonlocal n
        a = np.ascontiguousarray(np.broadcast_to(a, (P, a.shape[1]))).astype(np.float32)
        at[name] = (n, a.shape[1])
        parts.append(a)
        n += a.shape[1]

    put("ident", (p == c))
    put("ones", np.ones((P, P)))
    put("before", (p < c))
    put("upto", (p <= c))
    neg = -1e30
    put("window", np.concatenate([np.where(c > p, 0, neg), np.where(c <= p, 0, neg)], 1))
    key = np.arange(T2)[None, :]
    first, parts, first_n, n = parts, [], n, 0
    put("causal0", np.where(key <= META + p, 0, neg))
    put("causal1", np.where(key <= META + P + p, 0, neg))
    put("causal2", np.where(key[:, :META] <= p, 0, neg))
    put("iota", np.broadcast_to(c, (P, P)))
    put("block_starts", np.broadcast_to(BLK * (1 + np.arange(8))[None], (P, 8)))
    put("valid", np.concatenate([np.ones((P, 2)), (p < META)], 1))
    second, parts, second_n, n = parts, first, n, first_n
    inv = np.float32(10000.0) ** (-np.arange(32, dtype=np.float32) / np.float32(32))
    put("inv_freq", inv[None])
    inv2 = np.float32(10000.0) ** (-np.arange(0, 64, 2, dtype=np.float32) / np.float32(64))
    first, parts, first_n, n = parts, second, n, second_n
    pos = [np.arange(P) + META, np.arange(P) + META + P, np.minimum(np.arange(P), META - 1)]
    ang = np.stack([q.astype(np.float32)[:, None] * inv2[None] for q in pos], 1).astype(np.float32)
    put("cos2", np.cos(ang.astype(np.float64)).reshape(P, -1))
    put("sin2", np.sin(ang.astype(np.float64)).reshape(P, -1))
    second, parts, n = parts, first, first_n
    masks = []
    for s in LEVELS:
        if s:
            node = (p // (2 * s)) == (c // (2 * s))
            masks.append(node & (p % (2 * s) < s) & (c % (2 * s) >= s))
        else:
            masks.append(p == c)
    put("levels", np.concatenate(masks, 1))
    put("minus_half", np.full((P, 8), -0.5))
    return np.concatenate(parts, 1), np.concatenate(second, 1), at


CONSTS, CONSTS2, CONST_AT = const_table()
NCONST = CONSTS.shape[1]
NCONST2 = CONSTS2.shape[1]
SECOND = ("causal0", "causal1", "causal2", "iota", "block_starts", "valid", "cos2", "sin2")
ROWS2 = ["norm_mix_g_2", "norm_ffn_g_2", "kv_norm_g_2", "ckv_norm_g_2", "cq_norm_g_2", "conv_w_2",
         "hgrn_lb_logits"]


def row_starts(shapes):
    at, n = {}, 0
    for name in ROWS2:
        at[name] = n
        n += int(np.prod(shapes[name])) // P
    return at, n

ARENA = 12032


class Semaphores:

    def __init__(self, sem):
        self.const_loaded = sem("const_loaded")
        self.small_loaded = sem("small_loaded")
        self.h_loaded = sem("h_loaded")
        self.meta_loaded = sem("meta_loaded")
        self.rows_loaded = sem("rows_loaded")
        self.pad = sem("pad")
        self.h_upd = sem("h_upd")
        self.h_first_tile = sem("h_first_tile")
        self.ms_ready = sem("ms_ready")
        self.rstd_ready = sem("rstd_ready")
        self.square_done = sem("square_done")
        self.xn_ready = sem("xn_ready")
        self.xn_turned = sem("xn_turned")
        self.xT_ready = sem("xT_ready")
        self.gateup_done = sem("gateup_done")
        self.silu_ready = sem("silu_ready")
        self.hidden_ready = sem("hidden_ready")
        self.down_done = sem("down_done")
        self.qf_done = sem("qf_done")
        self.qf_copied = sem("qf_copied")
        self.z_done = sem("z_done")
        self.hihg_copied = sem("hihg_copied")
        self.susv_copied = sem("susv_copied")
        self.qkv_copied = sem("qkv_copied")
        self.hgrn_vec = sem("hgrn_vec")
        self.hgrn_act = sem("hgrn_act")
        self.hgrn_pe = sem("hgrn_pe")
        self.roped = sem("roped")
        self.qk_turned = sem("qk_turned")
        self.qkT_ready = sem("qkT_ready")
        self.scores_done = sem("scores_done")
        self.scores_ready = sem("scores_ready")
        self.probs_ready = sem("probs_ready")
        self.probs_turned = sem("probs_turned")
        self.probsT_ready = sem("probsT_ready")
        self.attn_done = sem("attn_done")
        self.sgw_turned = sem("sgw_turned")
        self.sgw_ready = sem("sgw_ready")
        self.centred = sem("centred")
        self.sv_ready = sem("sv_ready")
        self.spatial_done = sem("spatial_done")
        self.wout_done = sem("wout_done")
        self.gate_done = sem("gate_done")
        self.gate_ready = sem("gate_ready")
        self.p_turned = sem("p_turned")
        self.pT_ready = sem("pT_ready")
        self.proj_done = sem("proj_done")
        self.ple_ready = sem("ple_ready")
        self.lb_vec = sem("lb_vec")
        self.lb_act = sem("lb_act")
        self.rope_vec = sem("rope_vec")
        self.rope_ready = sem("rope_ready")
        self.rowsT_done = sem("rowsT_done")
        self.out_ready = sem("out_ready")
        self.out_stored = sem("out_stored")
        self.conv_products = sem("conv_products")
        self.conv_ready = sem("conv_ready")
        self.conv_copied = sem("conv_copied")
        self.mixed_done = sem("mixed_done")
        self.const2_loaded = sem("const2_loaded")
        self.final_loaded = sem("final_loaded")
        self.mla_down_done = sem("mla_down_done")
        self.mla_normed = sem("mla_normed")
        self.mla_turned = sem("mla_turned")
        self.mla_latents = sem("mla_latents")
        self.mla_copied = sem("mla_copied")
        self.mla_products = sem("mla_products")
        self.mla_roped = sem("mla_roped")
        self.mla_scores = sem("mla_scores")
        self.mla_probs = sem("mla_probs")
        self.mla_probs_turned = sem("mla_probs_turned")
        self.mla_probsT = sem("mla_probsT")
        self.mla_pv = sem("mla_pv")
        self.mla_out = sem("mla_out")
        self.mla_lat_copied = sem("mla_lat_copied")
        self.mla_masked = sem("mla_masked")


class MoeSemaphores:

    def __init__(self, sem):
        self.router_loaded = sem("router_loaded")
        self.logits = sem("logits")
        self.vec_step = sem("vec_step")
        self.act_step = sem("act_step")
        self.counted = sem("counted")
        self.tables = sem("tables")
        self.routed = sem("routed")
        self.onehot_ready = sem("onehot_ready")
        self.selected = sem("selected")
        self.xgT_ready = sem("xgT_ready")
        self.hid_turned = sem("hid_turned")
        self.hidT_ready = sem("hidT_ready")
        self.silu = sem("silu")
        self.hidden = sem("hidden")
        self.y_copied = sem("y_copied")
        self.cleared = sem("cleared")
        self.weights_ready = sem("weights_ready")
        self.combined = sem("combined")
        self.added = sem("added")




def build(nc, A, out):
    ctx = ExitStack()
    with ctx:
        def sb(name, shape, dt=F32):
            return ctx.enter_context(nc.sbuf_tensor(name, shape, dt))

        S = Semaphores(lambda name: ctx.enter_context(nc.semaphore(name)))
        S_mla = [ctx.enter_context(nc.semaphore(f"mla_loaded{i}")) for i in range(5)]
        unit_loaded = [ctx.enter_context(nc.semaphore(f"unit_loaded{i}")) for i in range(SLOTS)]
        unit_free = [ctx.enter_context(nc.semaphore(f"unit_free{i}")) for i in range(SLOTS)]

        ring = sb("ring", [P, SLOTS, UNIT])
        h = sb("h", [P, 3, D])
        xn = sb("xn", [P, 3, D])
        xT = sb("xT", [P, KD, T2])
        const = sb("const", [P, NCONST])
        gT1 = sb("gT1", [P, P])
        gT2 = sb("gT2", [P, P])
        small = sb("small", [P, 256])
        rows = sb("rows", [P, 4, D])
        arena = sb("arena", [P, ARENA])
        PS = ctx.enter_context(nc.psum_tensor("PS", [P, 8, 512], F32))

        rowsf = rows[:, :, :].rearrange("p a b -> p (a b)")
        const2 = rowsf[:, 0:NCONST2]
        xT2 = rowsf[:, 1024:1024 + KD * T2].rearrange("p (k t) -> p k t", k=KD)

        def cst(name):
            o, n = CONST_AT[name]
            return const2[:, o:o + n] if name in SECOND else const[:, o:o + n]

        ident = cst("ident")
        row_at, n_rows2 = row_starts({k: A[k].shape for k in ROWS2})

        ss = small[:, 0:8]
        ms = small[:, 8:16]
        rs = small[:, 16:24]
        mean = small[:, 24:26]
        lb = small[:, 32:44].rearrange("p (l v c) -> p l v c", l=2, v=3)
        lbl = small[:, 44:50].rearrange("p (v c) -> p v c", v=3)
        smax = small[:, 56:64]
        sneg = small[:, 64:72]
        ssink = small[:, 72:80]
        ssum = small[:, 80:88]
        sden = small[:, 88:96]
        srden = small[:, 96:104]
        posf = small[:, 104:106]
        posi = small[:, 106:108].bitcast(I32)
        lbt = small[:, 108:124]
        gl = sb("gl", [P, 8 * KD])
        rope_cos = sb("rope_cos", [P, 2, 32])[:, :, :]
        rope_sin = sb("rope_sin", [P, 2, 32])[:, :, :]
        sgw = sb("sgw", [P, 4, P])
        sgb = sb("sgb", [P, 4])
        lng = sb("lng", [P, 256])
        hgn = sb("hgn", [P, HD])
        sinks = sb("sinks", [P, 8])

        def take(at, shape):
            n = int(np.prod(shape))
            assert at + n <= ARENA, (at, shape)
            v = arena[:, at:at + n]
            if len(shape) == 2:
                v = v.rearrange("p (a b) -> p a b", a=shape[0])
            elif len(shape) == 3:
                v = v.rearrange("p (a b c) -> p a b c", a=shape[0], b=shape[1])
            elif len(shape) == 4:
                v = v.rearrange("p (a b c d) -> p a b c d", a=shape[0], b=shape[1], c=shape[2])
            return v

        silu = take(0, [2, 256])
        hid = take(512, [2, 256])
        z = take(0, [2, 1792])
        qT = take(3584, [2, 256])
        fs = take(4096, [2, 256])
        w1 = take(4608, [2, 256])
        w2 = take(5120, [2, 256])
        w3 = take(5632, [2, 256])
        w4 = take(6144, [2, 256])
        w5 = take(6656, [2, 256])
        w6 = take(7168, [2, 256])
        kT = take(7680, [2, 256])
        dif = take(5120, [2, 2, 256])
        ex = take(8192, [2, 2, 256])
        lev = take(9216, [2, 2, 256])
        att = xn[:, 2, :].rearrange("p (a b c q) -> p a b c q", a=2, b=2, c=2)
        att10 = take(11520, [2, 2, P])
        rprod = take(4608, [4, 1280 // 2])
        rot = take(8192, [2, 640])
        qkT = take(10240, [5, 256])
        ssb = take(3584, [8, 256])
        pT_ = take(7680, [8, 2, P])
        lnw = take(5760, [2, 256])
        sgwT = take(6272, [4, P])
        sgm_mix = take(6784, [2, 256])
        sgm = take(0, [2, D])
        pleT = take(2048, [2, 256])

        def xcol(t):
            return slice(META + P * t, META + P * (t + 1)) if t < 2 else slice(0, META)

        def yps(t):
            return PS[:, 2 * t:2 * t + 2, :]

        def tile2(v):
            return v.rearrange("p (a b) -> p a b", a=2)

        def slot_w(slot, k, w):
            return ring[:, slot, 0:k * w].rearrange("p (k w) -> p k w", k=k)

        def turned_tiles(q, tiles):
            return 2 * q if tiles == 2 else 2 * FIRST_TURNS + 3 * (q - FIRST_TURNS)

        FIRST_TURNS = 5 * DEPTH
        x_in = A["x"].rearrange("o (t p) d -> p (o t) d", p=P)
        block = ctx.enter_context(nc.Block())
        U_FFN1, U_IN, U_OUT, U_FFN2, U_PLE, U_LAYER = 0, 11, 16, 18, 29, 32
        USES = U_LAYER // SLOTS
        IN_COLS = [(0, 512), (512, 512), (1024, 512), (1536, 256), (1792, 512)]


        G2 = {k: row_at[k] for k in ROWS2}

        def cols(name, n, first=0):
            return gT2[:, G2[name] + first:G2[name] + first + n]

        def several(name, n):
            return [[ctx.enter_context(nc.semaphore(f"moe{i}_{name}{j}")) for j in range(n)] for i in range(DEPTH)]

        gu_loaded, gu_free = several("gu_loaded", SLOTS), several("gu_free", SLOTS)
        dn_loaded, dn_free = several("dn_loaded", 2), several("dn_free", 2)
        M = [MoeSemaphores(lambda name: ctx.enter_context(nc.semaphore(f"moe{i}_{name}"))) for i in range(DEPTH)]

        cb = take(0, [2, 2, T2])
        zp = take(1088, [2, T2 + 2])
        cy = take(1636, [2, T2])
        convT = take(2180, [KD, T2])
        wr = take(11400, [KD, NG + NE])
        gk = arena[:, 11976:11984]
        lg2 = take(576, [3, NG + NE])
        r8 = [take(800 + 24 * i, [3, 8]) for i in range(10)]
        r1 = [arena[:, 1044 + 4 * i:1047 + 4 * i] for i in range(12)]
        e1, e2, msel, rsel, ta, tb = [take(1100 + 192 * i, [3, NE]) for i in range(6)]
        thr = take(2252, [NE, 8])
        nextra, xend, xstart, first_slot, extra_slot = [arena[:, 2764 + 64 * i:2828 + 64 * i] for i in range(5)]
        dg = arena[:, 3084:3148]
        endcol = arena[:, 3148:3149]
        cmpe = arena[:, 3152:3184]
        eid = arena[:, 3184:3280].bitcast(I32)
        ng = arena[:, 3280:3281].bitcast(I32)
        pos = arena[:, 3292:3298]
        cmpk = arena[:, 3300:3308]
        ngf = arena[:, 3308:3309]
        oh1, onehot = take(3312, [3, P]), take(3696, [3, P])
        xgT = take(4400, [KD, P])
        sl = arena[:, 5424:5680]
        hid2 = arena[:, 5680:5936]
        hidT = take(5936, [2, P])
        ysb = arena[:, 6704:7728]
        weightsT = arena[:, 7728:7728 + T2]
        weights_, weights1 = take(8000, [3, P]), take(8400, [3, P])
        wgt = {i: arena[:, 10800 + 4 * i:10803 + 4 * i] for i in range(2)}

        lat = take(0, [3, KV_RANK + ROPE2 + Q_RANK])
        ckvT = take(2112, [2, T2])
        cqT = take(2656, [3, T2])
        krT = arena[:, 3472:3472 + T2]
        qrT = take(3744, [NH2 // 2, T2])
        val = take(4832, [3, NH2 * P])
        qr = take(7904, [3, NH2 * ROPE2])
        qro = take(9440, [3, NH2 * ROPE2])
        kro = take(10976, [3, 2, ROPE2])
        knT, qnT = xT2, xT
        prob = [take(0, [4, T2]), take(1088, [4, T2])]
        probT = [take(7904, [4, 3, P]), take(9440, [4, 3, P])]
        STEPS = [(t, hf) for t in range(3) for hf in range(2)]

        def keys(t):
            return {0: (META + P, [0, 2]), 1: (T2, [0, 1, 2]), 2: (META, [2])}[t]

        def mla_weights(sp, groups):
            def load(n, slot, parts):
                for dst, src in parts:
                    sp.dma_start(dst, src).then_inc(S_mla[n], 16)
            for j in range(SLOTS):
                sp.wait_ge(gu_free[0][j], groups + 1)
                sp.wait_ge(dn_free[0][j // 2], groups + 1)
                if j == 0:
                    dkv, dq = mla_down_views()
                    load(0, 0, [(dkv, A["w_dkv_2"].rearrange("(k p) f -> p k f", p=P)),
                                (dq[:, 0:4], A["w_dq_2"][0].rearrange("(k p) f -> p k f", p=P)[:, 0:4]),
                                (dq[:, 4:8], A["w_dq_2"][0].rearrange("(k p) f -> p k f", p=P)[:, 4:8])])
                elif j == 1:
                    src, dst = A["w_ukv_2"].rearrange("(k p) f -> p k f", p=P), slot_w(1, 2, 2 * D)
                    load(1, 1, [(dst[:, k:k + 1], src[:, k:k + 1]) for k in range(2)])
                elif j == 2:
                    src, dst = A["w_uq_2"][0].rearrange("(k p) f -> p k f", p=P), slot_w(2, 3, 1536)
                    load(2, 2, [(dst[:, k:k + 1], src[:, k:k + 1]) for k in range(3)])
            wo = A["w_o_2"][0].rearrange("(k p) f -> p k f", p=P)
            load(3, 3, [(slot_w(3, KD, 512)[:, a:a + 4], wo[:, a:a + 4, 0:512]) for a in (0, 4)])
            sp.wait_ge(S.mla_down_done, 1)
            load(4, 0, [(slot_w(0, KD, 512)[:, a:a + 4], wo[:, a:a + 4, 512:1024]) for a in (0, 4)])

        MLA_LOADS = [3, 2, 3, 2, 2]

        def mla_down_views():
            return (ring[:, 0, 0:KD * 320].rearrange("p (k f) -> p k f", k=KD),
                    ring[:, 0, KD * 320:KD * 704].rearrange("p (k f) -> p k f", k=KD))

        def mla_pe(pe, turn):
            mm = nc.tensor.matmul
            turn(12, 3)
            dkv, dq = mla_down_views()
            pe.wait_ge(S_mla[0], 16 * MLA_LOADS[0])
            for t in range(3):
                dense_rows(xT2, dkv, 5 + t, t, 320, KD)
                last = dense_rows(xT, dq, t, t, 384, KD)
            last.then_inc(S.mla_down_done, 1)
            pe.wait_ge(S.mla_normed, 1)
            for t in range(3):
                w = META if t == 2 else P
                for bank, c0 in ((3, 0), (4, P), (5, 320), (6, 320 + P), (7, 320 + 2 * P)):
                    nc.tensor.transpose(PS[:, bank, xcol(t)], lat[0:w, t, c0:c0 + P], ident[0:w, 0:w])
                last = nc.tensor.transpose(PS[:, 0, xcol(t)], kro[0:w, t].rearrange("p a b -> p (a b)"), ident[0:w, 0:w])
            last.then_inc(S.mla_turned, 1)
            pe.wait_ge(S.mla_latents, 1)
            ukv = slot_w(1, 2, 2 * D).rearrange("p k (h f) -> p k h f", h=NH2)
            uq = slot_w(2, 3, 1536).rearrange("p k (h f) -> p k h f", h=NH2)
            n = 0

            def bank_of(n):
                if n >= 8:
                    pe.wait_ge(S.mla_copied, n - 7)
                return n % 8
            pe.wait_ge(S_mla[2], 16 * MLA_LOADS[2])
            for t in range(3):
                w, b = (META if t == 2 else P), bank_of(n)
                for k in range(3):
                    last = mm(PS[0:w, b, :], lhsT=cqT[:, k, xcol(t)], rhs=uq[:, k, :, P:P + ROPE2], start=k == 0, stop=k == 2)
                last.then_inc(S.mla_products, 1)
                n += 1
            pe.wait_ge(S_mla[1], 16 * MLA_LOADS[1])
            for wt, src, kk in ((ukv, ckvT, 2), (uq, cqT, 3)):
                for hd in range(NH2):
                    b = bank_of(n)
                    for k in range(kk):
                        last = mm(PS[:, b, 0:T2], lhsT=wt[:, k, hd, 0:P], rhs=src[:, k, :], start=k == 0, stop=k == kk - 1)
                    last.then_inc(S.mla_products, 1)
                    n += 1
            for t in range(3):
                w = META if t == 2 else P
                for hf in range(2):
                    b = bank_of(n)
                    for k in range(2):
                        last = mm(PS[0:w, b, :], lhsT=ckvT[:, k, xcol(t)], rhs=ukv[:, k, 4 * hf:4 * hf + 4, P:2 * P],
                                  start=k == 0, stop=k == 1)
                    last.then_inc(S.mla_products, 1)
                    n += 1
            pe.wait_ge(S.mla_roped, 1)
            for pair in range(NH2 // 2):
                b = bank_of(n)
                for t in range(3):
                    w = META if t == 2 else P
                    last = nc.tensor.transpose(PS[:, b, xcol(t)], qro[0:w, t, pair * P:(pair + 1) * P], ident[0:w, 0:w])
                last.then_inc(S.mla_products, 1)
                n += 1
            assert n == MLA_ITEMS
            for slot in (1, 2):
                pe.drain().then_inc(gu_free[1][slot], 1)
            pe.wait_ge(S.mla_copied, MLA_ITEMS)

            def scores(s):
                (t, hf), nk = STEPS[s], keys(STEPS[s][0])[0]
                w = META if t == 2 else P
                if s >= 2:
                    pe.wait_ge(S.mla_out, s - 1)
                for i in range(4):
                    hd = 4 * hf + i
                    r = slice(64 * (hd % 2), 64 * (hd % 2) + 64)
                    o = PS[0:w, 4 * (s % 2) + i, 0:nk]
                    mm(o, lhsT=qnT[:, hd, xcol(t)], rhs=knT[:, hd, 0:nk], start=True, stop=False)
                    last = mm(o, lhsT=qrT[r, hd // 2, xcol(t)], rhs=krT[r, 0:nk], start=False, stop=True)
                last.then_inc(S.mla_scores, 1)

            def outputs(s):
                (t, hf), pieces = STEPS[s], keys(STEPS[s][0])[1]
                w, b = (META if t == 2 else P), 4 * (s % 2)
                pe.wait_ge(S.mla_probs, s + 1)
                for i in range(4):
                    for c in pieces:
                        ck = META if c == 2 else P
                        last = nc.tensor.transpose(PS[0:ck, b + i, c * P:c * P + w], prob[s % 2][0:w, i, xcol(c)], ident[0:w, 0:w])
                last.then_inc(S.mla_probs_turned, 1)
                pe.wait_ge(S.mla_probsT, s + 1)
                for i in range(4):
                    hd = 4 * hf + i
                    for n_, c in enumerate(pieces):
                        ck = META if c == 2 else P
                        last = mm(PS[0:w, b, i * P:(i + 1) * P], lhsT=probT[s % 2][0:ck, i, c, 0:w],
                                  rhs=val[0:ck, c, hd * P:(hd + 1) * P], start=n_ == 0, stop=n_ == len(pieces) - 1)
                last.then_inc(S.mla_pv, 1)
            scores(0)
            for s in range(len(STEPS)):
                if s + 1 < len(STEPS):
                    scores(s + 1)
                outputs(s)
            turn(13, 3)
            for i, (slot, n) in enumerate([(3, 3), (0, 4)]):
                pe.wait_ge(S_mla[n], 16 * MLA_LOADS[n])
                for t in range(3):
                    last = dense_rows(xT, slot_w(slot, KD, 512), 2 * t + i, t, 512, KD)
                pe.drain().then_inc(gu_free[1][slot], 1)
            for f in dn_free[1]:
                pe.drain().then_inc(f, 1)
            pe.drain().then_inc(S.mixed_done, 1)

        MLA_ITEMS = 3 + 2 * NH2 + 6 + NH2 // 2

        def mla_act(act, norm):
            a_ = nc.scalar
            norm(10, 3)
            router_loads(act, 1)
            act.wait_ge(S.mla_lat_copied, 1)
            for r, c0, n in ((23, 0, KV_RANK), (24, 320, Q_RANK)):
                act.wait_ge(S.ms_ready, r)
                for t in range(3):
                    w = META if t == 2 else P
                    last = a_.activation(xn[0:w, t, 0:n], lat[0:w, t, c0:c0 + n], ACT.Square, accum_out=ss[0:w, t:t + 1])
                last.then_inc(S.square_done, 1)
                if r == 23:
                    act.drain()
            n = 0

            def copy(dst, w, cols_):
                nonlocal n
                act.wait_ge(S.mla_products, n + 1)
                a_.activation(dst, PS[0:w, n % 8, 0:cols_], ACT.Copy).then_inc(S.mla_copied, 1)
                n += 1
            for t in range(3):
                w = META if t == 2 else P
                copy(qr[0:w, t, :], w, 512)
            for dst in (knT, qnT):
                for hd in range(NH2):
                    copy(dst[:, hd, :], P, T2)
            for t in range(3):
                for hf in range(2):
                    w = META if t == 2 else P
                    copy(val[0:w, t, hf * 512:(hf + 1) * 512], w, 512)
            for pair in range(NH2 // 2):
                copy(qrT[:, pair, :], P, T2)
            for s, (t, hf) in enumerate(STEPS):
                w, (nk, pieces), b = (META if t == 2 else P), keys(t), 4 * (s % 2)
                act.wait_ge(S.mla_masked, s + 1)
                for i in range(4):
                    last = a_.activation(prob[s % 2][0:w, i, 0:nk], prob[s % 2][0:w, i, 0:nk], ACT.Exp,
                                         bias=sneg[0:w, b + i:b + i + 1], accum_out=ssum[0:w, b + i:b + i + 1])
                last.then_inc(S.mla_probs, 1)
                act.wait_ge(S.mla_probs_turned, s + 1)
                nx = len(pieces) - 1
                if nx:
                    a_.activation(probT[s % 2][:, :, 0:nx, :], PS[:, b:b + 4, 0:nx * P].rearrange("p i (c q) -> p i c q", q=P), ACT.Copy)
                a_.activation(probT[s % 2][0:META, :, 2, 0:w], PS[0:META, b:b + 4, 2 * P:2 * P + w], ACT.Copy).then_inc(S.mla_probsT, 1)
            act.wait_ge(S.h_upd, 12)
            act.dma_start(rows[:, 3, :], A["final_norm_g_2"].unsqueeze(0).to_broadcast([P, D])).then_inc(S.final_loaded, 16)

        def mla_vec(dve, rstd, turned, norm):
            v_, settle = nc.vector, dve.drain
            norm(22, 12, [(xT, cols("norm_mix_g_2", 8, 8)), (xT2, cols("kv_norm_g_2", 8))], 3)
            dve.wait_ge(S.mla_down_done, 1)
            for t in range(3):
                w = META if t == 2 else P
                v_.tensor_copy(lat[0:w, t, 0:320], PS[0:w, 5 + t, 0:320])
                last = v_.tensor_copy(lat[0:w, t, 320:704], PS[0:w, t, 0:384])
            last.then_inc(S.mla_lat_copied, 1)
            settle()

            def rotate(w, ts, x, heads, out, scratch):
                nt = ts.stop - ts.start
                cs, sn = [cst(n).rearrange("p (t d) -> p t d", d=32)[0:w, ts].unsqueeze(2).to_broadcast([w, nt, heads, 32])
                          for n in ("cos2", "sin2")]
                size = nt * heads * 32
                pr = [scratch[0:w, i * size:(i + 1) * size].rearrange("p (t h d) -> p t h d", t=nt, d=32) for i in range(4)]
                for p_, (e, c) in zip(pr, [(0, cs), (1, sn), (0, sn), (1, cs)]):
                    v_.tensor_tensor(p_, x[:, :, :, e, :], c, ALU.mult)
                settle()
                outs = []
                for e, (a, b, op) in enumerate([(pr[0], pr[1], ALU.subtract), (pr[2], pr[3], ALU.add)]):
                    o = out(e)
                    if o.shape[2] != heads:
                        a, b = a.to_broadcast([w, nt, o.shape[2], 32]), b.to_broadcast([w, nt, o.shape[2], 32])
                    outs.append(v_.tensor_tensor(o, a, b, op))
                return outs[-1]

            TILES = ((P, slice(0, 2)), (META, slice(2, 3)))
            for w, ts in TILES:
                rotate(w, ts, lat[0:w, ts, KV_RANK:320].rearrange("p t (h e d) -> p t h e d", h=1, e=2), 1,
                       lambda e: kro[0:w, ts, :, e * 32:(e + 1) * 32], xn[:, 0, 512:1024])
                settle()
            for r, c0, n in ((23, 0, KV_RANK), (24, 320, Q_RANK)):
                rstd(r, 3, n)
                for t in range(3):
                    w = META if t == 2 else P
                    last = v_.tensor_scalar(lat[0:w, t, c0:c0 + n], lat[0:w, t, c0:c0 + n], rs[0:w, t:t + 1], None, ALU.mult)
            last.then_inc(S.mla_normed, 1)
            dve.wait_ge(S.mla_turned, 1)
            for k in range(2):
                v_.tensor_scalar(ckvT[:, k, :], PS[:, 3 + k, 0:T2], cols("ckv_norm_g_2", 1, k), None, ALU.mult)
            for k in range(3):
                v_.tensor_scalar(cqT[:, k, :], PS[:, 5 + k, 0:T2], cols("cq_norm_g_2", 1, k), None, ALU.mult)
            v_.tensor_copy(krT, PS[:, 0, 0:T2]).then_inc(S.mla_latents, 1)
            dve.wait_ge(S.mla_copied, 3)
            scratch = xn[:, :, :].rearrange("p t d -> p (t d)")
            for w, ts in TILES:
                x = qr[0:w, ts].rearrange("p t (h e d) -> p t h e d", h=NH2, e=2)
                y = qro[0:w, ts].rearrange("p t (h e d) -> p t h e d", h=NH2, e=2)
                last = rotate(w, ts, x, NH2, lambda e: y[:, :, :, e, :], scratch)
                if ts.start == 0:
                    settle()
            last.then_inc(S.mla_roped, 1)

            def masked(s):
                (t, hf), nk, b = STEPS[s], keys(STEPS[s][0])[0], 4 * (s % 2)
                w = META if t == 2 else P
                dve.wait_ge(S.mla_scores, s + 1)
                pv = prob[s % 2][0:w, :, 0:nk]
                v_.scalar_tensor_tensor(pv, PS[0:w, b:b + 4, 0:nk], (P + ROPE2) ** -0.5,
                                        cst(f"causal{t}")[0:w, 0:nk].unsqueeze(1).to_broadcast([w, 4, nk]), ALU.mult, ALU.add)
                settle()
                v_.tensor_reduce(smax[0:w, b:b + 4], pv, AX.X, ALU.max)
                settle()
                v_.tensor_scalar(sneg[0:w, b:b + 4], smax[0:w, b:b + 4], -1.0, None, ALU.mult).then_inc(S.mla_masked, 1)
            masked(0)
            for s, (t, hf) in enumerate(STEPS):
                w, b = (META if t == 2 else P), 4 * (s % 2)
                if s + 1 < len(STEPS):
                    masked(s + 1)
                dve.wait_ge(S.mla_pv, s + 1)
                v_.reciprocal(srden[0:w, b:b + 4], ssum[0:w, b:b + 4])
                settle()
                v_.tensor_tensor(xn[0:w, t, hf * 512:(hf + 1) * 512].rearrange("p (h e) -> p h e", e=P),
                                 PS[0:w, b, :].rearrange("p (h e) -> p h e", e=P),
                                 srden[0:w, b:b + 4].unsqueeze(2).to_broadcast([w, 4, P]), ALU.mult).then_inc(S.mla_out, 1)
            dve.drain().then_inc(S.xn_ready, 3)
            turned(13, 3, [(xT, None)])
            dve.wait_ge(S.mixed_done, 2)
            add_to_h()

        def second_weights(sp, load):
            bcu = A["conv_w_in_2"][0].rearrange("(k p) f -> p k f", p=P)
            for i in range(4):
                v = ring[:, i, :].rearrange("p (s k f) -> p s k f", s=3, k=KD)
                load(16, i, [(v[:, s], bcu[:, :, s * D + 256 * i:s * D + 256 * (i + 1)]) for s in range(3)])
            for i in range(2):
                w = A["conv_w_out_2"][0].rearrange("(k p) f -> p k f", p=P)
                dst = slot_w(i, KD, 512)
                load(17, i, [(dst[:, a:b], w[:, a:b, 512 * i:512 * (i + 1)]) for a, b in ((0, 3), (3, 6), (6, 8))])
            groups = experts(sp, 0)
            mla_weights(sp, groups)
            experts(sp, 1)

        def experts(sp, i):
            def gate_up(e, j, n):
                sp.wait_ge(gu_free[i][j], n)
                v = ring[:, j, 0:4096].rearrange("p (s k f) -> p s k f", s=2, k=KD)
                for s, name in enumerate(("w_gate_2", "w_up_2")):
                    sp.dma_start(v[:, s], A[name][i][e].rearrange("o (p k) f -> p (o k) f", k=KD)).then_inc(gu_loaded[i][j], 16)

            def down(e, j, n):
                sp.wait_ge(dn_free[i][j // 2], n)
                sp.dma_start(ring[:, j, 4096:6144].rearrange("p (f n) -> p f n", f=2),
                             A["w_down_2"][i][e].rearrange("o (f p) n -> p (o f) n", p=P)).then_inc(dn_loaded[i][j // 2], 16)

            for part in (gate_up, down):
                for j in range(GROUP):
                    part(slice(j, j + 1), j, 1)
            sp.wait_ge(M[i].routed, 1)
            groups = sp.value_load(ng[0:1, 0:1], min_val=NE // GROUP, max_val=MAX_GROUPS)
            with sp.Fori(1, groups) as g:
                es = [sp.value_load(eid[0:1, bass.ds(g * GROUP + j, 1)], min_val=0, max_val=NE - 1) for j in range(GROUP)]
                for part in (gate_up, down):
                    for j in range(GROUP):
                        part(bass.ds(es[j], 1), j, g + 1)
            return groups

        def second_pool(pool, rstd):
            rstd(20, 3)
            rstd(21, 3)
            rstd(22, 3)
            rstd(23, 3)
            rstd(24, 3)
            rstd(25, 3)
            rstd(26, 2)

        def second_act(act, norm, squares):
            a_ = nc.scalar
            act.wait_ge(S.h_upd, 9)
            act.dma_start(const2, A["const_table2"]).then_inc(S.const2_loaded, 16)
            router_loads(act, 0)
            act.wait_ge(S.h_first_tile, 9)
            norm(8, 3)
            for x in range(KD):
                act.wait_ge(S.conv_products, x + 1)
                if x >= 2:
                    act.wait_ge(S.conv_ready, x - 1)
                for s in range(2):
                    last = a_.activation(cb[:, x % 2, s, :], PS[:, 3 * (x % 2) + s, 0:T2], ACT.Copy)
                last.then_inc(S.conv_copied, 1)
            moe_act(act, 0, norm, 9)
            mla_act(act, norm)
            moe_act(act, 1, norm, 11)
            act.wait_ge(S.h_upd, 13)
            squares(0, 2, lambda t: h[:, t, :])

        def router_loads(act, i):
            with nc.allow_non_contiguous_dma(reason="short rows"):
                act.dma_start(wr[:, :, 0:NG], A["w_grp_2"][i].rearrange("(k p) f -> p k f", p=P)).then_inc(M[i].router_loaded, 16)
                act.dma_start(gk, A["norm_ffn_g_2"][i].rearrange("(p k) -> p k", k=KD)).then_inc(M[i].router_loaded, 16)
            act.dma_start(wr[:, :, NG:], A["w_exp_2"][i].rearrange("(k p) f -> p k f", p=P)).then_inc(M[i].router_loaded, 16)

        def moe_act(act, i, norm, n):
            a_ = nc.scalar
            norm(n, 3)
            act.wait_ge(M[i].vec_step, 1)
            a_.activation(r8[2], r8[1], ACT.Exp).then_inc(M[i].act_step, 1)
            act.wait_ge(M[i].vec_step, 2)
            a_.activation(r1[4], r1[3], ACT.Exp).then_inc(M[i].act_step, 1)
            act.wait_ge(M[i].routed, 1)
            groups = act.value_load(ng[0:1, 0:1], min_val=NE // GROUP, max_val=MAX_GROUPS)
            act.wait_ge(M[i].cleared, 1)
            act.sem_inc(M[i].y_copied, 1)
            with act.Fori(0, groups) as g:
                act.wait_ge(gu_free[i][GROUP - 1], g + 2)
                act.wait_ge(M[i].hidden, g + 1)
                a_.activation(sl, PS[:, 2, 0:DE], ACT.Silu).then_inc(M[i].silu, 1)
                act.wait_ge(M[i].hid_turned, g + 1)
                a_.activation(weightsT, PS[:, 4, 0:T2], ACT.Copy)
                a_.activation(hidT, PS[:, 3, 0:2 * P].rearrange("p (f c) -> p f c", f=2), ACT.Copy).then_inc(M[i].hidT_ready, 1)
                act.wait_ge(dn_free[i][1], g + 2)
                a_.activation(tile2(ysb), PS[:, 4:6, :], ACT.Copy).then_inc(M[i].y_copied, 1)

        def second_vec(dve, rstd, turned, norm):
            v_, settle = nc.vector, dve.drain
            v_.memset(zp[:, :, 0:2], 0.0)
            norm(20, 10, [(xT, cols("norm_mix_g_2", 8))], 3)
            for x in range(KD):
                b = x % 2
                dve.wait_ge(S.conv_copied, x + 1)
                v_.tensor_tensor(zp[:, b, 2:], cb[:, b, 1, :], PS[:, 3 * b + 2, 0:T2], ALU.mult)
                settle()
                w = [cols("conv_w_2", 1, 8 * k + x) for k in range(3)]
                v_.tensor_scalar(cy[:, b, :], zp[:, b, 0:T2], w[0], None, ALU.mult)
                settle()
                for k in (1, 2):
                    v_.scalar_tensor_tensor(cy[:, b, :], zp[:, b, k:k + T2], w[k], cy[:, b, :], ALU.mult, ALU.add)
                    settle()
                v_.tensor_tensor(convT[:, x, :], cy[:, b, :], cb[:, b, 0, :], ALU.mult).then_inc(S.conv_ready, 1)
            dve.wait_ge(S.mixed_done, 1)
            add_to_h()
            moe_vec(dve, 0, rstd, turned, norm, 21, 11)
            mla_vec(dve, rstd, turned, norm)
            moe_vec(dve, 1, rstd, turned, norm, 25, 14)
            rstd(26, 2, D)
            dve.wait_ge(S.final_loaded, 16)
            for t in range(2):
                last = v_.scalar_tensor_tensor(xn[:, t, :], h[:, t, :], rs[:, t:t + 1], rows[:, 3, :], ALU.mult, ALU.mult)
            last.then_inc(S.out_ready, 1)

        def add_to_h():
            for t in range(3):
                w = META if t == 2 else P
                last = nc.vector.tensor_tensor(tile2(h[0:w, t, :]), tile2(h[0:w, t, :]), PS[0:w, 2 * t:2 * t + 2, :], ALU.add)
            last.then_inc(S.h_upd, 1)

        def moe_vec(dve, i, rstd, turned, norm, r, q):
            v_, settle = nc.vector, dve.drain
            dve.wait_ge(S.const2_loaded, 16)
            iota = cst("iota")
            iota8 = iota[:, 0:8].unsqueeze(1).to_broadcast([P, 3, 8])

            def b8(v):
                return v.unsqueeze(2).to_broadcast([P, 3, 8])

            def first_of(dst, vals, top, cand, least):
                v_.tensor_tensor(cand, vals, b8(top), ALU.is_equal)
                settle()
                v_.scalar_tensor_tensor(cand, cand, -1000.0, iota8, ALU.mult, ALU.add)
                settle()
                v_.tensor_reduce(least, cand, AX.X, ALU.min)
                settle()
                v_.tensor_tensor(dst, cand, b8(least), ALU.is_equal)

            norm(r, q, [(xT, cols("norm_ffn_g_2", 8, 8 * i))], 3)
            v_.memset(lg2, 0.0)
            settle()
            dve.wait_ge(M[i].logits, 1)
            v_.tensor_copy(lg2[:, 0:2, :], PS[:, 5, 0:144].rearrange("p (t c) -> p t c", t=2))
            v_.tensor_copy(lg2[0:META, 2, :], PS[0:META, 5, 144:216])
            settle()
            gl8 = lg2[:, :, 0:NG]
            v_.tensor_reduce(r1[0], gl8, AX.X, ALU.max)
            settle()
            v_.tensor_tensor(r8[1], gl8, b8(r1[0]), ALU.subtract).then_inc(M[i].vec_step, 1)
            first_of(r8[3], gl8, r1[0], r8[0], r1[1])
            settle()
            tmp = e1.rearrange("p t (e g) -> p t e g", e=8)
            v_.tensor_tensor(tmp, lg2[:, :, NG:].rearrange("p t (g e) -> p t e g", g=NG),
                             r8[3].unsqueeze(2).to_broadcast([P, 3, 8, 8]), ALU.mult)
            settle()
            v_.tensor_reduce(r8[4], tmp, AX.X, ALU.add)
            settle()
            v_.tensor_reduce(r1[1], r8[4], AX.X, ALU.max)
            settle()
            first_of(r8[5], r8[4], r1[1], r8[0], r1[2])
            settle()
            v_.scalar_tensor_tensor(r8[6], r8[5], -1e30, r8[4], ALU.mult, ALU.add)
            settle()
            v_.tensor_reduce(r1[2], r8[6], AX.X, ALU.max)
            settle()
            v_.tensor_tensor(r1[3], r1[2], r1[1], ALU.subtract).then_inc(M[i].vec_step, 1)
            first_of(r8[7], r8[6], r1[2], r8[0], r1[5])
            v_.tensor_tensor(r8[8], r8[3], b8(cst("valid")), ALU.mult)
            settle()
            for dst, one in ((e1, r8[5]), (e2, r8[7])):
                v_.tensor_tensor(dst.rearrange("p t (g e) -> p t g e", g=NG), r8[8].unsqueeze(3).to_broadcast([P, 3, 8, 8]),
                                 one.unsqueeze(2).to_broadcast([P, 3, 8, 8]), ALU.mult)
            settle()
            v_.tensor_tensor(msel, e1, e2, ALU.add).then_inc(M[i].vec_step, 1)
            dve.wait_ge(M[i].act_step, 2)
            v_.tensor_reduce(r1[6], r8[2], AX.X, ALU.add)
            v_.tensor_scalar(r1[7], r1[4], 1.0, None, ALU.add)
            settle()
            v_.tensor_tensor(r1[6], r1[6], r1[7], ALU.mult)
            settle()
            v_.reciprocal(wgt[0], r1[6])
            settle()
            v_.tensor_tensor(wgt[1], wgt[0], r1[4], ALU.mult)
            dve.wait_ge(M[i].counted, 1)
            cnt = PS[:, 6, 192:256]
            v_.tensor_tensor(thr, cnt.unsqueeze(2).to_broadcast([P, NE, 8]),
                             cst("block_starts").unsqueeze(1).to_broadcast([P, NE, 8]), ALU.is_gt)
            settle()
            v_.tensor_reduce(nextra, thr, AX.X, ALU.add)
            settle()
            v_.tensor_tensor_scan(xend, cst("ones")[:, 0:NE], nextra, 0.0, ALU.mult, ALU.add)
            v_.tensor_scalar(first_slot, iota[:, 0:NE], float(BLK), None, ALU.mult)
            settle()
            v_.tensor_tensor(xstart, xend, nextra, ALU.subtract)
            v_.tensor_tensor(dg, xend, ident[:, 0:NE], ALU.mult)
            v_.tensor_scalar(cmpk, iota[:, 0:8], float(GROUP), xend[:, NE - 1:NE], ALU.mult, ALU.is_lt)
            v_.tensor_scalar(ta, PS[:, 6, 0:192].rearrange("p (t e) -> p t e", t=3), float(BLK), None, ALU.is_ge)
            settle()
            v_.scalar_tensor_tensor(extra_slot, xstart, float(BLK), first_slot, ALU.mult, ALU.subtract)
            v_.tensor_reduce(endcol, dg, AX.X, ALU.add)
            v_.tensor_reduce(ngf, cmpk, AX.X, ALU.add)
            settle()
            v_.tensor_scalar(extra_slot, extra_slot, float(BLK * (NE - 1)), None, ALU.add)
            v_.tensor_scalar(ngf, ngf, float(NE // GROUP), None, ALU.add)
            v_.tensor_tensor(rsel, PS[:, 6, 0:192].rearrange("p (t e) -> p t e", t=3),
                             first_slot.unsqueeze(1).to_broadcast([P, 3, NE]), ALU.add)
            settle()
            v_.tensor_scalar(cmpe[0:NE, :], iota[0:NE, 0:32], endcol[0:NE, :], None, ALU.is_ge).then_inc(M[i].vec_step, 1)
            v_.tensor_copy(ng, ngf)
            v_.tensor_copy(eid[:, 0:NE], iota[:, 0:NE])
            v_.tensor_tensor(ta, ta, extra_slot.unsqueeze(1).to_broadcast([P, 3, NE]), ALU.mult)
            settle()
            v_.tensor_tensor(rsel, rsel, ta, ALU.add)
            settle()
            v_.tensor_tensor(ta, e1, rsel, ALU.mult)
            v_.tensor_tensor(tb, e2, rsel, ALU.mult)
            settle()
            v_.tensor_reduce(pos[:, 0:3], ta, AX.X, ALU.add)
            v_.tensor_reduce(pos[:, 3:6], tb, AX.X, ALU.add)
            settle()

            def selection(first=False):
                if not first:
                    v_.tensor_scalar(pos, pos, -float(P), None, ALU.add)
                settle()
                for t in range(3):
                    v_.tensor_scalar(oh1[:, t, :], iota, pos[:, t:t + 1], None, ALU.is_equal)
                settle()
                for t in range(3):
                    last = v_.scalar_tensor_tensor(onehot[:, t, :], iota, pos[:, 3 + t:4 + t], oh1[:, t, :],
                                                   ALU.is_equal, ALU.add)
                last.then_inc(M[i].onehot_ready, 1)

            def weights():
                for t in range(3):
                    v_.tensor_scalar(weights_[:, t, :], iota, pos[:, t:t + 1], wgt[0][:, t:t + 1], ALU.is_equal, ALU.mult)
                    v_.tensor_scalar(weights1[:, t, :], iota, pos[:, 3 + t:4 + t], wgt[1][:, t:t + 1], ALU.is_equal, ALU.mult)
                settle()
                v_.tensor_tensor(weights_, weights_, weights1, ALU.add).then_inc(M[i].weights_ready, 1)

            def add_outputs(g):
                for t in range(3):
                    w = META if t == 2 else P
                    dve.wait_ge(M[i].combined, 3 * g + t + 1)
                    v_.tensor_tensor(tile2(h[0:w, t, :]), tile2(h[0:w, t, :]), PS[0:w, 6:8, :], ALU.add).then_inc(M[i].added, 1)
            selection(first=True)
            v_.memset(ysb, 0.0)
            v_.memset(weightsT, 0.0)
            dve.drain().then_inc(M[i].cleared, 1)
            dve.wait_ge(M[i].tables, 1)
            v_.tensor_scalar(eid[:, NE:NE + 32], PS[:, 7, 0:32], float(NE - 1), None, ALU.min).then_inc(M[i].routed, 1)
            dve.wait_ge(M[i].routed, 1)
            groups = dve.value_load(ng[0:1, 0:1], min_val=NE // GROUP, max_val=MAX_GROUPS)
            dve.sem_inc(M[i].hidden, 1)
            dve.sem_inc(M[i].added, 1)
            with dve.Fori(0, groups) as g:
                dve.wait_ge(M[i].selected, g + 1)
                dve.wait_ge(gu_free[i][GROUP - 1], g + 1)
                v_.tensor_tensor(xgT, PS[:, 0:2, :].rearrange("p a (k w) -> p (a k) w", w=P),
                                 gk.unsqueeze(2).to_broadcast([P, KD, P]), ALU.mult).then_inc(M[i].xgT_ready, 1)
                dve.wait_ge(M[i].y_copied, g + 1)
                weights()
                settle()
                selection()
                add_outputs(g)
                dve.wait_ge(M[i].silu, g + 1)
                v_.tensor_tensor(hid2, sl, PS[:, 2, DE:2 * DE], ALU.mult).then_inc(M[i].hidden, 1)
            dve.wait_ge(M[i].selected, groups + 1)
            add_outputs(groups)
            dve.drain().then_inc(S.h_upd, 1)

        def second_pe(pe, turn, loaded, dense):
            mm = nc.tensor.matmul
            turn(10, 3)
            for x in range(KD):
                slot, j, b = x // 2, x % 2, x % 2
                w = ring[:, slot, :].rearrange("p (s k f) -> p s k f", s=3, k=KD)
                if j == 0:
                    loaded(16, slot)
                if x >= 2:
                    pe.wait_ge(S.conv_ready, x - 1)
                for s in range(3):
                    for k in range(KD):
                        last = mm(PS[:, 3 * b + s, 0:T2], lhsT=w[:, s, k, j * P:(j + 1) * P], rhs=xT[:, k, :],
                                  start=k == 0, stop=k == KD - 1)
                last.then_inc(S.conv_products, 1)
                if j == 1:
                    pe.drain().then_inc(unit_free[slot] if slot < 2 else gu_free[0][slot], 1)
                    if slot == 3:
                        pe.drain().then_inc(dn_free[0][1], 1)
            pe.wait_ge(S.conv_ready, KD)
            for i in range(2):
                loaded(17, i)
                for t in range(3):
                    last = dense_rows(convT, slot_w(i, KD, 512), 2 * t + i, t, 512, KD)
                pe.drain().then_inc(gu_free[0][i], 1)
            pe.drain().then_inc(dn_free[0][0], 1)
            pe.drain().then_inc(S.mixed_done, 1)
            moe_pe(pe, 0, turn, 11)
            mla_pe(pe, turn)
            moe_pe(pe, 1, turn, 14)

        def dense_rows(src, w, bank, t, width, kk, at=0):
            rows_ = META if t == 2 else P
            for k in range(kk):
                last = nc.tensor.matmul(PS[0:rows_, bank, at:at + width], lhsT=src[:, k, xcol(t)], rhs=w[:, k, 0:width],
                                        start=k == 0, stop=k == kk - 1)
            return last

        def moe_pe(pe, i, turn, q):
            mm = nc.tensor.matmul
            turn(q, 3)
            pe.wait_ge(M[i].router_loaded, 48)
            for t in range(3):
                last = dense_rows(xT, wr, 5, t, NG + NE, KD, at=t * (NG + NE))
            last.then_inc(M[i].logits, 1)
            pe.wait_ge(M[i].vec_step, 3)
            for t in range(3):
                for s in range(t + 1):
                    mm(PS[:, 6, t * NE:(t + 1) * NE], lhsT=cst("before") if s == t else cst("ones"), rhs=msel[:, s, :],
                       start=s == 0, stop=s == t)
            for s in range(3):
                last = mm(PS[:, 6, 192:256], lhsT=cst("ones"), rhs=msel[:, s, :], start=s == 0, stop=s == 2)
            last.then_inc(M[i].counted, 1)
            pe.wait_ge(M[i].vec_step, 4)
            mm(PS[:, 7, 0:32], lhsT=cst("ones")[0:NE, :], rhs=cmpe[0:NE, :], start=True, stop=True).then_inc(M[i].tables, 1)

            def select(n):
                pe.wait_ge(M[i].onehot_ready, n)
                xk = xn[:, :, :].rearrange("p t (c k) -> p t k c", k=KD)
                for k in range(KD):
                    for t in range(3):
                        w = META if t == 2 else P
                        last = mm(PS[:, k // 4, (k % 4) * P:(k % 4 + 1) * P], lhsT=xk[0:w, t, k, :], rhs=onehot[0:w, t, :],
                                  start=t == 0, stop=t == 2)
                last.then_inc(M[i].selected, 1)
            select(1)
            pe.wait_ge(M[i].routed, 1)
            groups = pe.value_load(ng[0:1, 0:1], min_val=NE // GROUP, max_val=MAX_GROUPS)

            def combine(n, t):
                w = META if t == 2 else P
                if t == 0:
                    pe.wait_ge(M[i].y_copied, n + 1)
                pe.wait_ge(M[i].added, 3 * n + t + 1)
                for c in range(2):
                    last = mm(PS[0:w, 6 + c, :], lhsT=weightsT[:, P * t:P * t + w], rhs=ysb[:, c * 512:(c + 1) * 512],
                              start=True, stop=True)
                last.then_inc(M[i].combined, 1)

            with pe.Fori(0, groups) as g:
                pe.wait_ge(M[i].xgT_ready, g + 1)

                for j in range(GROUP):
                    pe.wait_ge(gu_loaded[i][j], g * 32 + 32)
                    w = ring[:, j, 0:4096].rearrange("p (s k f) -> p s k f", s=2, k=KD)
                    for k in range(KD):
                        last = mm(PS[BLK * j:BLK * (j + 1), 2, :], lhsT=xgT[:, k, j * BLK:(j + 1) * BLK], rhs=w[:, :, k, :],
                                  start=k == 0, stop=k == KD - 1)
                    last.then_inc(gu_free[i][j], 1)
                    if j < 3:
                        combine(g, j)
                select(g + 2)
                pe.wait_ge(M[i].hidden, g + 2)
                for f in range(2):
                    last = nc.tensor.transpose(PS[:, 3, f * P:(f + 1) * P], hid2[:, f * P:(f + 1) * P], ident)
                pe.wait_ge(M[i].weights_ready, g + 1)
                for t in range(3):
                    w = META if t == 2 else P
                    last = nc.tensor.transpose(PS[:, 4, P * t:P * t + w], weights_[0:w, t, :], ident[0:w, 0:w])
                last.then_inc(M[i].hid_turned, 1)
                pe.wait_ge(M[i].hidT_ready, g + 1)
                for j in range(GROUP):
                    if j % 2 == 0:
                        pe.wait_ge(dn_loaded[i][j // 2], g * 32 + 32)
                    w = ring[:, j, 4096:6144].rearrange("p (f n) -> p f n", f=2)
                    for n in range(2):
                        for f in range(2):
                            last = mm(PS[BLK * j:BLK * (j + 1), 4 + n, :], lhsT=hidT[:, f, j * BLK:(j + 1) * BLK],
                                      rhs=w[:, f, n * 512:(n + 1) * 512], start=f == 0, stop=f == 1)
                    if j % 2:
                        last.then_inc(dn_free[i][j // 2], 1)
            for t in range(3):
                combine(groups, t)

        @block.sync
        def _(sp):
            with nc.allow_non_contiguous_dma(reason="a few hundred words, once"):
                sp.dma_start(posi, A["positions"].rearrange("o (t p) -> p (o t)", p=P)).then_inc(S.small_loaded, 16)
            sp.dma_start(gT1[:, :], A["norm_gains"].rearrange("l n (k c) -> (l n k) c", c=P)).then_inc(S.small_loaded, 16)
            for name in ROWS2:
                r0, ap = row_at[name], A[name]
                n = int(np.prod(ap.shape)) // P
                dims = " ".join(f"d{i}" for i in range(len(ap.shape) - 1))
                src = ap.rearrange(f"{dims} (k c) -> ({dims} k) c", c=P) if dims else ap.rearrange("(k c) -> k c", c=P)
                sp.dma_start(gT2[r0:r0 + n, :], src).then_inc(S.small_loaded, 16)
            sp.dma_start(h[0:META, 2, :], A["meta_tokens_2"]).then_inc(S.meta_loaded, 16)
            sp.dma_start(const[:, :], A["const_table"]).then_inc(S.const_loaded, 16)
            sp.dma_start(h[:, 0:2, :], x_in).then_inc(S.h_loaded, 16)

            def load(use, slot, parts):
                assert len(parts) == 3
                sp.wait_ge(unit_free[slot], use + 1)
                for dst, src in parts:
                    sp.dma_start(dst, src).then_inc(unit_loaded[slot], 16)

            def kparts(slot, w, c0, n, splits=(0, 3, 6, 8)):
                dst = slot_w(slot, KD, n)
                src = w.rearrange("o (k p) f -> p (o k) f", p=P)
                return [(dst[:, a:b, :], src[:, a:b, c0:c0 + n]) for a, b in zip(splits, splits[1:])]

            def ff_parts(slot, gu, down, u):
                g = gu.rearrange("o (k p) f -> p (o k) f", p=P)
                v = ring[:, slot, 0:4096].rearrange("p (s k f) -> p s k f", s=2, k=KD)
                dn = ring[:, slot, 4096:6144].rearrange("p (j n) -> p j n", j=2)
                return [(v[:, 0], g[:, :, bass.ds(u * 256, 256)]),
                        (v[:, 1], g[:, :, bass.ds(u * 256 + D_FF, 256)]),
                        (dn, down[:, bass.ds(u * 256, 256), :].rearrange("o (j p) n -> p (o j) n", p=P))]

            def ffn(l, u0, gu, down):
                gu, down = A[gu][bass.ds(l, 1)], A[down][bass.ds(l, 1)]
                with sp.Fori(0, FF_UNITS // SLOTS) as it:
                    for j in range(SLOTS):
                        load(USES * l + it + (u0 + j) // SLOTS, (u0 + j) % SLOTS,
                             ff_parts((u0 + j) % SLOTS, gu, down, SLOTS * it + j))
                for u in range(SLOTS * (FF_UNITS // SLOTS), FF_UNITS):
                    load(USES * l + (u0 + u) // SLOTS, (u0 + u) % SLOTS,
                         ff_parts((u0 + u) % SLOTS, gu, down, u))

            with sp.Fori(0, DEPTH) as l:
                ffn(l, U_FFN1, "ffn1_gate_up", "ffn1_down")
                for i, (c0, n) in enumerate(IN_COLS):
                    u = U_IN + i
                    load(USES * l + u // SLOTS, u % SLOTS,
                         kparts(u % SLOTS, A["w_in"][bass.ds(l, 1)], c0, n))
                for i in range(2):
                    u = U_OUT + i
                    load(USES * l + u // SLOTS, u % SLOTS,
                         kparts(u % SLOTS, A["w_out"][bass.ds(l, 1)], 512 * i, 512))
                ffn(l, U_FFN2, "ffn2_gate_up", "ffn2_down")
                for i in range(2):
                    u = U_PLE + i
                    load(USES * l + u // SLOTS, u % SLOTS,
                         kparts(u % SLOTS, A["ple_gate"][bass.ds(l, 1)], 512 * i, 512))
                u = U_PLE + 2
                s = u % SLOTS
                proj = A["ple_proj"][bass.ds(l, 1)].rearrange("o (k p) n -> p (o k) n", p=P)
                load(USES * l + u // SLOTS, s, [
                    (ring[:, s, 0:D], proj[:, 0, :]), (ring[:, s, D:2 * D], proj[:, 1, :]),
                    (ring[:, s, 2 * D:2 * D + 512].rearrange("p (t d) -> p t d", t=2),
                     A["p"][bass.ds(l, 1), 0].rearrange("o (t p) d -> p (o t) d", p=P))])
            second_weights(sp, load)
            sp.wait_ge(S.out_ready, 1)
            sp.dma_start(out.rearrange("o (t p) d -> p (o t) d", p=P), xn[:, 0:2, :]).then_inc(S.out_stored, 16)
            sp.wait_ge(S.out_stored, 16)

        @block.gpsimd
        def _(pool):
            nc_ = nc.gpsimd

            def rstd(r, n):
                pool.wait_ge(S.ms_ready, r + 1)
                nc_.tensor_tensor(rs[:, 0:n], ms[:, 0:n], cst("minus_half")[:, 0:n], ALU.pow).then_inc(S.rstd_ready, 1)

            pool.wait_ge(S.const_loaded, 16)
            with pool.Fori(0, DEPTH) as l:
                pool.wait_ge(S.h_upd, 4 * l + 1)
                pool.sem_inc(S.pad, 1)
                rstd(10 * l, 2)
                for i in range(4):
                    nc_.dma_start(rows[:, i, :], A["norm_gains"][bass.ds(l, 1), 2 * i + 1, :].to_broadcast([P, D])).then_inc(S.rows_loaded, 16)
                nc_.dma_start(sgw[:, :, :], A["sg_spatial_w"][bass.ds(l, 1)].rearrange("o g t s -> t (o g) s")).then_inc(S.rows_loaded, 16)
                with nc.allow_non_contiguous_dma(reason="512 words"):
                    nc_.dma_start(sgb[:, :], A["sg_spatial_b"][bass.ds(l, 1)].rearrange("o g t -> t (o g)")).then_inc(S.rows_loaded, 16)
                nc_.dma_start(lng[:, :], A["sg_ln_gain"][bass.ds(l, 1), :].to_broadcast([P, 256])).then_inc(S.rows_loaded, 16)
                nc_.dma_start(hgn[:, :], A["hgrn_norm_gain"][bass.ds(l, 1), :].to_broadcast([P, HD])).then_inc(S.rows_loaded, 16)
                nc_.dma_start(sinks[:, :], A["attn_sinks"][bass.ds(l, 1), :].to_broadcast([P, 8])).then_inc(S.rows_loaded, 16)
                for i, n in enumerate([2, 2, 8, 2, 2, 2, 2, 2, 2]):
                    rstd(10 * l + 1 + i, n)
            second_pool(pool, rstd)

        @block.scalar
        def _(act):
            a_ = nc.scalar

            def squares(r, tiles, src, parts=P):
                for t in range(tiles):
                    pr = META if t == 2 else P
                    d = xn[0:pr, t, :]
                    s = src(t)
                    if len(s.shape) == 3:
                        d = tile2(d)
                    last = a_.activation(d, s, ACT.Square, accum_out=ss[0:pr, t:t + 1])
                last.then_inc(S.square_done, 1)

            def norm(n, tiles=2):
                if tiles == 2:
                    act.wait_ge(S.h_first_tile, n + 1)

                def tile(t):
                    if t == (1 if tiles == 2 else 0):
                        act.wait_ge(S.h_upd, n + 1)
                    return h[0:(META if t == 2 else P), t, :]
                squares(0, tiles, tile)

            def ffn(m):
                def one(f, b, first=False):
                    act.wait_ge(S.gateup_done, FT * m + f + 1)
                    if not first:
                        act.wait_ge(S.hidden_ready, FT * m + f - 1)
                    a_.activation(silu[:, b % 2, :], PS[:, 4 + b % 4, 0:256], ACT.Silu).then_inc(S.silu_ready, 1)
                one(0, 0, True)
                one(1, 1, True)
                with act.Fori(0, (FT - 2) // 4) as it:
                    for k in range(4):
                        one(4 * it + 2 + k, 2 + k)
                act.wait_ge(S.down_done, FT * (m + 1))
                squares(0, 2, yps)

            def mixer(l):
                act.wait_ge(S.qf_done, 2 * l + 1)
                a_.activation(qT, PS[:, 0, :].rearrange("p (c n) -> p c n", c=2), ACT.Copy)
                act.wait_ge(S.qf_done, 2 * l + 2)
                a_.activation(fs, PS[:, 1, :].rearrange("p (c n) -> p c n", c=2), ACT.Copy).then_inc(S.qf_copied, 1)
                for t in range(2):
                    act.wait_ge(S.z_done, 8 * l + 1 + t)
                    a_.activation(z[:, t, 0:256], PS[:, 2 + t, 0:256], ACT.Copy)
                    last = a_.activation(z[:, t, 256:512], PS[:, 2 + t, 256:512], ACT.Sigmoid)
                last.then_inc(S.hihg_copied, 1)
                act.preload_act_table_set("natural_log_exp_and_others")
                NV = 20
                act.wait_ge(S.hgrn_vec, NV * l + 1)
                a_.activation(w2, w1, ACT.Exp)
                act.drain()
                a_.activation(w3, w2, ACT.Ln, bias=1.0).then_inc(S.hgrn_act, 1)
                act.wait_ge(S.hgrn_vec, NV * l + 2)
                for c in range(2):
                    a_.activation(kT[:, c, :], w2[:, c, :], ACT.Exp, bias=lbl[:, 1, c:c + 1])
                a_.activation(w3, w5, ACT.Exp)
                act.drain()
                a_.activation(w4, w3, ACT.Ln, bias=1.0).then_inc(S.hgrn_act, 1)
                for i, s in enumerate([P] + LEVELS[:-1]):
                    act.wait_ge(S.hgrn_vec, NV * l + 3 + 2 * i)
                    dv = dif[:, i % 2].rearrange("p c (n e s) -> p (c n) e s", e=2, s=s)
                    ev = ex[:, i % 2].rearrange("p c (n e s) -> p (c n) e s", e=2, s=s)
                    a_.activation(ev[:, :, 0, :], dv[:, :, 0, :], ACT.Exp, scale=-1.0)
                    a_.activation(ev[:, :, 1, :], dv[:, :, 1, :], ACT.Exp).then_inc(S.hgrn_act, 1)
                for t in range(2):
                    act.wait_ge(S.z_done, 8 * l + 7 + t)
                    last = a_.activation(z[:, t, 1280:1792], PS[:, 5 + t, :], ACT.Gelu_apprx_tanh)
                last.then_inc(S.susv_copied, 1)
                act.wait_ge(S.hgrn_pe, 10 * l + 10)
                a_.activation(w4, PS[:, 4, :].rearrange("p (c n) -> p c n", c=2), ACT.Square).then_inc(S.square_done, 1)
                act.wait_ge(S.qk_turned, l + 1)
                for b in range(3):
                    n = 512 if b < 2 else 256
                    last = a_.activation(qkT[:, 2 * b:2 * b + n // 256, :],
                                         PS[:, 5 + b, 0:n].rearrange("p (c n) -> p c n", n=256), ACT.Copy)
                last.then_inc(S.qkT_ready, 1)
                for n in range(2):
                    nk = P * (n + 1)
                    act.wait_ge(S.scores_ready, 2 * l + n + 1)
                    for hd in range(8):
                        a_.activation(ssb[:, hd, 0:nk], ssb[:, hd, 0:nk], ACT.Exp, bias=sneg[:, hd:hd + 1],
                                      accum_out=ssum[:, hd:hd + 1])
                    a_.activation(sden, ssink, ACT.Exp).then_inc(S.probs_ready, 1)
                    act.wait_ge(S.probs_turned, 2 * l + n + 1)
                    for b in range(2):
                        src = (PS[:, 2 + b, :] if n == 0 else PS[:, 2 * b:2 * b + 2, :].rearrange("p a b -> p (a b)"))
                        dst = (pT_[:, 4 * b:4 * b + 4, 0:n + 1, :])
                        last = a_.activation(dst, src.rearrange("p (a c q) -> p a c q", a=4, q=P), ACT.Copy)
                    last.then_inc(S.probsT_ready, 1)
                    if n == 0:
                        act.wait_ge(S.centred, l + 1)
                        for t in range(2):
                            last = a_.activation(sgm_mix[:, t, :], lnw[:, t, :], ACT.Square, accum_out=ss[:, t:t + 1])
                        last.then_inc(S.square_done, 1)
                act.wait_ge(S.wout_done, l + 1)
                squares(0, 2, yps)

            def ple(l):
                act.wait_ge(S.gate_done, l + 1)
                for t in range(2):
                    last = a_.activation(tile2(sgm[:, t, :]), yps(t), ACT.Sigmoid)
                last.then_inc(S.gate_ready, 1)
                act.wait_ge(S.ple_ready, l + 1)
                squares(0, 2, lambda t: sgm[:, t, :])

            act.wait_ge(S.lb_vec, 1)
            a_.activation(lbt[:, 4:8], lbt[:, 0:4], ACT.Exp).then_inc(S.lb_act, 1)
            act.wait_ge(S.lb_vec, 2)
            a_.activation(lbt[:, 10:12], lbt[:, 8:10], ACT.Ln).then_inc(S.lb_act, 1)
            act.wait_ge(S.rope_vec, 1)
            a_.activation(rope_cos, rope_cos, ACT.Sin)
            a_.activation(rope_sin, rope_sin, ACT.Sin).then_inc(S.rope_ready, 1)

            with act.Fori(0, DEPTH) as l:
                norm(4 * l)
                ffn(2 * l)
                norm(4 * l + 1)
                mixer(l)
                norm(4 * l + 2)
                ffn(2 * l + 1)
                norm(4 * l + 3)
                ple(l)
            second_act(act, norm, squares)

        @block.vector
        def _(dve):
            v_ = nc.vector
            settle = dve.drain

            def rstd(r, n, width, sums=None):
                dve.wait_ge(S.square_done, r + 1)
                if sums is not None:
                    v_.tensor_reduce(ss[:, 0:n], sums, AX.X, ALU.add)
                    settle()
                v_.tensor_scalar(ms[:, 0:n], ss[:, 0:n], 1.0 / width, EPS, ALU.mult, ALU.add).then_inc(S.ms_ready, 1)
                dve.wait_ge(S.rstd_ready, r + 1)

            def turned(q, tiles, gains):
                for n_, (dst, g) in enumerate(gains):
                    for t in range(tiles):
                        w = META if t == 2 else P
                        src = (PS[:, 2 * t:2 * t + 2, :].rearrange("p a (k w) -> p (a k) w", w=w) if t < 2
                               else PS[:, 4, 0:KD * w].rearrange("p (k w) -> p k w", w=w))
                        if n_ == 0:
                            dve.wait_ge(S.xn_turned, turned_tiles(q, tiles) + t + 1)
                        if g is None:
                            last = v_.tensor_copy(dst[:, :, xcol(t)], src)
                        else:
                            last = v_.tensor_tensor(dst[:, :, xcol(t)], src,
                                                    g.unsqueeze(2).to_broadcast([P, KD, w]), ALU.mult)
                last.then_inc(S.xT_ready, 1)

            def norm(r, q, gains, tiles=2):
                rstd(r, tiles, D)
                for t in range(tiles):
                    pr = META if t == 2 else P
                    v_.tensor_scalar(xn[0:pr, t, :], h[0:pr, t, :], rs[0:pr, t:t + 1], None, ALU.mult).then_inc(S.xn_ready, 1)
                turned(q, tiles, gains)

            def postnorm(l, r, i, factor, src):
                rstd(r, 2, D)
                if i == 0:
                    dve.wait_ge(S.rows_loaded, 16 * 9 * l + 16 * 9)
                for t in range(2):
                    v_.scalar_tensor_tensor(tile2(xn[:, t, :]), src(t), rs[:, t:t + 1], tile2(rows[:, i, :]),
                                            ALU.mult, ALU.mult)
                    settle()
                    v_.scalar_tensor_tensor(h[:, t, :], xn[:, t, :], factor, h[:, t, :], ALU.mult,
                                            ALU.add).then_inc(S.h_upd if t else S.h_first_tile, 1)

            def ffn(m):
                def one(f, b, first=False):
                    dve.wait_ge(S.silu_ready, FT * m + f + 1)
                    if not first:
                        dve.wait_ge(S.down_done, FT * m + f - 1)
                    v_.tensor_tensor(hid[:, b % 2, :], silu[:, b % 2, :], PS[:, 4 + b % 4, 256:512],
                                     ALU.mult).then_inc(S.hidden_ready, 1)
                one(0, 0, True)
                one(1, 1, True)
                with dve.Fori(0, (FT - 2) // 4) as it:
                    for k in range(4):
                        one(4 * it + 2 + k, 2 + k)

            def mixer(l):
                dve.wait_ge(S.qf_copied, l + 1)
                v_.scalar_tensor_tensor(w1, fs, -1.0, fs, ALU.mult, ALU.min).then_inc(S.hgrn_vec, 1)
                v_.memset(att, 0.0)
                NA = 10
                dve.wait_ge(S.hgrn_act, NA * l + 1)
                v_.scalar_tensor_tensor(w1, fs, 0.0, w3, ALU.min, ALU.subtract)
                settle()
                v_.tensor_tensor(w2, w1, fs, ALU.subtract)
                for c in range(2):
                    v_.tensor_scalar(w4[:, c, :], w1[:, c, :], lbl[:, 2, c:c + 1], None, ALU.add)
                    v_.tensor_scalar(w6[:, c, :], w1[:, c, :], lbl[:, 1, c:c + 1], None, ALU.add)
                settle()
                v_.scalar_tensor_tensor(w5, w4, -1.0, w4, ALU.mult, ALU.min).then_inc(S.hgrn_vec, 1)
                dve.wait_ge(S.hgrn_act, NA * l + 2)
                for c in range(2):
                    v_.scalar_tensor_tensor(w5[:, c, :], w6[:, c, :], lbl[:, 0, c:c + 1], w4[:, c, :],
                                            ALU.max, ALU.add)
                settle()
                for c in range(2):
                    v_.tensor_tensor_scan(w1[:, c, :], cst("ones")[:, 0:1].to_broadcast([P, 256]), w5[:, c, :], 0.0,
                                          ALU.mult, ALU.add)
                settle()

                sizes = [P] + LEVELS[:-1]

                def distance(i):
                    s = sizes[i]
                    b = w1.rearrange("p c (n s) -> p (c n) s", s=2 * s)
                    n = b.shape[1]
                    v_.tensor_tensor(dif[:, i % 2].rearrange("p c (n s) -> p (c n) s", s=2 * s), b,
                                     b[:, :, s - 1:s].to_broadcast([P, n, 2 * s]), ALU.subtract).then_inc(S.hgrn_vec, 1)

                def decayed(i):
                    s = sizes[i]
                    split = lambda v: v.rearrange("p c (n e s) -> p (c n) e s", e=2, s=s)
                    dve.wait_ge(S.hgrn_act, NA * l + 3 + i)
                    v_.tensor_tensor(split(lev[:, i % 2])[:, :, 0, :], split(kT)[:, :, 0, :],
                                     split(ex[:, i % 2])[:, :, 0, :], ALU.mult)
                    v_.tensor_tensor(split(lev[:, i % 2])[:, :, 1, :], split(qT)[:, :, 1, :],
                                     split(ex[:, i % 2])[:, :, 1, :], ALU.mult).then_inc(S.hgrn_vec, 1)

                def gathered(i):
                    settle()
                    dve.wait_ge(S.hgrn_pe, 10 * l + 1 + i)
                    b = 2 * (i % 2)
                    if i == 0:
                        v_.tensor_copy(att10, PS[:, b:b + 2, 0:256].rearrange("p a (c n) -> p a c n", c=2))
                    else:
                        dve.sem_inc(S.pad, 1)
                        m = cst("levels")[:, (i - 1) * P:i * P].bitcast(I32)
                        v_.copy_predicated(att.rearrange("p a b c q -> p (a b c) q"), m.unsqueeze(1).to_broadcast([P, 8, P]),
                                           PS[:, b:b + 2, :].rearrange("p a (c q) -> p (a c) q", q=P))

                distance(0)
                for i in range(8):
                    if i < 7:
                        distance(i + 1)
                    decayed(i)
                    if i == 0:
                        for i, (a, b, bank) in enumerate([(512, 1024, 4), (1024, 1280, 6)]):
                            for t in range(2):
                                dve.wait_ge(S.z_done, 8 * l + 3 + 2 * i + t)
                                last = v_.tensor_copy(z[:, t, a:b], PS[:, bank + t, 0:b - a])
                        last.then_inc(S.qkv_copied, 1)
                    if i:
                        gathered(i - 1)
                gathered(7)
                dve.drain().then_inc(S.hgrn_vec, 1)
                gathered(8)
                dve.drain().then_inc(S.hgrn_vec, 1)
                dve.wait_ge(S.square_done, 10 * l + 4)
                rstd(10 * l + 3, 8, HD, sums=w4.rearrange("p c (h e) -> p (c h) e", e=HD))
                o = PS[:, 4, :].rearrange("p (n e) -> p n e", e=HD)
                wv = w2.rearrange("p c (h e) -> p (c h) e", e=HD)
                v_.tensor_tensor(wv, o, rs[:, 0:8].unsqueeze(2).to_broadcast([P, 8, HD]), ALU.mult)
                settle()
                v_.tensor_tensor(wv, wv, hgn[:, :].unsqueeze(1).to_broadcast([P, 8, HD]), ALU.mult)
                settle()
                dve.wait_ge(S.hihg_copied, l + 1)
                v_.tensor_tensor(xn[:, 0:2, 0:256], w2, z[:, :, 256:512], ALU.mult)

                x12 = z[:, :, 512:1152].rearrange("p t (h e d) -> p t h e d", e=2, d=32)
                cs = rope_cos[:, :, :].unsqueeze(2).to_broadcast([P, 2, 10, 32])
                sn = rope_sin[:, :, :].unsqueeze(2).to_broadcast([P, 2, 10, 32])
                settle()
                pr = [rprod[:, i, :].rearrange("p (t h d) -> p t h d", t=2, h=10) for i in range(4)]
                dve.wait_ge(S.rope_ready, 1)
                for i, (e, c) in enumerate([(0, cs), (1, sn), (1, cs), (0, sn)]):
                    v_.tensor_tensor(pr[i], x12[:, :, :, e, :], c, ALU.mult)
                settle()
                for e, (a, b, op) in enumerate([(pr[0], pr[1], ALU.subtract), (pr[2], pr[3], ALU.add)]):
                    for t in range(2):
                        ro = rot[:, t, 0:512].rearrange("p (j g e d) -> p g j e d", g=2, e=2, d=32)
                        v_.tensor_tensor(ro[:, :, :, e, :], a[:, t, 0:8, :].rearrange("p (g j) d -> p g j d", g=2),
                                         b[:, t, 0:8, :].rearrange("p (g j) d -> p g j d", g=2), op)
                    ro = rot[:, :, 512:640].rearrange("p t (h e d) -> p t h e d", e=2, d=32)
                    last = v_.tensor_tensor(ro[:, :, :, e, :], a[:, :, 8:10, :], b[:, :, 8:10, :], op)
                last.then_inc(S.roped, 1)
                settle()
                for n in range(2):
                    nk = P * (n + 1)
                    dve.wait_ge(S.scores_done, 2 * l + n + 1)
                    src = (PS[:, 0:2, :] if n == 0 else PS[:, 4:8, :]).rearrange("p a (h k) -> p (a h) k", k=nk)
                    bias = cst("window")[:, P:2 * P] if n == 0 else cst("window")
                    v_.scalar_tensor_tensor(ssb[:, :, 0:nk], src, HD ** -0.5,
                                            bias.unsqueeze(1).to_broadcast([P, 8, nk]), ALU.mult, ALU.add)
                    settle()
                    v_.tensor_reduce(smax, ssb[:, :, 0:nk], AX.X, ALU.max)
                    settle()
                    v_.tensor_tensor(smax, smax, sinks[:, :], ALU.max)
                    settle()
                    v_.tensor_scalar(sneg, smax, -1.0, None, ALU.mult)
                    v_.tensor_tensor(ssink, sinks[:, :], smax, ALU.subtract).then_inc(S.scores_ready, 1)
                    if n == 0:
                        dve.wait_ge(S.sgw_turned, l + 1)
                        v_.tensor_tensor(sgwT, PS[:, 5, :].rearrange("p (g t) -> p g t", g=4),
                                         cst("upto").unsqueeze(1).to_broadcast([P, 4, P]), ALU.mult)
                        dve.drain().then_inc(S.sgw_ready, 1)
                        dve.wait_ge(S.susv_copied, l + 1)
                        v_.tensor_reduce(mean, z[:, :, 1536:1792], AX.X, ALU.add)
                        settle()
                        v_.tensor_scalar(mean, mean, -1.0 / 256, None, ALU.mult)
                        settle()
                        for t in range(2):
                            last = v_.tensor_scalar(lnw[:, t, :], z[:, t, 1536:1792], mean[:, t:t + 1], None, ALU.add)
                        last.then_inc(S.centred, 1)
                    else:
                        rstd(10 * l + 4, 2, 256)
                        for t in range(2):
                            last = v_.scalar_tensor_tensor(lnw[:, t, :], lnw[:, t, :], rs[:, t:t + 1], lng[:, :], ALU.mult, ALU.mult)
                        last.then_inc(S.sv_ready, 1)
                    dve.wait_ge(S.attn_done, 2 * l + n + 1)
                    v_.tensor_tensor(srden, ssum, sden, ALU.add)
                    settle()
                    v_.reciprocal(srden, srden)
                    settle()
                    ob = PS[:, 0 if n == 0 else 4, :].rearrange("p (h e) -> p h e", e=HD)
                    v_.tensor_tensor(xn[:, n, 256:768].rearrange("p (h e) -> p h e", e=HD), ob,
                                     srden.unsqueeze(2).to_broadcast([P, 8, HD]), ALU.mult)
                dve.wait_ge(S.spatial_done, l + 1)
                v_.tensor_tensor(sgm_mix.rearrange("p t (g e) -> p t g e", e=HD),
                                 PS[:, 6, :].rearrange("p (t g e) -> p t g e", t=2, e=HD),
                                 sgb[:, :].unsqueeze(1).unsqueeze(3).to_broadcast([P, 2, 4, HD]), ALU.add)
                settle()
                v_.tensor_tensor(xn[:, 0:2, 768:1024], sgm_mix, z[:, :, 1280:1536], ALU.mult).then_inc(S.xn_ready, 2)
                turned(5 * l + 2, 2, [(xT, None)])

            def ple(l):
                dve.wait_ge(S.p_turned, l + 1)
                v_.tensor_copy(pleT, PS[:, 4, :].rearrange("p (k t) -> p k t", k=2)).then_inc(S.pT_ready, 1)
                dve.wait_ge(S.gate_ready, l + 1)
                dve.wait_ge(S.proj_done, l + 1)
                for t in range(2):
                    last = v_.tensor_tensor(tile2(sgm[:, t, :]), tile2(sgm[:, t, :]), PS[:, 4 + 2 * t:6 + 2 * t, :], ALU.mult)
                last.then_inc(S.ple_ready, 1)

            dve.wait_ge(S.rowsT_done, 1)
            v_.tensor_copy(gT1[:, :], PS[:, 0, 0:P])
            v_.tensor_copy(gT2[:, 0:n_rows2], PS[:, 1, 0:n_rows2])
            settle()
            lg = gT2[:, row_at["hgrn_lb_logits"]:row_at["hgrn_lb_logits"] + 4]
            v_.tensor_tensor(lbt[:, 12:14], lg[:, 0:2], lg[:, 2:4], ALU.max)
            settle()
            v_.tensor_tensor(lbt[:, 0:2], lg[:, 0:2], lbt[:, 12:14], ALU.subtract)
            v_.tensor_tensor(lbt[:, 2:4], lg[:, 2:4], lbt[:, 12:14], ALU.subtract).then_inc(S.lb_vec, 1)
            dve.wait_ge(S.lb_act, 1)
            v_.tensor_tensor(lbt[:, 8:10], lbt[:, 4:6], lbt[:, 6:8], ALU.add).then_inc(S.lb_vec, 1)
            dve.wait_ge(S.lb_act, 2)
            v_.memset(lb[:, 0, 0, :], LN_FLOOR)
            v_.memset(lb[:, 0, 1, :], 0.0)
            v_.memset(lb[:, 0, 2, :], -LN_FLOOR)
            v_.tensor_tensor(lb[:, 1, 0, :], lbt[:, 2:4], lbt[:, 10:12], ALU.subtract)
            v_.tensor_tensor(lb[:, 1, 1, :], lbt[:, 0:2], lbt[:, 10:12], ALU.subtract)
            settle()
            v_.tensor_scalar(lb[:, 1, 0, :], lb[:, 1, 0, :], LN_FLOOR, None, ALU.max)
            settle()
            v_.tensor_tensor(lb[:, 1, 2, :], lb[:, 1, 1, :], lb[:, 1, 0, :], ALU.subtract)
            v_.tensor_copy(posf, posi)
            settle()
            ang = arena[:, 0:64].rearrange("p (t d) -> p t d", t=2)
            k1 = arena[:, 64:128].rearrange("p (t d) -> p t d", t=2)
            k2 = arena[:, 128:192].rearrange("p (t d) -> p t d", t=2)
            for t in range(2):
                v_.tensor_scalar(ang[:, t, :], cst("inv_freq"), posf[:, t:t + 1], None, ALU.mult)
            settle()
            for k, quarter in ((k1, 0.0), (k2, 0.25)):
                v_.tensor_scalar(k, ang, 1.0 / TWO_PI, quarter, ALU.mult, ALU.add)
                settle()
                v_.tensor_scalar(k, k, ROUND, None, ALU.add)
                settle()
                v_.tensor_scalar(k, k, -ROUND, None, ALU.add)
                settle()
            for k, dst, quarter in ((k1, rope_sin, 0.0), (k2, rope_cos, np.pi / 2)):
                v_.scalar_tensor_tensor(dst[:, :, :], k, -C1, ang, ALU.mult, ALU.add)
                settle()
                v_.scalar_tensor_tensor(dst[:, :, :], k, -C2, dst[:, :, :], ALU.mult, ALU.add)
                settle()
                v_.scalar_tensor_tensor(dst[:, :, :], k, -C3, dst[:, :, :], ALU.mult, ALU.add)
                settle()
                v_.tensor_scalar(dst[:, :, :], dst[:, :, :], float(quarter), 3.1415925, ALU.add, ALU.min)
                settle()
                last = v_.tensor_scalar(dst[:, :, :], dst[:, :, :], -3.1415925, None, ALU.max)
            last.then_inc(S.rope_vec, 1)
            dve.wait_ge(S.h_loaded, 16)
            dve.wait_ge(S.meta_loaded, 16)
            dve.drain().then_inc(S.h_first_tile, 1)
            dve.drain().then_inc(S.h_upd, 1)

            with dve.Fori(0, DEPTH) as l:
                v_.tensor_copy(gl[:, :], gT1[:, bass.ds(l * 64, 64)])
                v_.tensor_copy(lbl, lb.rearrange("p l v c -> p l (v c)")[:, bass.ds(l, 1), :].rearrange("p o (v c) -> p (o v) c", v=3))
                settle()
                norm(10 * l, 5 * l, [(xT, gl[:, 0:8])])
                ffn(2 * l)
                postnorm(l, 10 * l + 1, 0, 0.5, yps)
                norm(10 * l + 2, 5 * l + 1, [(xT, gl[:, 16:24])])
                mixer(l)
                postnorm(l, 10 * l + 5, 1, 1.0, yps)
                norm(10 * l + 6, 5 * l + 3, [(xT, gl[:, 32:40])])
                ffn(2 * l + 1)
                postnorm(l, 10 * l + 7, 2, 0.5, yps)
                norm(10 * l + 8, 5 * l + 4, [(xT, gl[:, 48:56])])
                ple(l)
                postnorm(l, 10 * l + 9, 3, 1.0, lambda t: tile2(sgm[:, t, :]))
            second_vec(dve, rstd, turned, norm)

        @block.tensor
        def _(pe):
            mm = nc.tensor.matmul

            def turn(q, tiles=2):
                for t in range(tiles):
                    pe.wait_ge(S.xn_ready, turned_tiles(q, tiles) + t + 1)
                    w = META if t == 2 else P
                    for k in range(KD):
                        o = (PS[:, 2 * t + k // 4, (k % 4) * P:(k % 4) * P + P] if t < 2
                             else PS[:, 4, k * w:(k + 1) * w])
                        last = nc.tensor.transpose(o, xn[0:w, t, k * P:(k + 1) * P], ident[0:w, 0:w])
                    last.then_inc(S.xn_turned, 1)
                pe.wait_ge(S.xT_ready, q + 1)

            def loaded(use, slot):
                pe.wait_ge(unit_loaded[slot], 48 * use + 48)

            def ffn(l, m, u0):
                def gate_up(f, local):
                    unit = u0 + local // 2
                    slot = unit % SLOTS
                    w = ring[:, slot, 0:4096].rearrange("p (s k f) -> p s k f", s=2, k=KD)
                    j = local % 2
                    if j == 0:
                        loaded(USES * l + f[0] + unit // SLOTS, slot)
                    for s in range(2):
                        for k in range(KD):
                            last = mm(PS[:, 4 + local % 4, s * 256:(s + 1) * 256], lhsT=w[:, s, k, j * P:(j + 1) * P],
                                      rhs=xT[:, k, META:T2], start=k == 0, stop=k == KD - 1)
                            if s == k == 0 and j == 1 and local > 1:
                                last.then_inc(unit_free[(unit - 1) % SLOTS], 1)
                    last.then_inc(S.gateup_done, 1)

                def down(f, local, first=False, final=False):
                    slot = (u0 + local // 2) % SLOTS
                    j = local % 2
                    w = ring[:, slot, 4096:6144].rearrange("p (j n) -> p j n", j=2)
                    pe.wait_ge(S.hidden_ready, FT * m + 8 * f[0] + local + 1)
                    for t in range(2):
                        for n in range(2):
                            last = mm(PS[:, 2 * t + n, :], lhsT=hid[:, j, t * P:(t + 1) * P],
                                      rhs=w[:, j, n * 512:(n + 1) * 512], start=first, stop=final,
                                      skip_group_check=True)
                    last.then_inc(S.down_done, 1)
                    if final:
                        pe.drain().then_inc(unit_free[slot], 1)

                gate_up([0], 0)
                gate_up([0], 1)
                down([0], 0, first=True)
                with pe.Fori(0, 2) as it:
                    for k in range(8):
                        gate_up([it], 2 + k)
                        down([it], 1 + k)
                for local in range(17, FT):
                    if local + 1 < FT:
                        gate_up([0], local + 1)
                    down([0], local, final=local == FT - 1)

            def dense(slot, w, bank, t, width, src=xT, kk=KD, at=0):
                for k in range(kk):
                    last = mm(PS[:, bank, at:at + width], lhsT=src[:, k, xcol(t)], rhs=w[:, k, 0:width],
                              start=k == 0, stop=k == kk - 1)
                return last

            def mixer(l):
                slot, use = U_IN % SLOTS, USES * l + U_IN // SLOTS
                loaded(use, slot)
                w = slot_w(slot, KD, 512)
                for m in range(4):
                    for k in range(KD):
                        last = mm(PS[:, m // 2, (m % 2) * 256:(m % 2) * 256 + 256], lhsT=w[:, k, m * P:(m + 1) * P],
                                  rhs=xT[:, k, META:T2], start=k == 0, stop=k == KD - 1)
                    if m % 2:
                        last.then_inc(S.qf_done, 1)
                pe.drain().then_inc(unit_free[slot], 1)
                for i, bank in enumerate([2, 4, 6]):
                    u = U_IN + 1 + i
                    width = IN_COLS[1 + i][1]
                    slot = u % SLOTS
                    loaded(USES * l + u // SLOTS, slot)
                    for t in range(2):
                        last = dense(slot, slot_w(slot, KD, width), bank + t, t, width)
                        last.then_inc(S.z_done, 1)
                    pe.drain().then_inc(unit_free[slot], 1)
                su_slot = (U_IN + 4) % SLOTS

                def su_sv(i):
                    if i == 0:
                        loaded(USES * l + (U_IN + 4) // SLOTS, su_slot)
                        pe.wait_ge(S.qkv_copied, l + 1)
                    t = i // 4
                    for k in range(2 * (i % 4), 2 * (i % 4) + 2):
                        last = mm(PS[:, 5 + t, :], lhsT=xT[:, k, xcol(t)], rhs=slot_w(su_slot, KD, 512)[:, k, :],
                                  start=k == 0, stop=k == KD - 1)
                    if i % 4 == 3:
                        last.then_inc(S.z_done, 1)
                    if i == 7:
                        pe.drain().then_inc(unit_free[su_slot], 1)

                for i in range(9):
                    b = 2 * (i % 2)
                    if i < 8:
                        pe.wait_ge(S.hgrn_vec, 20 * l + 4 + 2 * i + (1 if i < 7 else 0))
                    for hd in range(4):
                        par, c = hd % 2, hd // 2
                        rows_ = slice(64 * par, 64 * par + 64)
                        ks = lev[rows_, i % 2, c, :] if i < 8 else kT[rows_, c, :]
                        qs = lev[rows_, i % 2, c, :] if i < 8 else qT[rows_, c, :]
                        if i == 0:
                            last = mm(PS[:, b + par, c * P:(c + 1) * P], lhsT=ks[:, 0:P], rhs=qs[:, P:2 * P],
                                      start=True, stop=True)
                        else:
                            for t in range(2):
                                last = mm(PS[:, b + par, (2 * c + t) * P:(2 * c + t + 1) * P],
                                          lhsT=ks[:, t * P:(t + 1) * P], rhs=qs[:, t * P:(t + 1) * P],
                                          start=True, stop=True)
                    last.then_inc(S.hgrn_pe, 1)
                    if i < 8:
                        su_sv(i)
                    if i == 7:
                        pe.wait_ge(S.hgrn_vec, 20 * l + 18 + 1)
                pe.wait_ge(S.hgrn_vec, 20 * l + 20)
                pe.wait_ge(S.hihg_copied, l + 1)
                for t in range(2):
                    for hd in range(4):
                        par, c = hd % 2, hd // 2
                        o = PS[:, 4, (4 * t + hd) * HD:(4 * t + hd + 1) * HD]
                        last = mm(o, lhsT=att[:, par, c, t, :], rhs=z[:, t, hd * HD:(hd + 1) * HD], start=True, stop=t == 0)
                        if t:
                            last = mm(o, lhsT=att10[:, par, c, :], rhs=z[:, 0, hd * HD:(hd + 1) * HD], start=False, stop=True)
                last.then_inc(S.hgrn_pe, 1)
                pe.wait_ge(S.roped, l + 1)
                pe.wait_ge(S.susv_copied, l + 1)
                for t in range(2):
                    for j in range(5):
                        src = rot[:, t, j * P:(j + 1) * P]
                        last = nc.tensor.transpose(PS[:, 5 + j // 2, (j % 2) * 256 + t * P:(j % 2) * 256 + (t + 1) * P],
                                                   src, ident)
                last.then_inc(S.qk_turned, 1)
                pe.wait_ge(S.qkT_ready, l + 1)
                for n in range(2):
                    nk = P * (n + 1)
                    for hd in range(8):
                        g, j = hd // 4, hd % 4
                        r = slice(64 * g, 64 * g + 64)
                        per = 512 // nk
                        last = mm(PS[:, (0 if n == 0 else 4) + hd // per, (hd % per) * nk:(hd % per + 1) * nk],
                                  lhsT=qkT[r, j, n * P:(n + 1) * P], rhs=qkT[r, 4, 0:nk], start=True, stop=True)
                    last.then_inc(S.scores_done, 1)
                    if n == 0:
                        for g in range(4):
                            last = nc.tensor.transpose(PS[:, 5, g * P:(g + 1) * P], sgw[:, g, :], ident)
                        last.then_inc(S.sgw_turned, 1)
                    pe.wait_ge(S.probs_ready, 2 * l + n + 1)
                    for hd in range(8):
                        for c in range(n + 1):
                            i = hd * (n + 1) + c
                            last = nc.tensor.transpose(PS[:, (2 if n == 0 else 0) + i // 4, (i % 4) * P:(i % 4 + 1) * P],
                                                       ssb[:, hd, c * P:(c + 1) * P], ident)
                    last.then_inc(S.probs_turned, 1)
                    if n == 1:
                        pe.wait_ge(S.sv_ready, l + 1)
                        for t in range(2):
                            for g in range(4):
                                last = mm(PS[:, 6, (4 * t + g) * HD:(4 * t + g + 1) * HD], lhsT=sgwT[:, g, :],
                                          rhs=lnw[:, t, g * HD:(g + 1) * HD], start=True, stop=True)
                        last.then_inc(S.spatial_done, 1)
                    pe.wait_ge(S.probsT_ready, 2 * l + n + 1)
                    if n == 0:
                        pe.wait_ge(S.qkv_copied, l + 1)
                        pe.wait_ge(S.sgw_ready, l + 1)
                    for hd in range(8):
                        for c in range(n + 1):
                            g = hd // 4
                            last = mm(PS[:, 0 if n == 0 else 4, hd * HD:(hd + 1) * HD], lhsT=pT_[:, hd, c, :],
                                      rhs=z[:, c, 1152 + g * HD:1152 + (g + 1) * HD], start=c == 0, stop=c == n)
                    last.then_inc(S.attn_done, 1)
                turn(5 * l + 2)
                for i in range(2):
                    u = U_OUT + i
                    slot = u % SLOTS
                    loaded(USES * l + u // SLOTS, slot)
                    for t in range(2):
                        last = dense(slot, slot_w(slot, KD, 512), 2 * t + i, t, 512)
                    last.then_inc(unit_free[slot], 1)
                pe.drain().then_inc(S.wout_done, 1)

            def ple(l):
                for i in range(2):
                    u = U_PLE + i
                    slot = u % SLOTS
                    loaded(USES * l + u // SLOTS, slot)
                    for t in range(2):
                        last = dense(slot, slot_w(slot, KD, 512), 2 * t + i, t, 512)
                    last.then_inc(unit_free[slot], 1)
                pe.drain().then_inc(S.gate_done, 1)
                u = U_PLE + 2
                slot = u % SLOTS
                loaded(USES * l + u // SLOTS, slot)
                pv = ring[:, slot, 2 * D:2 * D + 512].rearrange("p (t d) -> p t d", t=2)
                for t in range(2):
                    for k in range(2):
                        last = nc.tensor.transpose(PS[:, 4, k * 256 + t * P:k * 256 + (t + 1) * P], pv[:, t, k * P:(k + 1) * P], ident)
                last.then_inc(S.p_turned, 1)
                pe.wait_ge(S.pT_ready, l + 1)
                w = slot_w(slot, 2, D)
                for t in range(2):
                    for n in range(2):
                        for k in range(2):
                            last = mm(PS[:, 4 + 2 * t + n, :], lhsT=pleT[:, k, t * P:(t + 1) * P],
                                      rhs=w[:, k, n * 512:(n + 1) * 512], start=k == 0, stop=k == 1)
                last.then_inc(unit_free[slot], 1)
                pe.drain().then_inc(S.proj_done, 1)

            for f in unit_free:
                pe.sem_inc(f, 1)
            pe.wait_ge(S.const_loaded, 16)
            pe.wait_ge(S.small_loaded, 16 * (2 + len(ROWS2)))
            nc.tensor.transpose(PS[:, 0, 0:P], gT1[:, :], ident)
            nc.tensor.transpose(PS[:, 1, 0:n_rows2], gT2[0:n_rows2, :], ident[0:n_rows2, 0:n_rows2]).then_inc(S.rowsT_done, 1)
            with pe.Fori(0, DEPTH) as l:
                turn(5 * l)
                ffn(l, 2 * l, U_FFN1)
                turn(5 * l + 1)
                mixer(l)
                turn(5 * l + 3)
                ffn(l, 2 * l + 1, U_FFN2)
                turn(5 * l + 4)
                ple(l)
            second_pe(pe, turn, loaded, dense)




def kernel(**inputs):
    import concourse.bacc as bacc
    from concourse.bass_utils import run_bass_kernel_spmd

    nc = bacc.Bacc("TRN2", target_bir_lowering=False, num_devices=1)
    arrays = {k: np.ascontiguousarray(v) for k, v in inputs.items()}
    arrays["const_table"] = CONSTS
    arrays["const_table2"] = CONSTS2
    aps = {k: nc.dram_tensor(k, a.shape, mybir.dt.from_np(a.dtype), kind="ExternalInput").ap()
           for k, a in arrays.items()}
    out = nc.dram_tensor("out", (1, SEQ, D), F32, kind="ExternalOutput").ap()
    build(nc, aps, out)
    r = run_bass_kernel_spmd(nc, [arrays], core_ids=[0])
    return r.results[0]["out"]
```
